# Optimizing a Trainium2 kernel written in Bass

```python
import math
import jax, jax.numpy as jnp
from jax import lax
import numpy as np

D_MODEL = 1024
BATCH = 1
SEQ = 256
DEPTH = 2
DEC_BATCH = 8
DEC_SEQ = 8
PAST_LEN = 1024
PAGE_SIZE = 128

D_MIX = D_MODEL
D_A = D_MIX // 2
H_A = 4
DV_A = D_A // H_A
DQK_A = DV_A // 2
D_B = D_MIX - D_A
H_B = 4
DK_B = D_B // H_B
DV_B = D_B // H_B
CONV_W = 4
CHUNK = 64
Q_BLOCK = 128
D_FF = 2816
N_EXPERTS = 8
TOP_K = 2
D_FF_E = 2816
ALPHA = (2 * DEPTH) ** 0.25
BETA_INIT = (8 * DEPTH) ** -0.25
LN_EPS = 1e-5
N_DENSE = (DEPTH + 1) // 2
N_MOE = DEPTH // 2

A_Q = 2 * H_A * DQK_A
A_K = 2 * H_A * DQK_A
A_V = H_A * DV_A
B_QKV = 3 * D_B
B_BETA = H_B
B_DECAY = H_B
B_GATE = D_B
D_IN = A_Q + A_K + A_V + B_QKV + B_BETA + B_DECAY + B_GATE
SPLIT_IDX = (A_Q, A_Q + A_K, A_Q + A_K + A_V, A_Q + A_K + A_V + B_QKV,
             A_Q + A_K + A_V + B_QKV + B_BETA, A_Q + A_K + A_V + B_QKV + B_BETA + B_DECAY)

kernel_name = 'hymba_diffattn_gdn_deepnorm_adaln_step'

def _layernorm(x):
    xf = x.astype(jnp.float32)
    mu = jnp.mean(xf, axis=-1, keepdims=True)
    var = jnp.mean(jnp.square(xf - mu), axis=-1, keepdims=True)
    return ((xf - mu) * lax.rsqrt(var + LN_EPS)).astype(x.dtype)

def _rmsnorm(x, g):
    xf = x.astype(jnp.float32)
    y = xf * lax.rsqrt(jnp.mean(xf * xf, axis=-1, keepdims=True) + 1e-6)
    return (y * g.astype(jnp.float32)).astype(x.dtype)

def _l2norm(x):
    xf = x.astype(jnp.float32)
    return xf * lax.rsqrt(jnp.sum(xf * xf, axis=-1, keepdims=True) + 1e-6)

def _alibi_slopes():
    return jnp.asarray([2.0 ** (-8.0 * (h + 1) / H_A) for h in range(H_A)], dtype=jnp.float32)

def _diff_attn_block(q, k, v, q_pos, k_pos, lam, slopes):
    s = jnp.einsum('bqhmd,bkhmd->bhmqk', q, k).astype(jnp.float32) * (DQK_A ** -0.5)
    dist = (q_pos[:, None] - k_pos[None, :]).astype(jnp.float32)
    s = s - slopes[None, :, None, None, None] * dist
    s = jnp.where(dist >= 0, s, -jnp.inf)
    p = jax.nn.softmax(s, axis=-1)
    a = p[:, :, 0] - lam * p[:, :, 1]
    return jnp.einsum('bhqk,bkhd->bqhd', a.astype(v.dtype), v)

def _diff_attention(q, k_all, v_all, q_pos, lam_p, subln_g, layer):
    B, L = q.shape[0], q.shape[1]
    lam_init = 0.8 - 0.6 * math.exp(-0.3 * layer)
    lp = lam_p.astype(jnp.float32)
    lam = jnp.exp(jnp.sum(lp[0] * lp[1])) - jnp.exp(jnp.sum(lp[2] * lp[3])) + lam_init
    k_all = k_all.reshape(B, k_all.shape[1], H_A, 2, DQK_A)
    k_pos = jnp.arange(k_all.shape[1], dtype=jnp.int32)
    slopes = _alibi_slopes()
    blk = Q_BLOCK if L % Q_BLOCK == 0 else L
    nblk = L // blk
    qb = q.reshape(B, nblk, blk, H_A, 2, DQK_A).swapaxes(0, 1)
    pb = q_pos.reshape(nblk, blk)
    o = lax.map(lambda a: _diff_attn_block(a[0], k_all, v_all, a[1], k_pos, lam, slopes), (qb, pb))
    o = o.swapaxes(0, 1).reshape(B, L, H_A, DV_A)
    o = _rmsnorm(o, subln_g) * (1.0 - lam_init)
    return o.reshape(B, L, D_A)

def _short_conv(buf, x, w):
    L = x.shape[1]
    xx = jnp.concatenate([buf.astype(x.dtype), x], axis=1)
    y = xx[:, 0:L] * w[0]
    for i in range(1, CONV_W):
        y = y + xx[:, i:i + L] * w[i]
    return jax.nn.silu(y), xx[:, L:]

def _to_chunks(t, n, c):
    t = t.reshape((t.shape[0], n, c) + t.shape[2:])
    return jnp.moveaxis(t, 3, 1)

def _chunked_gated_delta(q, k, v, beta, g, s0):
    B, L = q.shape[0], q.shape[1]
    C = min(CHUNK, L)
    n = -(-L // C)
    pad = n * C - L
    if pad:
        pw = lambda t: jnp.pad(t, [(0, 0), (0, pad)] + [(0, 0)] * (t.ndim - 2))
        q, k, v, beta, g = pw(q), pw(k), pw(v), pw(beta), pw(g)
    q, k, v = _to_chunks(q, n, C), _to_chunks(k, n, C), _to_chunks(v, n, C)
    beta, g = _to_chunks(beta, n, C), _to_chunks(g, n, C)
    G = jnp.cumsum(g, axis=-1)
    diff = G[..., :, None] - G[..., None, :]
    tril = jnp.tril(jnp.ones((C, C), dtype=bool))
    strict = jnp.tril(jnp.ones((C, C), dtype=bool), -1)
    decay = jnp.exp(jnp.where(tril, diff, -jnp.inf))
    kb = k * beta[..., None]
    lmat = jnp.where(strict, jnp.einsum('bhnid,bhnjd->bhnij', kb, k) * decay, 0.0)
    lhs = lmat + jnp.eye(C, dtype=jnp.float32)
    rhs = jnp.concatenate([v * beta[..., None], kb * jnp.exp(G)[..., None]], axis=-1)
    sol = lax.linalg.triangular_solve(lhs, rhs, left_side=True, lower=True, unit_diagonal=True)
    u, w = sol[..., :DV_B], sol[..., DV_B:]
    qk = jnp.einsum('bhnid,bhnjd->bhnij', q, k) * decay
    q_dec = q * jnp.exp(G)[..., None]
    k_dec = k * jnp.exp(G[..., -1:] - G)[..., None]
    g_tot = jnp.exp(G[..., -1])

    def step(S, xs):
        u_c, w_c, qk_c, qd_c, kd_c, gt_c = xs
        v_new = u_c - jnp.einsum('bhck,bhkv->bhcv', w_c, S)
        o = jnp.einsum('bhck,bhkv->bhcv', qd_c, S) + jnp.einsum('bhij,bhjv->bhiv', qk_c, v_new)
        S = S * gt_c[..., None, None] + jnp.einsum('bhck,bhcv->bhkv', kd_c, v_new)
        return S, o

    xs = tuple(jnp.moveaxis(t, 2, 0) for t in (u, w, qk, q_dec, k_dec, g_tot))
    s_fin, o = lax.scan(step, s0, xs)
    o = jnp.transpose(o, (1, 0, 3, 2, 4)).reshape(B, n * C, H_B, DV_B)[:, :L]
    return o, s_fin

def _gated_deltanet(qkv, b_raw, a_raw, z, conv_buf, s0, conv_w_l, a_log_l, dt_bias_l, norm_g):
    B, L = qkv.shape[0], qkv.shape[1]
    y, new_buf = _short_conv(conv_buf, qkv, conv_w_l)
    qc, kc, vc = jnp.split(y, 3, axis=-1)
    q = _l2norm(qc.reshape(B, L, H_B, DK_B)) * (DK_B ** -0.5)
    k = _l2norm(kc.reshape(B, L, H_B, DK_B))
    v = vc.reshape(B, L, H_B, DV_B).astype(jnp.float32)
    beta = jax.nn.sigmoid(b_raw.astype(jnp.float32))
    g = -jnp.exp(a_log_l.astype(jnp.float32)) * jax.nn.softplus(a_raw.astype(jnp.float32) + dt_bias_l.astype(jnp.float32))
    o, s_new = _chunked_gated_delta(q, k, v, beta, g, s0.astype(jnp.float32))
    o = _rmsnorm(o, norm_g) * jax.nn.silu(z.reshape(B, L, H_B, DV_B).astype(jnp.float32))
    return o.reshape(B, L, D_B).astype(qkv.dtype), new_buf, s_new.astype(s0.dtype)

def _swiglu(x, w_up, w_down):
    gt, up = jnp.split(x @ w_up, 2, axis=-1)
    return (jax.nn.silu(gt) * up) @ w_down

def _moe_swiglu(x, w_r, b_r, w_up, w_down):
    logits = (x @ w_r + b_r).astype(jnp.float32)
    top_v, top_i = lax.top_k(logits, TOP_K)
    gates = jax.nn.softmax(top_v, axis=-1)
    gate_e = jnp.sum(jax.nn.one_hot(top_i, N_EXPERTS, dtype=jnp.float32) * gates[..., None], axis=-2).astype(x.dtype)
    y = jnp.zeros_like(x)
    for e in range(N_EXPERTS):
        y = y + gate_e[..., e:e + 1] * _swiglu(x, w_up[e], w_down[e])
    return y

def _trunk(x, c, pos0, conv_bufs, delta_states, past_k, past_v, weights):
    (w_in, w_out, lam_params, subln_a, conv_w, a_log, dt_bias, norm_b, ada_w, ada_b,
     ln1_g, ln1_b, ln2_g, ln2_b, dense_w_up, dense_w_down,
     moe_router, moe_router_b, moe_w_up, moe_w_down) = weights
    B, L = x.shape[0], x.shape[1]
    q_pos = pos0 + jnp.arange(L, dtype=jnp.int32)
    new_k, new_v, new_conv, new_delta = [], [], [], []
    for l in range(DEPTH):
        mod = jax.nn.silu(c) @ ada_w[l] + ada_b[l]
        sh1, sc1, g1, sh2, sc2, g2 = [m[:, None, :] for m in jnp.split(mod, 6, axis=-1)]
        h = _layernorm(x) * (1.0 + sc1) + sh1
        proj = h @ w_in[l]
        qa, ka, va, qkv_b, b_raw, a_raw, z = jnp.split(proj, SPLIT_IDX, axis=-1)
        k_heads = ka.reshape(B, L, H_A, 2 * DQK_A)
        v_heads = va.reshape(B, L, H_A, DV_A)
        new_k.append(k_heads)
        new_v.append(v_heads)
        if past_k is None:
            k_all, v_all = k_heads, v_heads
        else:
            k_all = jnp.concatenate([past_k[l].astype(k_heads.dtype), k_heads], axis=1)
            v_all = jnp.concatenate([past_v[l].astype(v_heads.dtype), v_heads], axis=1)
        o_a = _diff_attention(qa.reshape(B, L, H_A, 2, DQK_A), k_all, v_all, q_pos, lam_params[l], subln_a[l], l)
        o_b, buf_l, s_l = _gated_deltanet(qkv_b, b_raw, a_raw, z, conv_bufs[l], delta_states[l],
                                          conv_w[l], a_log[l], dt_bias[l], norm_b[l])
        new_conv.append(buf_l)
        new_delta.append(s_l)
        mix = jnp.concatenate([o_a, o_b], axis=-1) @ w_out[l]
        x = _layernorm(ALPHA * x + g1 * mix) * ln1_g[l] + ln1_b[l]
        h2 = _layernorm(x) * (1.0 + sc2) + sh2
        if l % 2 == 0:
            f = _swiglu(h2, dense_w_up[l // 2], dense_w_down[l // 2])
        else:
            j = l // 2
            f = _moe_swiglu(h2, moe_router[j], moe_router_b[j], moe_w_up[j], moe_w_down[j])
        x = _layernorm(ALPHA * x + g2 * f) * ln2_g[l] + ln2_b[l]
    return x, jnp.stack(new_k), jnp.stack(new_v), jnp.stack(new_conv), jnp.stack(new_delta)

def setup_inputs(seed: int = 0) -> dict:
    key = jax.random.key(seed)
    ks = iter(jax.random.split(key, 40))
    f32 = jnp.float32

    def nrm(shape, s):
        return jax.random.normal(next(ks), shape, f32) * s

    n_pages = PAST_LEN // PAGE_SIZE
    n_used = DEC_BATCH * n_pages
    n_pool = (n_used * 5) // 4
    x_prompt = nrm((BATCH, SEQ, D_MODEL), 1.0)
    x_sample = nrm((DEC_BATCH, DEC_SEQ, D_MODEL), 1.0)
    cache_k = nrm((DEPTH, n_pool, PAGE_SIZE, H_A, 2 * DQK_A), 1.0)
    cache_v = nrm((DEPTH, n_pool, PAGE_SIZE, H_A, DV_A), 0.5)
    state_conv = nrm((DEPTH, DEC_BATCH, CONV_W - 1, 3 * D_B), 0.5)
    state_delta = nrm((DEPTH, DEC_BATCH, H_B, DK_B, DV_B), 0.05)
    page_table = jax.random.permutation(next(ks), n_pool)[:n_used].reshape(DEC_BATCH, n_pages).astype(jnp.int32)
    c_prompt = nrm((BATCH, D_MODEL), 1.0)
    c_sample = nrm((DEC_BATCH, D_MODEL), 1.0)
    col_scale = jnp.concatenate([jnp.ones((A_Q + A_K,), f32), jnp.full((A_V,), BETA_INIT, f32),
                                 jnp.ones((2 * D_B,), f32), jnp.full((D_B,), BETA_INIT, f32),
                                 jnp.ones((B_BETA + B_DECAY + B_GATE,), f32)])
    w_in = nrm((DEPTH, D_MODEL, D_IN), D_MODEL ** -0.5) * col_scale
    w_out = nrm((DEPTH, D_MIX, D_MODEL), BETA_INIT * D_MIX ** -0.5)
    lam_params = nrm((DEPTH, 4, DQK_A), 0.1)
    subln_a = 1.0 + nrm((DEPTH, DV_A), 0.02)
    conv_w = nrm((DEPTH, CONV_W, 3 * D_B), CONV_W ** -0.5)
    a_log = jnp.log(jax.random.uniform(next(ks), (DEPTH, H_B), f32, minval=1.0, maxval=16.0))
    dt = jnp.exp(jax.random.uniform(next(ks), (DEPTH, H_B), f32, minval=math.log(1e-3), maxval=math.log(1e-1)))
    dt_bias = dt + jnp.log(-jnp.expm1(-dt))
    norm_b = 1.0 + nrm((DEPTH, DV_B), 0.02)
    ada_w = nrm((DEPTH, D_MODEL, 6 * D_MODEL), 0.5 * D_MODEL ** -0.5)
    ada_b = nrm((DEPTH, 6 * D_MODEL), 0.01)
    ln1_g = 1.0 + nrm((DEPTH, D_MODEL), 0.02)
    ln1_b = nrm((DEPTH, D_MODEL), 0.02)
    ln2_g = 1.0 + nrm((DEPTH, D_MODEL), 0.02)
    ln2_b = nrm((DEPTH, D_MODEL), 0.02)
    dense_w_up = nrm((N_DENSE, D_MODEL, 2 * D_FF), D_MODEL ** -0.5)
    dense_w_down = nrm((N_DENSE, D_FF, D_MODEL), BETA_INIT * D_FF ** -0.5)
    moe_router = nrm((N_MOE, D_MODEL, N_EXPERTS), D_MODEL ** -0.5)
    moe_router_b = nrm((N_MOE, N_EXPERTS), 0.01)
    moe_w_up = nrm((N_MOE, N_EXPERTS, D_MODEL, 2 * D_FF_E), D_MODEL ** -0.5)
    moe_w_down = nrm((N_MOE, N_EXPERTS, D_FF_E, D_MODEL), BETA_INIT * D_FF_E ** -0.5)
    return {'x_prompt': x_prompt, 'x_sample': x_sample, 'cache_k': cache_k, 'cache_v': cache_v,
            'state_conv': state_conv, 'state_delta': state_delta, 'page_table': page_table,
            'c_prompt': c_prompt, 'c_sample': c_sample, 'w_in': w_in, 'w_out': w_out,
            'lam_params': lam_params, 'subln_a': subln_a, 'conv_w': conv_w, 'a_log': a_log,
            'dt_bias': dt_bias, 'norm_b': norm_b, 'ada_w': ada_w, 'ada_b': ada_b,
            'ln1_g': ln1_g, 'ln1_b': ln1_b, 'ln2_g': ln2_g, 'ln2_b': ln2_b,
            'dense_w_up': dense_w_up, 'dense_w_down': dense_w_down,
            'moe_router': moe_router, 'moe_router_b': moe_router_b,
            'moe_w_up': moe_w_up, 'moe_w_down': moe_w_down}

def reference(x_prompt, x_sample, cache_k, cache_v, state_conv, state_delta, page_table,
              c_prompt, c_sample, w_in, w_out, lam_params, subln_a, conv_w, a_log, dt_bias,
              norm_b, ada_w, ada_b, ln1_g, ln1_b, ln2_g, ln2_b, dense_w_up, dense_w_down,
              moe_router, moe_router_b, moe_w_up, moe_w_down):
    weights = (w_in, w_out, lam_params, subln_a, conv_w, a_log, dt_bias, norm_b, ada_w, ada_b,
               ln1_g, ln1_b, ln2_g, ln2_b, dense_w_up, dense_w_down,
               moe_router, moe_router_b, moe_w_up, moe_w_down)
    nbp = x_prompt.shape[0]
    conv0 = jnp.zeros((DEPTH, nbp, CONV_W - 1, 3 * D_B), x_prompt.dtype)
    delta0 = jnp.zeros((DEPTH, nbp, H_B, DK_B, DV_B), x_prompt.dtype)
    y_prompt, k_prompt, v_prompt, conv_prompt, delta_prompt = _trunk(
        x_prompt, c_prompt, 0, conv0, delta0, None, None, weights)
    nbs, n_pages = page_table.shape
    past_len = n_pages * cache_k.shape[2]
    past_k = [cache_k[l][page_table].reshape(nbs, past_len, H_A, 2 * DQK_A) for l in range(DEPTH)]
    past_v = [cache_v[l][page_table].reshape(nbs, past_len, H_A, DV_A) for l in range(DEPTH)]
    y_sample, k_sample, v_sample, conv_sample, delta_sample = _trunk(
        x_sample, c_sample, past_len, state_conv, state_delta, past_k, past_v, weights)
    return (y_prompt, y_sample, k_prompt, v_prompt, conv_prompt, delta_prompt,
            k_sample, v_sample, conv_sample, delta_sample)


_drawn_inputs = setup_inputs


def setup_inputs(seed=0):
    import zlib

    import numpy as np

    out = dict(_drawn_inputs(seed))
    spreads = {}
    factors = {'lam_params': 5.885,
     'subln_a': 37.943,
     'norm_b': 40.652,
     'ada_b': 2.745,
     'moe_router_b': 117.123}
    for name, (base, spread) in spreads.items():
        noise = np.random.default_rng([zlib.crc32(name.encode()), seed]).standard_normal(out[name].shape)
        drawn = base * np.exp(spread * noise) if base else spread * noise
        out[name] = __import__('jax').numpy.asarray(drawn.astype(out[name].dtype))
    for name, factor in factors.items():
        out[name] = (out[name] * factor).astype(out[name].dtype)
    return out
```

```python
from contextlib import ExitStack
import math

import numpy as np

import concourse.bass as bass
from concourse import mybir

ALU = mybir.AluOpType
ACT = mybir.ActivationFunctionType
AX = mybir.AxisListType
F32 = mybir.dt.float32
I32 = mybir.dt.int32

P = 128
D = 1024
KT = D // P
SEQ = 256
NSEQ = 8
DSEQ = 8
NS = NSEQ * DSEQ
NTOK = SEQ + NS
DEPTH = 2
H = 4
DQK = 64
PAST = 1024
PAGE = 128
NPG = PAST // PAGE
NPOOL = 80
FF = 2816
FT = FF // P
NE = 8
CW = 4
D_IN = 3592
PB = 3 + SEQ + NSEQ * (3 + DSEQ) + 1
ALPHA = (2 * DEPTH) ** 0.25
LN_EPS = 1e-5
NEG = -1e30
LAM_INIT = [0.8 - 0.6 * math.exp(-0.3 * l) for l in range(DEPTH)]
SLOPE = [2.0 ** (-8.0 * (h + 1) / H) for h in range(H)]
LEVELS = [1, 2, 4, 8, 16, 32, 64]
TILES = [(0, 128), (128, 128), (256, 64)]

RING = 6
CH = 256
ADA_CH = 6 * D // CH
WIN_COLS = [0, 256, 512, 768] + [1536 + 256 * j for j in range(6)] + [3080, 3336]
N_WIN = len(WIN_COLS)
N_VO = 6
UP = FF // CH
DN_ROWS = [(0, 8), (8, 8), (16, 6)]
MLP_CH = 2 * UP + 4 * len(DN_ROWS)
MLP_POS = 36
POS_WIN = [2 * ADA_CH, 2 * ADA_CH + N_WIN + N_VO + MLP_POS]
POS_VO = [p + N_WIN for p in POS_WIN]
POS_MLP = [p + N_VO for p in POS_VO]

C_ID, C_TRI, C_TRIS, C_SAME, C_LEV = 0, 128, 256, 320, 384
C_SEQM = C_LEV + 7 * 128
C_LOW = C_SEQM + 8
C_ROW = C_LOW + 64
NC = C_ROW + 3


def constant_tables():
    c = np.zeros((P, NC), np.float32)
    j, i = np.arange(P)[:, None], np.arange(P)[None, :]
    c[:, C_ID:C_ID + P] = j == i
    c[:, C_TRI:C_TRI + P] = j <= i
    js, is_ = j[:NS], i[:, :NS]
    c[:NS, C_TRIS:C_TRIS + NS] = (js <= is_) & (js // DSEQ == is_ // DSEQ)
    c[:NS, C_SAME:C_SAME + NS] = js // DSEQ == is_ // DSEQ
    for n, s in enumerate(LEVELS):
        c[:, C_LEV + n * P:C_LEV + (n + 1) * P] = (i // (2 * s) == j // (2 * s)) & (i % (2 * s) >= s) & (j % (2 * s) < s)
    c[:NS, C_SEQM:C_SEQM + 8] = np.arange(NS)[:, None] // DSEQ == np.arange(8)[None, :]
    e, f = np.arange(8)[:, None], np.arange(8)[None, :]
    c[:, C_LOW:C_LOW + 64] = (f < e).astype(np.float32).reshape(1, 64)
    row = np.arange(64)
    c[:64, C_ROW] = [SLOPE[r // 16] for r in row]
    c[:64, C_ROW + 1] = (row // 8) % 2 == 0
    c[:64, C_ROW + 2] = (row // 8) % 2 == 1
    dp = np.full((P, 2, SEQ), NEG, np.float32)
    for qt in range(2):
        q, k = qt * P + np.arange(P)[:, None], np.arange(SEQ)[None, :]
        dp[:, qt] = np.where(q >= k, k - q, NEG)
    t = (row % 8)[:, None]
    ds = (np.arange(PAST)[None, :] - (PAST + t)).astype(np.float32)
    dn = np.full((64, NSEQ, NS), NEG, np.float32)
    for s in range(NSEQ):
        for u in range(DSEQ):
            dn[:, s, s * DSEQ + u] = np.where(u <= t[:, 0], u - t[:, 0], NEG)
    return c, dp.reshape(P, 2 * SEQ), ds, dn.reshape(64, NSEQ * NS)


class Chain:

    def __init__(self, eng, sem):
        self.eng, self.sem, self.n, self.extra, self.start = eng, sem, 0, 0, 0

    def __call__(self, ins):
        self.n += 1
        ins.then_inc(self.sem, 1)
        self.eng.wait_ge(self.sem, self.extra + self.n)

    def loop(self, reg, per):
        self.extra, self.start = reg * per, self.n

    def done(self, per, times):
        assert self.n - self.start == per, (self.n - self.start, per)
        self.extra, self.n = 0, self.start + per * times


def trunk_kernel(nc, x_p, x_s, cache_k, cache_v, st_conv, st_delta, ptab, c_p, c_s, w_in, w_out, lam_p,
                 subln, conv_w, a_log, dt_bias, norm_b, ada_w, ada_b, ln1_g, ln1_b, ln2_g, ln2_b,
                 dw_up, dw_dn, m_r, m_rb, mw_up, mw_dn, t_c, t_dp, t_ds, t_dn,
                 y_p, y_s, k_p, v_p, cv_p, dl_p, k_s, v_s, cv_s, dl_s):
    with ExitStack() as ctx:
        def sb(name, shape, dt=F32):
            return ctx.enter_context(nc.sbuf_tensor(name, shape, dt))

        def sem(name):
            return ctx.enter_context(nc.semaphore(name))

        ps = ctx.enter_context(nc.psum_tensor("ps", [P, 8, 512], F32))

        xT = sb("xT", [P, KT, NTOK])
        hT = sb("hT", [P, KT, NTOK])
        mixT = sb("mixT", [P, KT, NTOK])
        big = sb("big", [P, 12 * NTOK + 12 * PB])
        pA = big[:, 0:12 * NTOK].rearrange("p (f t) -> p f t", t=NTOK)
        pB = big[:, 12 * NTOK:].rearrange("p (f t) -> p f t", t=PB)
        pBs = pB[:, :, 3 + SEQ:3 + SEQ + 88].rearrange("p f (s r) -> p f s r", r=3 + DSEQ)
        xc = big[:, 0:KT * NTOK].rearrange("p (f t) -> p f t", t=NTOK)
        sq = big[:, KT * NTOK:2 * KT * NTOK].rearrange("p (f t) -> p f t", t=NTOK)
        ff = big[:, 0:FT * NTOK].rearrange("p (f t) -> p f t", t=NTOK)
        xrow = big[:, 0:3 * D].rearrange("p (a n) -> p a n", a=3)
        yrow = xrow
        va = sb("va", [P, 3, 512])
        ring = sb("ring", [P, RING, KT * CH])
        mod = sb("mod", [P, DEPTH, 48, 9])
        vrow = sb("vrow", [P, 4, P])
        vecT = sb("vecT", [P, 3, P])
        siluC = sb("siluC", [P, KT, 9])
        C = sb("C", [P, NC])
        dP = sb("dP", [P, 2, SEQ])
        dS = sb("dS", [64, PAST])
        dN = sb("dN", [64, NSEQ, NS])
        onesm = sb("onesm", [P, P])
        mean1 = sb("mean1", [P, P])
        cols = sb("cols", [P, 4])
        rstd = sb("rstd", [P, 2, NTOK])
        lnv = sb("lnv", [P, NTOK])
        wba = sb("wba", [P, DEPTH, KT, 8])
        wr = sb("wr", [P, KT, NE])
        small = sb("small", [P, 128])
        lamb = sb("lamb", [P, DEPTH, 256])
        lamw = sb("lamw", [P, 8])
        lamc = sb("lamc", [P, DEPTH, 2])
        adt = sb("adt", [P, 2, DEPTH, H])
        brb = sb("brb", [P, NE])
        pt_sb = sb("pt_sb", [1, NSEQ * NPG], I32)
        rowb = mixT[:, :, :].rearrange("p k t -> p (k t)")[0:27, 0:3 * 512]
        tail = sb("tail", [P, 12, 27])
        kst = sb("kst", [P, 3, 512])
        ctmp = sb("ctmp", [P, 2, NTOK])
        Sp = sb("Sp", [P, H, P])
        region = sb("region", [P, 12512])
        off = [0]

        def cut(n):
            off[0] += n
            assert off[0] <= 12512, off[0]
            return region[:, off[0] - n:off[0]]

        vring = cut(8 * 512).rearrange("p (a n) -> p a n", a=8)
        kring = cut(4 * 512).rearrange("p (a n) -> p a n", a=4)
        ktb = cut(2 * 512).rearrange("p (a n) -> p a n", a=2)
        scb = cut(2 * (PAST + NS)).rearrange("p (a n) -> p a n", a=2)
        ptb = cut(9 * 64).rearrange("p (a n) -> p a n", a=9)
        atb = cut(9 * 32).rearrange("p (a n) -> p a n", a=9)
        qbd = cut(2 * 256).rearrange("p (a h n) -> p a h n", a=2, h=H)
        oA = cut(H * NTOK).rearrange("p (h t) -> p h t", h=H)
        ptr = cut(2 * 256).rearrange("p (a n) -> p a n", a=2)
        off[0] = 0
        Ss = cut(NSEQ * H * P).rearrange("p (s h v) -> p s h v", s=NSEQ, h=H)
        g4 = lambda: cut(512)
        Gb_e, bbs, DT, LT, QK, LM, X, XT, PP, rT, rr, vn, kd, qd, oG, sG = [g4() for _ in range(16)]
        kdm = DT, LT
        off[0] = 0
        gateB = cut(NE * NTOK).rearrange("p (e t) -> p e t", e=NE)
        dtmp = cut(2 * NTOK).rearrange("p (a t) -> p a t", a=2)
        sil = kst[:, :, :].rearrange("p a n -> p (a n)")[:, 0:4 * NTOK].rearrange("p (b a t) -> p b a t", b=2, a=2)

        ident = C[:, C_ID:C_ID + P]
        tri = C[:, C_TRI:C_TRI + P]

        def c3(t, a):
            return t.rearrange("p (h t) -> p h t", h=H)[:, :, 0:a]

        s_tab = sem("tables_loaded")
        s_pt = sem("page_table_loaded")
        s_ones = sem("ones_written")
        s_full = [sem(f"chunk_loaded_{i}") for i in range(RING)]
        s_chunk = sem("chunk_done")
        s_vecT = sem("vectors_transposed")
        s_vec = sem("vectors_copied")
        s_xt = sem("x_transposed")
        s_silc = sem("silu_c")
        s_modev = sem("mod_copied")
        s_mod = sem("mod_ready")
        s_lnin = sem("ln_input")
        s_mean = sem("ln_mean")
        s_xc = sem("ln_centered")
        s_sq = sem("ln_squared")
        s_var = sem("ln_var")
        s_rstd = sem("ln_rstd")
        s_xn = sem("ln_scaled")
        s_h = sem("h_prompt")
        s_hs = sem("h_sample")
        s_xa = sem("x_times_alpha")
        s_pev = sem("proj_copied")
        s_va = sem("v_rows")
        s_ba = sem("ba_done")
        s_bae = sem("ba_copied")
        s_hist = sem("history_loaded")
        s_histT = sem("history_transposed")
        s_histc = sem("history_placed")
        s_kT = sem("k_rows_psum")
        s_kst = sem("k_rows")
        s_tail = sem("tail_gathered")
        s_tailT = sem("tail_transposed")
        s_tailc = sem("tail_rows")
        s_conv = sem("conv_done")
        s_csil = sem("conv_silu")
        s_l2q = sem("l2_squared")
        s_l2s = sem("l2_summed")
        s_l2r = sem("l2_rinv")
        s_l2d = sem("l2_done")
        s_lam = sem("lambda_ready")
        s_pS = sem("p_scores")
        s_pM = sem("p_max")
        s_pE = sem("p_exp")
        s_pA = sem("p_probs")
        s_pT = sem("p_probsT_psum")
        s_pTc = sem("p_probsT")
        s_pV = sem("p_pv")
        s_pO = sem("p_out")
        s_qbz = sem("q_blocks_zero")
        s_qb = sem("q_blocks")
        s_kf = [sem(f"k_page_{i}") for i in range(4)]
        s_vf = [sem(f"v_page_{i}") for i in range(8)]
        s_kt = sem("k_page_transposed")
        s_ktA = sem("k_page_copied_act")
        s_ktD = sem("k_page_copied_dve")
        s_kmm = sem("k_page_scored")
        s_sS = sem("s_scores")
        s_sM = sem("s_max")
        s_sE = sem("s_exp")
        s_sP = sem("s_probs")
        s_sT = sem("s_probsT_psum")
        s_sTc = sem("s_probsT")
        s_sA = sem("s_probs_diff")
        s_sV = sem("s_pv")
        s_sO = sem("s_out")
        s_oq = sem("attn_squared")
        s_os = sem("attn_summed")
        s_or = sem("attn_rstd")
        s_mA = sem("attn_mixed")
        s_bt = sem("beta_g_ready")
        s_bta = sem("beta_g_act")
        s_btd = sem("beta_g_dve")
        s_S0 = sem("state_loaded")
        s_gG = sem("g_sums")
        s_gGc = sem("g_sums_copied")
        s_gE = sem("g_exp")
        s_gK = sem("g_kk_kq_k")
        s_gL = sem("g_L_ready")
        s_gkd = sem("g_kdec")
        s_lm = sem("g_level_mask")
        s_g1 = sem("g_level_P")
        s_g1c = sem("g_level_P_copied")
        s_g2 = sem("g_level_Q")
        s_g2c = sem("g_level_updated")
        s_gR = sem("g_kS")
        s_gRc = sem("g_rT")
        s_gRt = sem("g_r_psum")
        s_gr = sem("g_r")
        s_gV = sem("g_vnew_psum")
        s_gv = sem("g_vnew")
        s_gO = sem("g_o_psum")
        s_go = sem("g_o")
        s_gS = sem("g_state_psum")
        s_gSc = sem("g_state")
        s_gkm = sem("g_kdec_masked")
        s_goq = sem("g_o_squared")
        s_gos = sem("g_o_summed")
        s_gor = sem("g_o_rstd")
        s_mB = sem("gdn_mixed")
        s_res = sem("wout_added")
        s_rt = sem("router_logits")
        s_rtm = sem("router_max")
        s_rte = sem("router_exp")
        s_gate = sem("gates_ready")
        s_gb = sem("gates_broadcast")
        s_gbc = sem("gates_copied")
        s_sil = sem("gate_silu")
        s_ff = sem("ff_ready")
        s_dn = sem("down_copied")
        s_turn = sem("values_begun")
        s_vturn = sem("v_pages_begun")
        s_yT = sem("y_rows_psum")
        s_y = sem("y_rows")
        s_out = sem("outputs_stored")
        s_cd = sem("dve_chain")
        s_ca = sem("act_chain")
        s_cp = sem("pool_chain")
        N_OUT = [0]

        block = ctx.enter_context(nc.Block())

        def full(pos, e=0):
            return s_full[pos % RING], 16 * (pos // RING + 1) + e * (16 * MLP_POS // RING)

        def chunk(pos):
            return ring[:, pos % RING, :].rearrange("p (k n) -> p k n", n=CH)

        def wsrc(w, col):
            return w[:, bass.ds(col, CH)].rearrange("(k p) n -> p k n", p=P)

        N_TAB = [0]

        def tables(sp):
            def ld(dst, src):
                N_TAB[0] += 16
                sp.dma_start(dst, src).then_inc(s_tab, 16)

            ld(C[:], t_c)
            ld(vrow[0:96, 0, :], ada_b.rearrange("l (f p) -> (l f) p", p=P))
            ld(vrow[96:98, 0, :], subln)
            ld(vrow[98:100, 0, :], norm_b)
            ld(vrow[0:96, 1, :], conv_w.rearrange("l w (f p) -> (l w f) p", p=P))
            for n, v in enumerate((ln1_g, ln1_b, ln2_g, ln2_b)):
                ld(vrow[16 * n:16 * n + 16, 2, :], v.rearrange("l (f p) -> (l f) p", p=P))
            ld(vrow[0:8, 3, :], c_p.rearrange("a (f p) -> (a f) p", p=P))
            ld(vrow[8:72, 3, :], c_s.rearrange("a (f p) -> (a f) p", p=P))
            ld(xrow[:, 0:2, :], x_p[0].rearrange("(a p) n -> p a n", p=P))
            ld(xrow[0:NS, 2, :], x_s.rearrange("s t n -> (s t) n"))
            ld(dP[:], t_dp.rearrange("p (a n) -> p a n", a=2))
            ld(dS[:], t_ds)
            ld(dN[:], t_dn.rearrange("p (a n) -> p a n", a=NSEQ))
            for l in range(DEPTH):
                ld(wba[:, l, :, :], w_in[l][:, 3072:3080].rearrange("(k p) n -> p k n", p=P))
                ld(lamb[:, l, :], lam_p[l:l + 1].rearrange("o a b -> o (a b)").to_broadcast([P, 256]))
                ld(adt[:, 0, l, :], a_log[l:l + 1, :].to_broadcast([P, H]))
                ld(adt[:, 1, l, :], dt_bias[l:l + 1, :].to_broadcast([P, H]))
            ld(wr[:], m_r[0].rearrange("(k p) n -> p k n", p=P))
            ld(brb[:], m_rb[0:1, :].to_broadcast([P, NE]))

        N_TABLES = 16 * 26

        @block.sync
        def _(sp):
            tables(sp)
            assert N_TAB[0] == N_TABLES, N_TAB[0]
            sp.dma_start(pt_sb[:], ptab.rearrange("(o a) b -> o (a b)", o=1)).then_inc(s_pt, 16)

            def load(dst, src, pos, e=0, first=False):
                if not first:
                    sp.wait_ge(s_chunk, pos - RING + 1 + e * MLP_POS)
                sp.dma_start(dst, src).then_inc(full(pos)[0], 16)

            for c in range(RING):
                load(chunk(c), wsrc(ada_w[0], CH * c), c, first=True)
            for l in range(DEPTH):
                with sp.Fori(1 if l == 0 else 0, ADA_CH // RING) as i:
                    for c in range(RING):
                        sp.wait_ge(s_chunk, ADA_CH * l + c - RING + 1 + i * RING)
                        sp.dma_start(chunk(c), wsrc(ada_w[l], i * (RING * CH) + CH * c)).then_inc(s_full[c], 16)

            def mlp(w_up, w_dn, pos, e=0):
                for j in range(UP):
                    for part in range(2):
                        p = pos + 2 * j + part
                        load(chunk(p), wsrc(w_up, part * FF + CH * j), p, e)
                for d in range(4):
                    for n, (f0, nf) in enumerate(DN_ROWS):
                        p = pos + 2 * UP + 3 * d + n
                        load(chunk(p)[:, 0:nf, :],
                             w_dn[f0 * P:(f0 + nf) * P, CH * d:CH * (d + 1)].rearrange("(k p) n -> p k n", p=P), p, e)
                for p in range(pos + MLP_CH, pos + MLP_POS):
                    sp.wait_ge(s_chunk, p - RING + 1 + e * MLP_POS)
                    sp.sem_inc(full(p)[0], 16)

            for l in range(DEPTH):
                for c in range(N_WIN):
                    load(chunk(POS_WIN[l] + c), wsrc(w_in[l], WIN_COLS[c]), POS_WIN[l] + c)
                if l > 0:
                    sp.wait_ge(s_chunk, POS_VO[l - 1] + N_VO)
                sp.dma_start(rowb[0:24, :], st_conv[l].rearrange("s r n -> (s r) n")).then_inc(s_hist, 16)
                for c in range(2):
                    load(chunk(POS_VO[l] + c), wsrc(w_in[l], 1024 + CH * c), POS_VO[l] + c)
                for c in range(4):
                    load(chunk(POS_VO[l] + 2 + c), wsrc(w_out[l], CH * c), POS_VO[l] + 2 + c)
                if l == 0:
                    mlp(dw_up[0], dw_dn[0], POS_MLP[0])
                else:
                    with sp.Fori(0, NE) as e:
                        mlp(mw_up[0, bass.ds(e, 1)].rearrange("o a b -> (o a) b"),
                            mw_dn[0, bass.ds(e, 1)].rearrange("o a b -> (o a) b"), POS_MLP[1], e)

        @block.gpsimd
        def _(pool):
            link = Chain(pool, s_cp)
            nc.gpsimd.memset(onesm[:], 1.0).then_inc(s_ones, 1)
            nc.gpsimd.memset(mean1[:], 1.0 / D).then_inc(s_ones, 1)
            nc.gpsimd.memset(cols[:, 0:1], LN_EPS).then_inc(s_ones, 1)
            nc.gpsimd.memset(cols[:, 1:2], 1e-6).then_inc(s_ones, 1)
            nc.gpsimd.memset(cols[:, 2:3], -0.5 * math.log(P)).then_inc(s_ones, 1)
            nc.gpsimd.memset(cols[:, 3:4], 1.0).then_inc(s_ones, 1)
            nc.gpsimd.memset(small[:], 0.0).then_inc(s_ones, 1)
            pool.wait_ge(s_pt, 16)
            n_out = 0

            def store(dst, src):
                pool.dma_start(dst, src).then_inc(s_out, 16)

            for l in range(DEPTH):
                if l > 0:
                    pool.wait_ge(s_mB, 3 * l)
                    pool.wait_ge(s_out, 16 * 8 * l)
                nc.gpsimd.memset(qbd[:], 0.0).then_inc(s_qbz, 1)

                def pages(s):
                    for p in range(NPG):
                        pg = pool.value_load(pt_sb[0:1, bass.ds(s * NPG + p, 1)], min_val=0, max_val=NPOOL - 1)
                        if p >= 4 or not isinstance(s, int) or s > 0 or l > 0:
                            pool.wait_ge(s_kt, 64 * l + s * NPG + p - 3)
                        pool.dma_start(kring[:, p % 4, :], cache_k[l, bass.ds(pg, 1)].rearrange("o k h d -> (o k) (h d)")
                                       ).then_inc(s_kf[p % 4], 16)
                    if not isinstance(s, int) or s > 0 or l > 0:
                        pool.wait_ge(s_sV, 8 * l + s)
                    pool.sem_inc(s_vturn, 1)
                    for p in range(NPG):
                        pg = pool.value_load(pt_sb[0:1, bass.ds(s * NPG + p, 1)], min_val=0, max_val=NPOOL - 1)
                        pool.dma_start(vring[:, p, :], cache_v[l, bass.ds(pg, 1)].rearrange("o k h d -> (o k) (h d)")
                                       ).then_inc(s_vf[p], 16)

                pages(0)
                with pool.Fori(1, NSEQ) as s:
                    pages(s)
                pool.wait_ge(s_va, 2 * (l + 1))
                store(v_p[l, 0].rearrange("(a p) h d -> p a (h d)", p=P), va[:, 0:2, :])
                store(v_s[l].rearrange("s t h d -> (s t) (h d)"), va[0:NS, 2, :])
                pool.wait_ge(s_kst, l + 1)
                store(k_p[l, 0].rearrange("(a p) h d -> p a (h d)", p=P), kst[:, 0:2, :])
                store(k_s[l].rearrange("s t h d -> (s t) (h d)"), kst[0:NS, 2, :])
                pool.wait_ge(s_tailc, l + 1)
                store(cv_p[l, 0], rowb[0:3, :])
                store(cv_s[l].rearrange("s r n -> (s r) n"), rowb[3:27, :])
                pool.wait_ge(s_mA, H * (l + 1))
                pool.dma_start(Ss, st_delta[l].rearrange("s h k v -> k s h v")).then_inc(s_S0, 16)
                pool.wait_ge(s_gSc, 34 * l + 2)
                store(dl_p[l, 0].rearrange("h k v -> k h v"), Sp[:])
                pool.wait_ge(s_gSc, 34 * l + 34)
                store(dl_s[l].rearrange("s h k v -> k s h v"), Ss)
            pool.wait_ge(s_y, 3)
            store(y_p[0].rearrange("(a p) n -> p a n", p=P), yrow[:, 0:2, :])
            store(y_s.rearrange("s t n -> (s t) n"), yrow[0:NS, 2, :])
            pool.wait_ge(s_out, 16 * 18)

        @block.tensor
        def _(pe):
            mm, tr = nc.tensor.matmul, nc.tensor.transpose

            def ln(n):
                for k in range(KT):
                    pe.wait_ge(s_lnin, KT * n + k + 1)
                    m = mm(ps[:, 0, 0:NTOK], mean1[:], xT[:, k, :], start=(k == 0), stop=(k == KT - 1))
                m.then_inc(s_mean, 1)
                for k in range(KT):
                    if k % 2 == 0:
                        pe.wait_ge(s_sq, 4 * n + k // 2 + 1)
                    m = mm(ps[:, 1, 0:NTOK], mean1[:], sq[:, k, :], start=(k == 0), stop=(k == KT - 1))
                m.then_inc(s_var, 1)

            def take(pos, e=0):
                pe.wait_ge(*full(pos, e))
                return chunk(pos)

            def two_tiles(w, b, rhs, n=NTOK, nk=KT, first=True, last=True):
                for o in range(2):
                    for k in range(nk):
                        m = mm(ps[:, b + o, 0:n], w[:, k, o * P:(o + 1) * P], rhs[:, k, :],
                               start=(first and k == 0), stop=(last and k == nk - 1))
                return m

            def h_ready(m):
                pe.wait_ge(s_h, KT * (m + 1))
                pe.wait_ge(s_hs, m + 1)

            def mlp(pos, e, nff, ndn, first):
                for j in range(UP):
                    b = 4 * (j % 2)
                    if j >= 2:
                        pe.wait_ge(s_ff, nff + j - 1)
                    elif not first:
                        pe.wait_ge(s_dn, ndn - 2 + 2 * j)
                    w = take(pos + 2 * j, e)
                    two_tiles(w, b, hT).then_inc(s_chunk, 1)
                    w = take(pos + 2 * j + 1, e)
                    two_tiles(w, b + 2, hT).then_inc(s_chunk, 1)
                pe.wait_ge(s_ff, nff + UP)
                for d in range(4):
                    for i, (f0, nf) in enumerate(DN_ROWS):
                        p = pos + 2 * UP + 3 * d + i
                        w = take(p, e)
                        m = None
                        for o in range(2):
                            for k in range(nf):
                                m = mm(ps[:, 2 * d + o, 0:NTOK], w[:, k, o * P:(o + 1) * P], ff[:, f0 + k, :],
                                       start=(i == 0 and k == 0), stop=(i == 2 and k == nf - 1))
                        m.then_inc(s_chunk, 1 + (MLP_POS - MLP_CH if d == 3 and i == 2 else 0))

            pe.wait_ge(s_tab, N_TABLES)
            pe.wait_ge(s_ones, 7)
            for b, n in enumerate((100, 96, 64, 72)):
                m = tr(ps[:, 0, b * P:b * P + n], vrow[0:n, b, :], ident[0:n, 0:n])
            m.then_inc(s_vecT, 1)
            for k in range(KT):
                if k >= 4:
                    pe.wait_ge(s_lnin, k - 3)
                for t, (c0, nt) in enumerate(TILES):
                    m = tr(ps[:, 1 + k % 4, c0:c0 + nt], xrow[0:nt, t, k * P:(k + 1) * P], ident[0:nt, 0:nt])
                m.then_inc(s_xt, 1)
            pe.wait_ge(s_silc, 1)
            def ada(i):
                for c in range(RING):
                    pe.wait_ge(s_full[c], 16 + 16 * i)
                    if c >= 2 or not isinstance(i, int):
                        pe.wait_ge(s_modev, c - 1 + i * RING)
                    for o in range(2):
                        for k in range(KT):
                            m = mm(ps[:, 6 + c % 2, 16 * o:16 * o + 9], chunk(c)[:, k, o * P:(o + 1) * P],
                                   siluC[:, k, :], start=(k == 0), stop=(k == KT - 1))
                    m.then_inc(s_chunk, 1)

            ada(0)
            with pe.Fori(1, DEPTH * ADA_CH // RING) as i:
                ada(i)

            for l in range(DEPTH):
                ln(4 * l)
                h_ready(2 * l)
                for c in range(N_WIN):
                    w = take(POS_WIN[l] + c)
                    if c >= 4:
                        pe.wait_ge(s_pev, N_WIN * l + c - 3)
                    two_tiles(w, 2 * (c % 4), hT).then_inc(s_chunk, 1)
                pe.wait_ge(s_pev, N_WIN * (l + 1))
                for t, (c0, nt) in enumerate(TILES):
                    for k in range(KT):
                        m = mm(ps[0:nt, 6, 8 * t:8 * t + 8], hT[:, k, c0:c0 + nt], wba[:, l, k, :],
                               start=(k == 0), stop=(k == KT - 1))
                m.then_inc(s_ba, 1)
                pe.wait_ge(s_hist, 16 * (l + 1))
                for f in range(12):
                    m = tr(ps[:, 7, 24 * f:24 * f + 24], rowb[0:24, f * P:(f + 1) * P], ident[0:24, 0:24])
                m.then_inc(s_histT, 1)
                for c in range(2):
                    w = take(POS_VO[l] + c)
                    for t, (c0, nt) in enumerate(TILES):
                        for k in range(KT):
                            m = mm(ps[0:nt, 3 * c + t, 0:CH], hT[:, k, c0:c0 + nt], w[:, k, :],
                                   start=(k == 0), stop=(k == KT - 1))
                    m.then_inc(s_chunk, 1)
                pe.wait_ge(s_va, 2 * (l + 1))
                for t, (c0, nt) in enumerate(TILES):
                    for h in range(H):
                        m = tr(ps[0:nt, t, h * P:(h + 1) * P], pA[:, 4 + h, c0:c0 + nt], ident)
                m.then_inc(s_kT, 1)
                pe.wait_ge(s_tail, l + 1)
                for f in range(12):
                    m = tr(ps[0:27, 3 + f // 4, (f % 4) * P:(f % 4 + 1) * P], tail[:, f, :], ident)
                m.then_inc(s_tailT, 1)
                pe.wait_ge(s_histc, l + 1)
                pe.wait_ge(s_bae, l + 1)
                for f in range(8):
                    pe.wait_ge(s_l2q, 8 * l + f + 1)
                    if f >= 2:
                        pe.wait_ge(s_l2r, 8 * l + f - 1)
                    mm(ps[:, 6 + f % 2, 0:NTOK], onesm[:], ctmp[:, f % 2, :], start=True, stop=True).then_inc(s_l2s, 1)

                units = [(h, qt) for h in range(H) for qt in range(2)]

                def scores(u):
                    h, qt = units[u]
                    nk = P * (qt + 1)
                    if u == 0:
                        pe.wait_ge(s_kst, l + 1)
                        pe.wait_ge(s_tailc, l + 1)
                        pe.wait_ge(s_l2r, 8 * (l + 1))
                    if u >= 2:
                        pe.wait_ge(s_pM, 8 * l + u - 1)
                    for m_ in range(2):
                        r = slice(64 * m_, 64 * m_ + 64)
                        m = mm(ps[:, 2 * (u % 2) + m_, 0:nk], pA[r, h, qt * P:(qt + 1) * P],
                               pA[r, 4 + h, 0:nk], start=True, stop=True)
                    m.then_inc(s_pS, 1)

                scores(0)
                for u, (h, qt) in enumerate(units):
                    if u + 1 < 8:
                        scores(u + 1)
                    pe.wait_ge(s_pA, 8 * l + u + 1)
                    if u >= 1:
                        pe.wait_ge(s_pTc, 8 * l + u)
                    for kb in range(qt + 1):
                        m = tr(ps[:, 4, kb * P:(kb + 1) * P], scb[:, u % 2, kb * P:(kb + 1) * P], ident)
                    m.then_inc(s_pT, 1)
                    pe.wait_ge(s_pTc, 8 * l + u + 1)
                    if u >= 2:
                        pe.wait_ge(s_pO, 8 * l + u - 1)
                    for kb in range(qt + 1):
                        m = mm(ps[:, 5 + u % 2, 0:P], va[:, kb, h * P:(h + 1) * P], ptr[:, u % 2, kb * P:(kb + 1) * P],
                               start=(kb == 0), stop=(kb == qt))
                    m.then_inc(s_pV, 1)

                pe.wait_ge(s_pO, 8 * (l + 1))

                def seq_scores(s, a):
                    base = 64 * l + s * NPG
                    pe.wait_ge(s_qb, 8 * l + s + 1)

                    def turn(p):
                        pe.wait_ge(s_kf[p % 4], 16 * (16 * l + 2 * s + p // 4 + 1))
                        cnt = 32 * l + s * 4 + p // 2
                        if isinstance(cnt, int) and cnt == 0:
                            pass
                        else:
                            pe.wait_ge(s_ktA if p % 2 == 0 else s_ktD, cnt)
                        for h in range(H):
                            m = tr(ps[:, p % 2, h * P:(h + 1) * P], kring[:, p % 4, h * P:(h + 1) * P], ident)
                        m.then_inc(s_kt, 1)

                    turn(0)
                    for p in range(NPG):
                        if p + 1 < NPG:
                            turn(p + 1)
                        pe.wait_ge(s_ktA if p % 2 == 0 else s_ktD, 32 * l + s * 4 + p // 2 + 1)
                        if p == 0:
                            pe.wait_ge(s_sM, 8 * l + s) if a else (pe.wait_ge(s_sM, 8 * l + s) if l or not isinstance(s, int) else None)
                        for h in range(H):
                            m = mm(ps[0:64, 2 + p // 4, (p % 4) * P:(p % 4 + 1) * P], qbd[:, a, h, :], ktb[:, p % 2, h * P:(h + 1) * P],
                                   start=(h == 0), stop=(h == H - 1))
                        m.then_inc(s_kmm, 1)
                    for h in range(H):
                        m = mm(ps[0:64, 4, 0:NS], qbd[:, a, h, :], pA[:, 4 + h, SEQ:NTOK], start=(h == 0), stop=(h == H - 1))
                    m.then_inc(s_sS, 1)

                def seq_values(s, a):
                    pe.wait_ge(s_sP, 8 * l + s + 1)
                    if a or l or not isinstance(s, int):
                        pe.wait_ge(s_sTc, 8 * l + s)
                    pe.sem_inc(s_turn, 1)
                    for p in range(NPG):
                        tr(ps[:, 5, p * 64:(p + 1) * 64], scb[0:64, a, p * P:(p + 1) * P], ident[0:64, 0:64])
                    tr(ps[0:64, 6, 0:64], scb[0:64, a, PAST:PAST + NS], ident[0:64, 0:64]).then_inc(s_sT, 1)
                    pe.wait_ge(s_sA, 8 * l + s + 1)
                    if a or l or not isinstance(s, int):
                        pe.wait_ge(s_sO, 8 * l + s)
                    for h in range(H):
                        for p in range(NPG):
                            if h == 0:
                                pe.wait_ge(s_vf[p], 16 * (8 * l + s + 1))
                            mm(ps[:, 7, h * 8:h * 8 + 8], vring[:, p, h * P:(h + 1) * P], atb[:, p, h * 8:h * 8 + 8],
                               start=(p == 0), stop=False)
                        m = mm(ps[:, 7, h * 8:h * 8 + 8], va[0:NS, 2, h * P:(h + 1) * P], atb[0:NS, 8, h * 8:h * 8 + 8],
                               start=False, stop=True)
                    m.then_inc(s_sV, 1)

                def pair(i):
                    seq_scores(2 * i, 0)
                    seq_scores(2 * i + 1, 1)
                    seq_values(2 * i, 0)
                    seq_values(2 * i + 1, 1)

                pair(0)
                with pe.Fori(1, NSEQ // 2) as i:
                    pair(i)

                for h in range(H):
                    pe.wait_ge(s_oq, H * l + h + 1)
                    if h >= 2:
                        pe.wait_ge(s_or, H * l + h - 1)
                    mm(ps[:, h % 2, 0:NTOK], onesm[:], ctmp[:, h % 2, :], start=True, stop=True).then_inc(s_os, 1)

                pe.wait_ge(s_or, H * (l + 1))
                pe.wait_ge(s_bt, l + 1)
                pe.wait_ge(s_l2d, 8 * (l + 1))
                for T, (c0, nt) in enumerate(TILES):
                    n = 3 * l + T
                    smp = T == 2
                    lev = 3 if smp else 7
                    triT = C[0:nt, C_TRIS:C_TRIS + nt] if smp else tri
                    same = C[0:nt, C_SAME:C_SAME + nt] if smp else onesm[:]
                    if n > 0:
                        pe.wait_ge(s_mB, n)
                    gcol = small[0:nt, 24 + 4 * T:28 + 4 * T]
                    bcol = small[0:nt, 36 + 4 * T:40 + 4 * T]
                    mm(ps[0:nt, 0, 0:4], triT, gcol, start=True, stop=True)
                    mm(ps[0:nt, 0, 4:8], same, gcol, start=True, stop=True)
                    for h in range(H):
                        mm(ps[:, 1, h * P:h * P + nt], gcol[:, h:h + 1].to_broadcast([nt, P]), triT, start=True, stop=True)
                    for h in range(H):
                        m = mm(ps[:, 2, h * P:h * P + nt], bcol[:, h:h + 1].to_broadcast([nt, P]), ident[0:nt, 0:nt],
                               start=True, stop=True)
                    m.then_inc(s_gG, 1)
                    kT = pB[:, 4:8, c0:c0 + nt]
                    qT = pB[:, 0:4, c0:c0 + nt]
                    for h in range(H):
                        mm(ps[0:nt, 3, h * P:h * P + nt], kT[:, h, :], kT[:, h, :], start=True, stop=True)
                    for h in range(H):
                        mm(ps[0:nt, 4, h * P:h * P + nt], kT[:, h, :], qT[:, h, :], start=True, stop=True)
                    for h in range(H):
                        m = tr(ps[0:nt, 5, h * P:(h + 1) * P], kT[:, h, :], ident)
                    m.then_inc(s_gK, 1)
                    LM3, X3, XT3, PP3 = c3(LM, nt), c3(X, nt), c3(XT, nt), c3(PP, nt)
                    for v in range(lev):
                        i0 = 17 * l + 7 * T + v
                        pe.wait_ge(s_lm, i0 + 1)
                        for h in range(H):
                            m = mm(ps[0:nt, 6, h * P:h * P + nt], LM3[0:nt, h, :], X3[0:nt, h, :], start=True, stop=True)
                        m.then_inc(s_g1, 1)
                        pe.wait_ge(s_g1c, i0 + 1)
                        for h in range(H):
                            mm(ps[0:nt, 7, h * P:h * P + nt], XT3[0:nt, h, :], PP3[0:nt, h, :], start=True, stop=True)
                        if v == 0:
                            pe.wait_ge(s_gE, n + 1)
                        for h in range(H):
                            m = mm(ps[0:nt, 0, h * P:h * P + nt], PP3[0:nt, h, :], XT3[0:nt, h, :], start=True, stop=True)
                        m.then_inc(s_g2, 1)
                    if smp:
                        pe.wait_ge(s_S0, 16 * (l + 1))
                    if T == 1:
                        pe.wait_ge(s_gSc, 34 * l + 1)
                    for h in range(H):
                        if smp:
                            for s in range(NSEQ):
                                m = mm(ps[:, 1, h * P + 8 * s:h * P + 8 * s + 8], Ss[:, s, h, :], kT[:, h, 8 * s:8 * s + 8],
                                       start=True, stop=True)
                        else:
                            m = mm(ps[:, 1, h * P:h * P + nt], Sp[:, h, :], kT[:, h, :], start=True, stop=True)
                    m.then_inc(s_gR, 1)
                    pe.wait_ge(s_gRc, n + 1)
                    for h in range(H):
                        m = tr(ps[0:nt, 2, h * P:(h + 1) * P], c3(rT, nt)[:, h, :], ident)
                    m.then_inc(s_gRt, 1)
                    pe.wait_ge(s_gr, n + 1)
                    pe.wait_ge(s_g2c, 17 * l + 7 * T + lev)
                    for h in range(H):
                        m = mm(ps[0:nt, 3, h * P:(h + 1) * P], XT3[0:nt, h, :], c3(rr, P)[0:nt, h, :], start=True, stop=True)
                    m.then_inc(s_gV, 1)
                    pe.wait_ge(s_gv, n + 1)
                    for h in range(H):
                        mm(ps[:, 4, h * P:h * P + nt], c3(vn, P)[0:nt, h, :], c3(QK, nt)[0:nt, h, :], start=True, stop=False)
                        if smp:
                            for s in range(NSEQ):
                                m = mm(ps[:, 4, h * P + 8 * s:h * P + 8 * s + 8], Ss[:, s, h, :], c3(qd, nt)[:, h, 8 * s:8 * s + 8],
                                       start=False, stop=(s == NSEQ - 1))
                        else:
                            m = mm(ps[:, 4, h * P:h * P + nt], Sp[:, h, :], c3(qd, nt)[:, h, :], start=False, stop=True)
                    m.then_inc(s_gO, 1)
                    if smp:
                        for h in range(H):
                            pe.wait_ge(s_gkm, H * l + h + 1)
                            if h > 0:
                                pe.wait_ge(s_gSc, 34 * l + 2 + 8 * h)
                            for s in range(NSEQ):
                                m = mm(ps[:, 5 + s // 4, (s % 4) * P:(s % 4 + 1) * P], kdm[s // 4][0:nt, (s % 4) * P:(s % 4 + 1) * P],
                                       c3(vn, P)[0:nt, h, :], start=True, stop=True)
                            m.then_inc(s_gS, 1)
                    else:
                        pe.wait_ge(s_gkd, n + 1)
                        for h in range(H):
                            m = mm(ps[:, 5, h * P:(h + 1) * P], c3(kd, P)[0:nt, h, :], c3(vn, P)[0:nt, h, :], start=True, stop=True)
                        m.then_inc(s_gS, 1)
                    pe.wait_ge(s_goq, n + 1)
                    mm(ps[:, 7, 0:H * nt], onesm[:], sG[:, 0:H * nt], start=True, stop=True).then_inc(s_gos, 1)

                pe.wait_ge(s_mB, 3 * (l + 1))
                pe.wait_ge(s_mA, H * (l + 1))
                for c in range(4):
                    w = take(POS_VO[l] + 2 + c)
                    two_tiles(w, 2 * c, mixT).then_inc(s_chunk, 1)
                ln(4 * l + 1)
                ln(4 * l + 2)
                h_ready(2 * l + 1)
                if l == 0:
                    mlp(POS_MLP[0], 0, 0, 0, True)
                else:
                    for t, (c0, nt) in enumerate(TILES):
                        for k in range(KT):
                            m = mm(ps[0:nt, 2, 8 * t:8 * t + 8], hT[:, k, c0:c0 + nt], wr[:, k, :], start=(k == 0), stop=(k == KT - 1))
                    m.then_inc(s_rt, 1)
                    pe.wait_ge(s_gate, 1)
                    for e in range(NE):
                        if e >= 4:
                            pe.wait_ge(s_gbc, e - 3)
                        for t, (c0, nt) in enumerate(TILES):
                            m = mm(ps[:, 4 + e % 4, c0:c0 + nt], small[0:nt, 72 + 8 * t + e:73 + 8 * t + e].to_broadcast([nt, P]),
                                   ident[0:nt, 0:nt], start=True, stop=True)
                        m.then_inc(s_gb, 1)
                    pe.wait_ge(s_gbc, NE)
                    with pe.Fori(0, NE) as e:
                        mlp(POS_MLP[1], e, UP + e * UP, 4 + e * 4, False)
                ln(4 * l + 3)
            pe.wait_ge(s_lnin, KT * 8 + KT)
            for t, (c0, nt) in enumerate(TILES):
                for k in range(KT):
                    m = tr(ps[0:nt, 2 * t + k // 4, (k % 4) * P:(k % 4 + 1) * P], xT[:, k, c0:c0 + nt], ident)
                m.then_inc(s_yT, 1)

        @block.scalar
        def _(act):
            A = nc.scalar.activation
            link = Chain(act, s_ca)

            def ln_stats(n):
                for p in range(4):
                    act.wait_ge(s_xc, 4 * n + p + 1)
                    A(sq[:, 2 * p:2 * p + 2, :], xc[:, 2 * p:2 * p + 2, :], ACT.Square).then_inc(s_sq, 1)
                act.wait_ge(s_var, n + 1)
                link(A(lnv[:], ps[:, 1, 0:NTOK], ACT.Ln, bias=cols[:, 0:1]))
                A(rstd[:, 0, :], lnv[:], ACT.Exp, scale=-0.5).then_inc(s_rstd, 1)

            def ln_mod(n, l, half):
                ln_stats(n)
                for k in range(KT):
                    act.wait_ge(s_xn, 4 * n + k // 2 + 1)
                    A(hT[:, k, 0:SEQ], xc[:, k, 0:SEQ], ACT.Identity, scale=mod[:, l, 24 * half + 8 + k, 0:1],
                      bias=mod[:, l, 24 * half + k, 0:1]).then_inc(s_h, 1)

            def ln_post(n, l, half):
                ln_stats(n)
                for k in range(KT):
                    act.wait_ge(s_xn, 4 * n + k // 2 + 1)
                    c = 32 * half + 8 * l + k
                    A(xT[:, k, :], xc[:, k, :], ACT.Identity, scale=vecT[:, 2, c:c + 1],
                      bias=vecT[:, 2, c + 16:c + 17]).then_inc(s_lnin, 1)

            def rinv(out, psum, scale, bias, last):
                act.wait_ge(*last)
                link(A(lnv[:, 0:psum.shape[-1]], psum, ACT.Ln, scale=scale, bias=cols[:, 1:2]))
                return A(out, lnv[:, 0:psum.shape[-1]], ACT.Exp, scale=-0.5, **({"bias": bias} if bias is not None else {}))

            act.wait_ge(s_vecT, 1)
            act.wait_ge(s_ones, 7)
            cps = ps[:, 0, 3 * P:3 * P + 72]
            A(vecT[:, 0, 0:100], ps[:, 0, 0:100], ACT.Copy).then_inc(s_vec, 1)
            A(vecT[:, 1, 0:96], ps[:, 0, P:P + 96], ACT.Copy).then_inc(s_vec, 1)
            A(vecT[:, 2, 0:64], ps[:, 0, 2 * P:2 * P + 64], ACT.Copy).then_inc(s_vec, 1)
            link(A(siluC[:, :, 0:1], cps[:, 0:8].rearrange("p (k o) -> p k o", o=1), ACT.Silu))
            A(siluC[:, :, 1:9], cps[:, 8:72].rearrange("p (s k) -> p k s", k=8), ACT.Silu).then_inc(s_silc, 1)

            for l in range(DEPTH):
                act.wait_ge(s_mod, 2 * (l + 1))
                act.wait_ge(s_vec, 3)
                act.wait_ge(s_lam, 3 * l + 1)
                A(lamw[:, 2:4], lamw[:, 0:2], ACT.Exp).then_inc(s_lam, 1)
                ln_mod(4 * l, l, 0)
                for c in range(N_WIN):
                    act.wait_ge(s_chunk, POS_WIN[l] + c + 1)
                    b = 2 * (c % 4)
                    if c < 4:
                        A(pA[:, 2 * c:2 * c + 2, :], ps[:, b:b + 2, 0:NTOK], ACT.Copy,
                          scale=DQK ** -0.5 if c < 2 else 1.0).then_inc(s_pev, 1)
                    elif c < 10:
                        f = 2 * (c - 4)
                        A(pB[:, f:f + 2, 3:3 + SEQ], ps[:, b:b + 2, 0:SEQ], ACT.Copy)
                        A(pBs[:, f:f + 2, :, 3:11], ps[:, b:b + 2, SEQ:NTOK].rearrange("p a (s r) -> p a s r", r=8),
                          ACT.Copy).then_inc(s_pev, 1)
                    else:
                        f = 8 + 2 * (c - 10)
                        A(pA[:, f:f + 2, :], ps[:, b:b + 2, 0:NTOK], ACT.Silu).then_inc(s_pev, 1)
                act.wait_ge(s_histT, l + 1)
                act.wait_ge(s_pev, N_WIN * (l + 1))
                A(pBs[:, :, :, 0:3], ps[:, 7, 0:288].rearrange("p (f s r) -> p f s r", f=12, r=3), ACT.Copy).then_inc(s_histc, 1)
                A(tail[:, :, 0:3], pB[:, :, SEQ:SEQ + 3], ACT.Copy)
                A(tail[:, :, 3:27].rearrange("p f (s r) -> p f s r", r=3), pBs[:, :, :, 8:11], ACT.Copy).then_inc(s_tail, 1)
                for f in range(12):
                    act.wait_ge(s_conv, 12 * l + f + 1)
                    A(pB[:, f, 0:NTOK], ctmp[:, f % 2, :], ACT.Silu).then_inc(s_csil, 1)
                act.wait_ge(s_csil, 12 * (l + 1))
                for f in range(9):
                    if f < 8:
                        if f >= 2:
                            act.wait_ge(s_l2s, 8 * l + f - 1)
                        A(ctmp[:, f % 2, :], pB[:, f, 0:NTOK], ACT.Square).then_inc(s_l2q, 1)
                    if f >= 1:
                        g = f - 1
                        act.wait_ge(s_l2s, 8 * l + g + 1)
                        if g >= 2:
                            act.wait_ge(s_l2d, 8 * l + g - 1)
                        rinv(rstd[:, g % 2, :], ps[:, 6 + g % 2, 0:NTOK], 1.0, cols[:, 2:3] if g < 4 else None, (s_l2r, 8 * l + g)).then_inc(s_l2r, 1)
                act.wait_ge(s_btd, l + 1)
                link(A(small[:, 48:60], small[:, 48:60], ACT.Exp, scale=-1.0))
                link(A(small[:, 48:60], small[:, 48:60], ACT.Ln, bias=cols[:, 3:4]))
                link(A(small[:, 60:64], adt[:, 0, l, :], ACT.Exp))
                A(small[:, 36:48].rearrange("p (t e) -> p t e", e=4), small[:, 0:24].rearrange("p (t e) -> p t e", e=8)[:, :, 0:4], ACT.Exp, scale=-1.0).then_inc(s_bta, 1)

                for u in range(8):
                    h, qt = u // 2, u % 2
                    nk = P * (qt + 1)
                    act.wait_ge(s_pM, 8 * l + u + 1)
                    for m_ in range(2):
                        m = A(scb[:, u % 2, 512 * m_:512 * m_ + nk], scb[:, u % 2, 512 * m_:512 * m_ + nk], ACT.Exp,
                              bias=small[:, 100 + 4 * (u % 2) + m_:101 + 4 * (u % 2) + m_],
                              accum_out=small[:, 102 + 4 * (u % 2) + m_:103 + 4 * (u % 2) + m_])
                        if m_ == 0:
                            link(m)
                    m.then_inc(s_pE, 1)
                    act.wait_ge(s_pT, 8 * l + u + 1)
                    if u >= 2:
                        act.wait_ge(s_pV, 8 * l + u - 1)
                    A(ptr[:, u % 2, 0:nk], ps[:, 4, 0:nk], ACT.Copy).then_inc(s_pTc, 1)
                    act.wait_ge(s_pV, 8 * l + u + 1)
                    A(oA[:, h, qt * P:(qt + 1) * P], ps[:, 5 + u % 2, 0:P], ACT.Copy).then_inc(s_pO, 1)

                act.wait_ge(s_qbz, l + 1)

                def seq_q(s, a):
                    if l or not isinstance(s, int):
                        act.wait_ge(s_sS, 8 * l + s - 1)
                    for h in range(H):
                        for m_ in range(2):
                            r = slice(64 * m_, 64 * m_ + 64)
                            m = A(qbd[r, a, h, 16 * h + 8 * m_:16 * h + 8 * m_ + 8], pA[r, h, bass.ds(SEQ + s * DSEQ, DSEQ)], ACT.Copy)
                    m.then_inc(s_qb, 1)

                def seq_k(s):
                    for p in range(0, NPG, 2):
                        act.wait_ge(s_kt, 64 * l + s * NPG + p + 1)
                        if p >= 2 or l or not isinstance(s, int):
                            act.wait_ge(s_kmm, 64 * l + s * NPG + p - 1)
                        elif s:
                            act.wait_ge(s_kmm, s * NPG + p - 1)
                        A(ktb[:, p % 2, :], ps[:, p % 2, :], ACT.Copy).then_inc(s_ktA, 1)

                def seq_exp(s, a):
                    act.wait_ge(s_sM, 8 * l + s + 1)
                    A(scb[0:64, a, :], scb[0:64, a, :], ACT.Exp, bias=small[0:64, 108 + a:109 + a],
                      accum_out=small[0:64, 110 + a:111 + a]).then_inc(s_sE, 1)

                def seq_out(s, a):
                    act.wait_ge(s_sT, 8 * l + s + 1)
                    if a or l or not isinstance(s, int):
                        act.wait_ge(s_sA, 8 * l + s)
                    A(ptb[:, 0:8, :], ps[:, 5, :].rearrange("p (a n) -> p a n", a=8), ACT.Copy)
                    A(ptb[0:64, 8, :], ps[0:64, 6, 0:64], ACT.Copy).then_inc(s_sTc, 1)
                    act.wait_ge(s_sV, 8 * l + s + 1)
                    A(oA[:, :, bass.ds(SEQ + s * DSEQ, DSEQ)], ps[:, 7, 0:32].rearrange("p (h t) -> p h t", h=H),
                      ACT.Copy).then_inc(s_sO, 1)

                def pair(i):
                    seq_q(2 * i, 0)
                    seq_q(2 * i + 1, 1)
                    seq_k(2 * i)
                    seq_exp(2 * i, 0)
                    seq_k(2 * i + 1)
                    seq_out(2 * i, 0)
                    seq_exp(2 * i + 1, 1)
                    seq_out(2 * i + 1, 1)

                pair(0)
                with act.Fori(1, NSEQ // 2) as i:
                    pair(i)

                act.wait_ge(s_sO, 8 * (l + 1))
                act.wait_ge(s_l2d, 8 * (l + 1))
                for h in range(H + 1):
                    if h < H:
                        if h >= 2:
                            act.wait_ge(s_os, H * l + h - 1)
                        A(ctmp[:, h % 2, :], oA[:, h, :], ACT.Square).then_inc(s_oq, 1)
                    if h >= 1:
                        g = h - 1
                        act.wait_ge(s_os, H * l + g + 1)
                        if g >= 2:
                            act.wait_ge(s_mA, H * l + g - 1)
                        rinv(rstd[:, g % 2, :], ps[:, g % 2, 0:NTOK], 1.0 / P, None, (s_or, H * l + g)).then_inc(s_or, 1)

                for T, (c0, nt) in enumerate(TILES):
                    n = 3 * l + T
                    smp = T == 2
                    act.wait_ge(s_gG, n + 1)
                    act.wait_ge(s_gGc, n + 1)
                    act.wait_ge(s_mA, H * (l + 1))
                    link(A(c3(Gb_e, nt), c3(ps[:, 1, :], nt), ACT.Exp))
                    link(A(c3(DT, nt)[0:nt], c3(DT, nt)[0:nt], ACT.Exp))
                    A(small[0:nt, 120:124], small[0:nt, 120:124], ACT.Exp).then_inc(s_gE, 1)
                    act.wait_ge(s_gE, n + 1)
                    act.wait_ge(s_gK, n + 1)
                    for h in range(H):
                        m = A(c3(kd, P)[0:nt, h, :], ps[0:nt, 5, h * P:(h + 1) * P], ACT.Copy, scale=small[0:nt, 120 + h:121 + h])
                    m.then_inc(s_gkd, 1)
                    for v in range(3 if smp else 7):
                        i0 = 17 * l + 7 * T + v
                        act.wait_ge(s_g1, i0 + 1)
                        A(c3(PP, nt)[0:nt], c3(ps[0:nt, 6, :], nt), ACT.Copy).then_inc(s_g1c, 1)
                    act.wait_ge(s_gRt, n + 1)
                    A(rr[0:nt, :], ps[0:nt, 2, :], ACT.Copy).then_inc(s_gr, 1)
                    act.wait_ge(s_gV, n + 1)
                    A(vn[0:nt, :], ps[0:nt, 3, :], ACT.Copy).then_inc(s_gv, 1)
                    act.wait_ge(s_gO, n + 1)
                    link(A(c3(oG, nt), c3(ps[:, 4, :], nt), ACT.Copy))
                    A(sG[:, 0:H * nt].rearrange("p (h t) -> p h t", h=H), c3(oG, nt), ACT.Square).then_inc(s_goq, 1)
                    act.wait_ge(s_gos, n + 1)
                    link(A(sG[:, 0:H * nt], ps[:, 7, 0:H * nt], ACT.Ln, scale=1.0 / P, bias=cols[:, 1:2]))
                    A(sG[:, 0:H * nt], sG[:, 0:H * nt], ACT.Exp, scale=-0.5).then_inc(s_gor, 1)

                ln_post(4 * l + 1, l, 0)
                ln_mod(4 * l + 2, l, 1)

                def silu(pos, e, n0, first):
                    for j in range(UP):
                        act.wait_ge(s_chunk, pos + 2 * j + 1 + e * MLP_POS)
                        if j >= 2 or not first:
                            act.wait_ge(s_ff, n0 + j - 1)
                        A(sil[:, j % 2], ps[:, 4 * (j % 2):4 * (j % 2) + 2, 0:NTOK], ACT.Silu).then_inc(s_sil, 1)

                act.wait_ge(s_out, 16 * (8 * l + 6))
                if l == 0:
                    silu(POS_MLP[0], 0, 0, True)
                else:
                    act.wait_ge(s_out, 16 * 8 * DEPTH)
                    act.wait_ge(s_rtm, 1)
                    A(small[:, 72:96], small[:, 72:96], ACT.Exp).then_inc(s_rte, 1)
                    for e in range(NE):
                        act.wait_ge(s_gb, e + 1)
                        A(gateB[:, e, :], ps[:, 4 + e % 4, 0:NTOK], ACT.Copy).then_inc(s_gbc, 1)
                    with act.Fori(0, NE) as e:
                        silu(POS_MLP[1], e, UP + e * UP, False)
                ln_post(4 * l + 3, l, 1)
            for t, (c0, nt) in enumerate(TILES):
                act.wait_ge(s_yT, t + 1)
                A(yrow[0:nt, t, :].rearrange("p (a n) -> p a n", a=2), ps[0:nt, 2 * t:2 * t + 2, :], ACT.Copy).then_inc(s_y, 1)

        @block.vector
        def _(dve):
            V = nc.vector
            link = Chain(dve, s_cd)

            def ln(n):
                dve.wait_ge(s_mean, n + 1)
                for p in range(4):
                    V.tensor_tensor(xc[:, 2 * p:2 * p + 2, :], xT[:, 2 * p:2 * p + 2, :],
                                    ps[:, 0:1, 0:NTOK].to_broadcast([P, 2, NTOK]), ALU.subtract).then_inc(s_xc, 1)
                dve.wait_ge(s_rstd, n + 1)
                for p in range(4):
                    V.tensor_tensor(xc[:, 2 * p:2 * p + 2, :], xc[:, 2 * p:2 * p + 2, :],
                                    rstd[:, 0:1, :].to_broadcast([P, 2, NTOK]), ALU.mult).then_inc(s_xn, 1)

            def seqs(t):
                return t.rearrange("p k (s r) -> p k s r", r=DSEQ)

            def per_seq(l, f0, nf):
                m = mod[:, l, f0:f0 + nf, 1:9].rearrange("p k (s o) -> p k s o", o=1)
                return m.to_broadcast([P, nf, NSEQ, DSEQ])

            def ln_mod(n, l, half):
                ln(n)
                dve.wait_ge(s_xn, 4 * (n + 1))
                link(V.tensor_tensor(seqs(hT[:, :, SEQ:]), seqs(xc[:, :, SEQ:]), per_seq(l, 24 * half + 8, 8), ALU.mult))
                V.tensor_tensor(seqs(hT[:, :, SEQ:]), seqs(hT[:, :, SEQ:]), per_seq(l, 24 * half, 8), ALU.add).then_inc(s_hs, 1)
                V.tensor_scalar(xT[:], xT[:], ALPHA, None, ALU.mult).then_inc(s_xa, 1)

            def residual(src, k0, l, half):
                g0 = 24 * half + 16 + k0
                for o in range(2):
                    V.scalar_tensor_tensor(out=xT[:, k0 + o, 0:SEQ], in0=src[:, o, 0:SEQ], scalar=mod[:, l, g0 + o, 0:1],
                                           in1=xT[:, k0 + o, 0:SEQ], op0=ALU.mult, op1=ALU.add)
                t = seqs(ctmp[:, :, 0:NS])
                dve.wait_ge(s_lnin, KT * (4 * l + 2 * half + 1) + k0)
                link(V.tensor_tensor(t, seqs(src[:, :, SEQ:NTOK]), per_seq(l, g0, 2), ALU.mult))
                V.tensor_tensor(xT[:, k0:k0 + 2, SEQ:], xT[:, k0:k0 + 2, SEQ:], ctmp[:, :, 0:NS], ALU.add).then_inc(s_lnin, 2)

            for k in range(KT):
                dve.wait_ge(s_xt, k + 1)
                V.tensor_copy(xT[:, k, :], ps[:, 1 + k % 4, 0:NTOK]).then_inc(s_lnin, 1)
            dve.wait_ge(s_vec, 3)
            for l in range(DEPTH):
                with dve.Fori(0, ADA_CH // RING) as i:
                    for c in range(RING):
                        dve.wait_ge(s_chunk, ADA_CH * l + c + 1 + i * RING)
                        b = vecT[:, 0, bass.ds(48 * l + 2 * c + i * (2 * RING), 2)].rearrange("p (a o) -> p a o", o=1)
                        V.tensor_tensor(mod[:, l, bass.ds(2 * c + i * (2 * RING), 2), :],
                                        ps[:, 6 + c % 2, 0:32].rearrange("p (a n) -> p a n", a=2)[:, :, 0:9],
                                        b.to_broadcast([P, 2, 9]), ALU.add).then_inc(s_modev, 1)
                dve.wait_ge(s_modev, ADA_CH * (l + 1))
                for half in range(2):
                    f = 24 * half + 8
                    V.tensor_scalar(mod[:, l, f:f + 8, :], mod[:, l, f:f + 8, :], 1.0, None, ALU.add).then_inc(s_mod, 1)

            for l in range(DEPTH):
                for a in range(2):
                    link(V.tensor_tensor(ctmp[:, 0, 0:64], lamb[:, l, 128 * a:128 * a + 64], lamb[:, l, 128 * a + 64:128 * a + 128], ALU.mult))
                    m = V.tensor_reduce(lamw[:, a:a + 1], ctmp[:, 0, 0:64], AX.X, ALU.add)
                    if a == 0:
                        link(m)
                m.then_inc(s_lam, 1)
                dve.wait_ge(s_lam, 3 * l + 2)
                link(V.tensor_tensor(lamw[:, 4:5], lamw[:, 3:4], lamw[:, 2:3], ALU.subtract))
                link(V.tensor_scalar(lamc[:, l, 0:1], lamw[:, 4:5], -LAM_INIT[l], None, ALU.add))
                link(V.scalar_tensor_tensor(out=lamc[0:64, l, 1:2], in0=C[0:64, C_ROW + 2:C_ROW + 3], scalar=lamc[0:64, l, 0:1],
                                            in1=C[0:64, C_ROW + 1:C_ROW + 2], op0=ALU.mult, op1=ALU.add))
                V.tensor_scalar(lamw[:, 5:6], vecT[:, 0, 96 + l:97 + l], 1.0 - LAM_INIT[l], None, ALU.mult).then_inc(s_lam, 1)
                dve.wait_ge(s_lam, 3 * l + 3)
                dve.wait_ge(s_mod, 2 * (l + 1))
                ln_mod(4 * l, l, 0)

                dve.wait_ge(s_ba, l + 1)
                link(V.tensor_copy(small[:, 0:16], ps[:, 6, 0:16]))
                V.tensor_copy(small[0:NS, 16:24], ps[0:NS, 6, 16:24]).then_inc(s_bae, 1)
                dve.wait_ge(s_bae, l + 1)
                ba = small[:, 0:24].rearrange("p (t e) -> p t e", e=8)
                u = small[:, 24:36].rearrange("p (t e) -> p t e", e=4)
                t3 = lambda a: small[:, a:a + 12].rearrange("p (t e) -> p t e", e=4)
                bc3 = lambda t: t.rearrange("p (o e) -> p o e", o=1).to_broadcast([P, 3, H])
                link(V.tensor_tensor(u, ba[:, :, 4:8], bc3(adt[:, 1, l, :]), ALU.add))
                V.scalar_tensor_tensor(out=small[:, 48:60], in0=small[:, 24:36], scalar=-1.0, in1=small[:, 24:36],
                                       op0=ALU.mult, op1=ALU.max).then_inc(s_btd, 1)
                for c in range(2):
                    dve.wait_ge(s_chunk, POS_VO[l] + c + 1)
                    for t, (c0, nt) in enumerate(TILES):
                        m = V.tensor_copy(va[0:nt, t, CH * c:CH * (c + 1)], ps[0:nt, 3 * c + t, 0:CH])
                        if t < 2:
                            link(m)
                    m.then_inc(s_va, 1)
                dve.wait_ge(s_kT, l + 1)
                if l:
                    dve.wait_ge(s_ff, UP * l)
                link(V.tensor_copy(kst[:, 0:2, :], ps[:, 0:2, :]))
                V.tensor_copy(kst[0:NS, 2, :], ps[0:NS, 2, :]).then_inc(s_kst, 1)
                dve.wait_ge(s_tailT, l + 1)
                dve.wait_ge(s_histT, l + 1)
                V.tensor_copy(rowb[0:27, :].rearrange("p (a n) -> p a n", a=3), ps[0:27, 3:6, :]).then_inc(s_tailc, 1)
                dve.wait_ge(s_histc, l + 1)
                dve.wait_ge(s_tail, l + 1)
                link(V.memset(pB[:, :, 0:3], 0.0))
                for f in range(12):
                    if f >= 2:
                        dve.wait_ge(s_csil, 12 * l + f - 1)
                    smp = pB[:, f, 3 + SEQ:3 + SEQ + 88].rearrange("p (s r) -> p s r", r=11)
                    out_s = ctmp[:, f % 2, SEQ:].rearrange("p (s r) -> p s r", r=DSEQ)
                    out_p = ctmp[:, f % 2, 0:SEQ]
                    wc = lambda i: vecT[:, 1, 48 * l + 12 * i + f:48 * l + 12 * i + f + 1]
                    V.tensor_scalar(out_p, pB[:, f, 0:SEQ], wc(0), None, ALU.mult)
                    link(V.tensor_scalar(out_s, smp[:, :, 0:DSEQ], wc(0), None, ALU.mult))
                    for i in range(1, CW):
                        m = V.scalar_tensor_tensor(out=out_p, in0=pB[:, f, i:i + SEQ], scalar=wc(i), in1=out_p, op0=ALU.mult, op1=ALU.add)
                        m = V.scalar_tensor_tensor(out=out_s, in0=smp[:, :, i:i + DSEQ], scalar=wc(i), in1=out_s, op0=ALU.mult, op1=ALU.add)
                        if i < CW - 1:
                            link(m)
                    m.then_inc(s_conv, 1)
                for f in range(8):
                    dve.wait_ge(s_l2r, 8 * l + f + 1)
                    V.tensor_tensor(pB[:, f, 0:NTOK], pB[:, f, 0:NTOK], rstd[:, f % 2, :], ALU.mult).then_inc(s_l2d, 1)
                dve.wait_ge(s_bta, l + 1)
                link(V.tensor_scalar(small[:, 36:48], small[:, 36:48], 1.0, None, ALU.add))
                link(V.reciprocal(small[:, 36:48], small[:, 36:48]))
                link(V.scalar_tensor_tensor(out=small[:, 24:36], in0=small[:, 24:36], scalar=0.0, in1=small[:, 48:60],
                                            op0=ALU.max, op1=ALU.add))
                link(V.tensor_tensor(u, u, bc3(small[:, 60:64]), ALU.mult))
                V.tensor_scalar(small[:, 24:36], small[:, 24:36], -1.0, None, ALU.mult).then_inc(s_bt, 1)

                def p_max(uu):
                    h, qt = uu // 2, uu % 2
                    nk = P * (qt + 1)
                    dve.wait_ge(s_pS, 8 * l + uu + 1)
                    if uu >= 2:
                        dve.wait_ge(s_pT, 8 * l + uu - 1)
                    for m_ in range(2):
                        m = V.scalar_tensor_tensor(out=scb[:, uu % 2, 512 * m_:512 * m_ + nk], in0=dP[:, qt, 0:nk], scalar=SLOPE[h],
                                                   in1=ps[:, 2 * (uu % 2) + m_, 0:nk], op0=ALU.mult, op1=ALU.add)
                    link(m)
                    V.tensor_reduce(small[:, 100 + 4 * (uu % 2):102 + 4 * (uu % 2)],
                                    scb[:, uu % 2, 0:1024].rearrange("p (a n) -> p a n", a=2)[:, :, 0:nk],
                                    AX.X, ALU.max, negate=True).then_inc(s_pM, 1)

                def p_probs(uu):
                    nk = P * (uu % 2 + 1)
                    b = 102 + 4 * (uu % 2)
                    dve.wait_ge(s_pE, 8 * l + uu + 1)
                    link(V.reciprocal(small[:, b:b + 2], small[:, b:b + 2]))
                    link(V.tensor_scalar(small[:, b + 1:b + 2], small[:, b + 1:b + 2], lamc[:, l, 0:1], None, ALU.mult))
                    p1, p2 = scb[:, uu % 2, 0:nk], scb[:, uu % 2, 512:512 + nk]
                    link(V.tensor_scalar(p1, p1, small[:, b:b + 1], None, ALU.mult))
                    V.scalar_tensor_tensor(out=p1, in0=p2, scalar=small[:, b + 1:b + 2], in1=p1, op0=ALU.mult, op1=ALU.add).then_inc(s_pA, 1)

                p_max(0)
                for uu in range(8):
                    if uu + 1 < 8:
                        p_max(uu + 1)
                    p_probs(uu)

                def seq_k(s):
                    for p in range(1, NPG, 2):
                        dve.wait_ge(s_kt, 64 * l + s * NPG + p + 1)
                        if p >= 3 or l or not isinstance(s, int) or s:
                            dve.wait_ge(s_kmm, 64 * l + s * NPG + p - 1)
                        V.tensor_copy(ktb[:, p % 2, :], ps[:, p % 2, :]).then_inc(s_ktD, 1)

                def seq_max(s, a):
                    dve.wait_ge(s_sS, 8 * l + s + 1)
                    if l or not isinstance(s, int):
                        dve.wait_ge(s_sT, 8 * l + s - 1)
                    V.scalar_tensor_tensor(out=scb[0:64, a, 0:PAST], in0=dS[:], scalar=C[0:64, C_ROW:C_ROW + 1],
                                           in1=ps[0:64, 2:4, :].rearrange("p a n -> p (a n)"), op0=ALU.mult, op1=ALU.add)
                    link(V.scalar_tensor_tensor(out=scb[0:64, a, PAST:PAST + NS], in0=dN[:, bass.ds(s, 1), :].rearrange("p o n -> p (o n)"),
                                                scalar=C[0:64, C_ROW:C_ROW + 1], in1=ps[0:64, 4, 0:NS], op0=ALU.mult, op1=ALU.add))
                    V.tensor_reduce(small[0:64, 108 + a:109 + a], scb[0:64, a, :], AX.X, ALU.max, negate=True).then_inc(s_sM, 1)

                def seq_probs(s, a):
                    dve.wait_ge(s_sE, 8 * l + s + 1)
                    link(V.reciprocal(small[0:64, 110 + a:111 + a], small[0:64, 110 + a:111 + a]))
                    V.tensor_scalar(scb[0:64, a, :], scb[0:64, a, :], small[0:64, 110 + a:111 + a], lamc[0:64, l, 1:2],
                                    ALU.mult, ALU.mult).then_inc(s_sP, 1)

                def seq_diff(s):
                    dve.wait_ge(s_sTc, 8 * l + s + 1)
                    if not (isinstance(s, int) and s == 0) or l:
                        dve.wait_ge(s_sV, 8 * l + s)
                    v = ptb[:, 0:8, :].rearrange("p a (h m t) -> p (a h) m t", m=2, t=8)
                    link(V.tensor_tensor(atb[:, 0:8, :].rearrange("p a (h t) -> p (a h) t", t=8), v[:, :, 0, :], v[:, :, 1, :], ALU.add))
                    w = ptb[0:64, 8, :].rearrange("p (h m t) -> p h m t", m=2, t=8)
                    V.tensor_tensor(atb[0:64, 8, :].rearrange("p (h t) -> p h t", t=8), w[:, :, 0, :], w[:, :, 1, :], ALU.add).then_inc(s_sA, 1)

                DVE_PAIR = 6

                def pair(i):
                    seq_k(2 * i)
                    seq_max(2 * i, 0)
                    seq_probs(2 * i, 0)
                    seq_k(2 * i + 1)
                    seq_max(2 * i + 1, 1)
                    seq_diff(2 * i)
                    seq_probs(2 * i + 1, 1)
                    seq_diff(2 * i + 1)

                pair(0)
                with dve.Fori(1, NSEQ // 2) as i:
                    link.loop(i - 1, DVE_PAIR)
                    pair(i)
                link.done(DVE_PAIR, NSEQ // 2 - 1)

                dve.wait_ge(s_out, 16 * (8 * l + 6))
                for h in range(H):
                    dve.wait_ge(s_or, H * l + h + 1)
                    V.scalar_tensor_tensor(out=mixT[:, h, :], in0=oA[:, h, :], scalar=lamw[:, 5:6], in1=rstd[:, h % 2, :],
                                           op0=ALU.mult, op1=ALU.mult).then_inc(s_mA, 1)

                dve.wait_ge(s_mA, H * (l + 1))
                if l > 0:
                    dve.wait_ge(s_out, 16 * 8 * l)
                V.memset(Sp[:], 0.0)
                for T, (c0, nt) in enumerate(TILES):
                    n = 3 * l + T
                    smp = T == 2
                    lev = 3 if smp else 7
                    mask = (C[0:nt, C_TRIS:C_TRIS + nt] if smp else tri).rearrange("p (o t) -> p o t", o=1).to_broadcast([nt, H, nt])
                    dve.wait_ge(s_gG, n + 1)
                    link(V.tensor_copy(small[0:nt, 112:120], ps[0:nt, 0, 0:8]))
                    V.tensor_copy(c3(bbs, nt), c3(ps[:, 2, :], nt))
                    for h in range(H):
                        V.tensor_scalar(c3(DT, nt)[0:nt, h, :], ps[0:nt, 1, h * P:h * P + nt], small[0:nt, 112 + h:113 + h], 0.0,
                                        ALU.subtract, ALU.min)
                    V.tensor_tensor(small[0:nt, 120:124], small[0:nt, 116:120], small[0:nt, 112:116], ALU.subtract).then_inc(s_gGc, 1)
                    dve.wait_ge(s_gE, n + 1)
                    V.tensor_tensor(c3(qd, nt), pB[:, 0:4, c0:c0 + nt], c3(Gb_e, nt), ALU.mult)
                    link(V.tensor_tensor(c3(DT, nt)[0:nt], c3(DT, nt)[0:nt], mask, ALU.mult))
                    dve.wait_ge(s_gK, n + 1)
                    V.tensor_tensor(c3(QK, nt)[0:nt], c3(ps[0:nt, 4, :], nt), c3(DT, nt)[0:nt], ALU.mult)
                    link(V.tensor_tensor(c3(LT, nt)[0:nt], c3(ps[0:nt, 3, :], nt), c3(DT, nt)[0:nt], ALU.mult))
                    idb = ident[0:nt, 0:nt].rearrange("p (o t) -> p o t", o=1).to_broadcast([nt, H, nt])
                    V.tensor_copy(c3(X, nt)[0:nt], idb)
                    V.tensor_copy(c3(XT, nt)[0:nt], idb)
                    link(V.tensor_tensor(c3(LT, nt)[0:nt], c3(LT, nt)[0:nt], c3(bbs, nt)[0:nt], ALU.mult))
                    for v in range(lev):
                        i0 = 17 * l + 7 * T + v
                        lm = C[0:nt, C_LEV + v * P:C_LEV + v * P + nt].rearrange("p (o t) -> p o t", o=1).to_broadcast([nt, H, nt])
                        V.tensor_tensor(c3(LM, nt)[0:nt], c3(LT, nt)[0:nt], lm, ALU.mult).then_inc(s_lm, 1)
                        dve.wait_ge(s_g2, i0 + 1)
                        V.tensor_tensor(c3(X, nt)[0:nt], c3(X, nt)[0:nt], c3(ps[0:nt, 7, :], nt), ALU.subtract)
                        V.tensor_tensor(c3(XT, nt)[0:nt], c3(XT, nt)[0:nt], c3(ps[0:nt, 0, :], nt), ALU.subtract).then_inc(s_g2c, 1)
                    dve.wait_ge(s_gR, n + 1)
                    link(V.tensor_tensor(c3(rT, nt), c3(ps[:, 1, :], nt), c3(Gb_e, nt), ALU.mult))
                    link(V.tensor_tensor(c3(rT, nt), pB[:, 8:12, c0:c0 + nt], c3(rT, nt), ALU.subtract))
                    V.tensor_tensor(c3(rT, nt), c3(rT, nt), c3(bbs, nt), ALU.mult).then_inc(s_gRc, 1)
                    if smp:
                        dve.wait_ge(s_gO, n + 1)
                        dve.wait_ge(s_gkd, n + 1)
                        for h in range(H):
                            if h > 0:
                                dve.wait_ge(s_gS, 6 * l + 2 + h)
                            for half in range(2):
                                m = V.tensor_tensor(kdm[half][0:nt, :].rearrange("p (s k) -> p s k", s=4),
                                                    c3(kd, P)[0:nt, h:h + 1, :].to_broadcast([nt, 4, P]),
                                                    C[0:nt, C_SEQM + 4 * half:C_SEQM + 4 * half + 4].rearrange("p (s o) -> p s o", o=1).to_broadcast([nt, 4, P]),
                                                    ALU.mult)
                            m.then_inc(s_gkm, 1)
                            dve.wait_ge(s_gS, 6 * l + 3 + h)
                            for s in range(NSEQ):
                                V.scalar_tensor_tensor(out=Ss[:, s, h, :], in0=Ss[:, s, h, :], scalar=c3(Gb_e, nt)[:, h, 8 * s + 7:8 * s + 8],
                                                       in1=ps[:, 5 + s // 4, (s % 4) * P:(s % 4 + 1) * P], op0=ALU.mult, op1=ALU.add
                                                       ).then_inc(s_gSc, 1)
                    else:
                        dve.wait_ge(s_gS, 6 * l + T + 1)
                        for h in range(H):
                            m = V.scalar_tensor_tensor(out=Sp[:, h, :], in0=Sp[:, h, :], scalar=c3(Gb_e, nt)[:, h, nt - 1:nt],
                                                       in1=ps[:, 5, h * P:(h + 1) * P], op0=ALU.mult, op1=ALU.add)
                        m.then_inc(s_gSc, 1)
                    dve.wait_ge(s_gor, n + 1)
                    g3 = sG[:, 0:H * nt].rearrange("p (h t) -> p h t", h=H)
                    link(V.tensor_tensor(c3(oG, nt), c3(oG, nt), g3, ALU.mult))
                    V.scalar_tensor_tensor(out=mixT[:, 4:8, c0:c0 + nt], in0=c3(oG, nt), scalar=vecT[:, 0, 98 + l:99 + l],
                                           in1=pA[:, 8:12, c0:c0 + nt], op0=ALU.mult, op1=ALU.mult).then_inc(s_mB, 1)

                for c in range(4):
                    dve.wait_ge(s_chunk, POS_VO[l] + 2 + c + 1)
                    if c == 0:
                        dve.wait_ge(s_xa, 2 * l + 1)
                    residual(ps[:, 2 * c:2 * c + 2, :], 2 * c, l, 0)
                ln(4 * l + 1)
                ln_mod(4 * l + 2, l, 1)
                dve.wait_ge(s_xa, 2 * l + 2)

                def swiglu(pos, e, n0):
                    for j in range(UP):
                        dve.wait_ge(s_sil, n0 + j + 1)
                        dve.wait_ge(s_chunk, pos + 2 * j + 2 + e * MLP_POS)
                        b = 4 * (j % 2) + 2
                        V.tensor_tensor(ff[:, 2 * j:2 * j + 2, :], sil[:, j % 2], ps[:, b:b + 2, 0:NTOK], ALU.mult).then_inc(s_ff, 1)

                if l == 0:
                    swiglu(POS_MLP[0], 0, 0)
                    for d in range(4):
                        dve.wait_ge(s_chunk, POS_MLP[0] + 2 * UP + 3 * d + 3)
                        residual(ps[:, 2 * d:2 * d + 2, :], 2 * d, l, 1)
                else:
                    dve.wait_ge(s_rt, 1)
                    lg = small[:, 72:96].rearrange("p (t e) -> p t e", e=8)
                    link(V.memset(small[:, 64:96], 0.0))
                    V.tensor_tensor(lg[:, 0:2, :], ps[:, 2, 0:16].rearrange("p (t e) -> p t e", e=8),
                                    brb[:].rearrange("p (o e) -> p o e", o=1).to_broadcast([P, 2, 8]), ALU.add)
                    link(V.tensor_tensor(small[0:NS, 88:96], ps[0:NS, 2, 16:24], brb[0:NS, :], ALU.add))
                    sel = small[:, 0:24].rearrange("p (t e) -> p t e", e=8)
                    pw = ctmp[:, 0, 0:64].rearrange("p (i j) -> p i j", i=8)
                    pw2 = ctmp[:, 1, 0:64].rearrange("p (i j) -> p i j", i=8)
                    low = C[:, C_LOW:C_LOW + 64].rearrange("p (i j) -> p i j", i=8)
                    for t in range(3):
                        lj = lg[:, t:t + 1, :].to_broadcast([P, 8, 8])
                        li = small[:, 72 + 8 * t:80 + 8 * t].rearrange("p (i o) -> p i o", o=1).to_broadcast([P, 8, 8])
                        V.tensor_tensor(pw, lj, li, ALU.is_equal)
                        link(V.tensor_tensor(pw2, lj, li, ALU.is_gt))
                        link(V.tensor_tensor(pw, pw, low, ALU.mult))
                        link(V.tensor_tensor(pw, pw, pw2, ALU.add))
                        link(V.tensor_reduce(sel[:, t, :], pw, AX.X, ALU.add))
                    link(V.tensor_scalar(small[:, 0:24], small[:, 0:24], 2.0, None, ALU.is_lt))
                    link(V.tensor_reduce(small[:, 64:67], lg, AX.X, ALU.max))
                    mx = small[:, 64:67].rearrange("p (t o) -> p t o", o=1).to_broadcast([P, 3, 8])
                    V.tensor_tensor(lg, lg, mx, ALU.subtract).then_inc(s_rtm, 1)
                    dve.wait_ge(s_rte, 1)
                    link(V.tensor_tensor(lg, lg, sel, ALU.mult))
                    link(V.tensor_reduce(small[:, 64:67], lg, AX.X, ALU.add))
                    link(V.reciprocal(small[:, 64:67], small[:, 64:67]))
                    V.tensor_tensor(lg, lg, mx, ALU.mult).then_inc(s_gate, 1)
                    V.memset(mixT[:], 0.0).then_inc(s_dn, 4)
                    dve.wait_ge(s_dn, 4)
                    dve.wait_ge(s_gbc, NE)
                    DN_LOOP = 4
                    with dve.Fori(0, NE) as e:
                        link.loop(e, DN_LOOP)
                        swiglu(POS_MLP[1], e, UP + e * UP)
                        for d in range(4):
                            dve.wait_ge(s_chunk, POS_MLP[1] + 2 * UP + 3 * d + 3 + e * MLP_POS)
                            dve.wait_ge(s_dn, 4 + d + 4 * e)
                            link(V.tensor_tensor(dtmp, ps[:, 2 * d:2 * d + 2, 0:NTOK], gateB[:, bass.ds(e, 1), :].to_broadcast([P, 2, NTOK]), ALU.mult))
                            V.tensor_tensor(mixT[:, 2 * d:2 * d + 2, :], mixT[:, 2 * d:2 * d + 2, :], dtmp, ALU.add).then_inc(s_dn, 1)
                    link.done(DN_LOOP, NE)
                    dve.wait_ge(s_dn, 4 * (NE + 1))
                    for d in range(4):
                        residual(mixT[:, 2 * d:2 * d + 2, :], 2 * d, l, 1)
                ln(4 * l + 3)


_INS = ['x_prompt', 'x_sample', 'cache_k', 'cache_v', 'state_conv', 'state_delta', 'page_table', 'c_prompt', 'c_sample',
        'w_in', 'w_out', 'lam_params', 'subln_a', 'conv_w', 'a_log', 'dt_bias', 'norm_b', 'ada_w', 'ada_b',
        'ln1_g', 'ln1_b', 'ln2_g', 'ln2_b', 'dense_w_up', 'dense_w_down', 'moe_router', 'moe_router_b', 'moe_w_up', 'moe_w_down']
_OUTS = [(1, SEQ, D), (NSEQ, DSEQ, D), (DEPTH, 1, SEQ, H, P), (DEPTH, 1, SEQ, H, P), (DEPTH, 1, 3, 1536), (DEPTH, 1, H, P, P),
         (DEPTH, NSEQ, DSEQ, H, P), (DEPTH, NSEQ, DSEQ, H, P), (DEPTH, NSEQ, 3, 1536), (DEPTH, NSEQ, H, P, P)]


def kernel(**inputs):
    import concourse.bacc as _bacc
    from concourse.bass_utils import run_bass_kernel_spmd as _run

    nc = _bacc.Bacc("TRN2", target_bir_lowering=False, num_devices=1)
    arrays, args = {}, []
    host = [(n, np.ascontiguousarray(inputs[n])) for n in _INS]
    host += list(zip(("table_c", "table_dp", "table_ds", "table_dn"), constant_tables()))
    for name, a in host:
        arrays[f"in_{name}_dram"] = a
        args.append(nc.dram_tensor(f"in_{name}_dram", a.shape, mybir.dt.from_np(a.dtype), kind="ExternalInput").ap())
    for i, shape in enumerate(_OUTS):
        args.append(nc.dram_tensor(f"out_{i}_dram", shape, F32, kind="ExternalOutput").ap())
    trunk_kernel(nc, *args)
    r = _run(nc, [arrays], core_ids=[0])
    return tuple(r.results[0][f"out_{i}_dram"] for i in range(len(_OUTS)))
```

```python
from contextlib import ExitStack
import math

import numpy as np

import concourse.bass as bass
from concourse import mybir

ALU = mybir.AluOpType
ACT = mybir.ActivationFunctionType
AX = mybir.AxisListType
F32 = mybir.dt.float32
I32 = mybir.dt.int32

P = 128
D = 1024
KT = D // P
SEQ = 256
NSEQ = 8
DSEQ = 8
NS = NSEQ * DSEQ
NTOK = SEQ + NS
DEPTH = 2
H = 4
DQK = 64
PAST = 1024
PAGE = 128
NPG = PAST // PAGE
NPOOL = 80
FF = 2816
FT = FF // P
NE = 8
CW = 4
D_IN = 3592
PB = 3 + SEQ + NSEQ * (3 + DSEQ) + 1
ALPHA = (2 * DEPTH) ** 0.25
LN_EPS = 1e-5
NEG = -1e30
LAM_INIT = [0.8 - 0.6 * math.exp(-0.3 * l) for l in range(DEPTH)]
SLOPE = [2.0 ** (-8.0 * (h + 1) / H) for h in range(H)]
LEVELS = [1, 2, 4, 8, 16, 32, 64]
TILES = [(0, 128), (128, 128), (256, 64)]

RING = 6
CH = 256
ADA_CH = 6 * D // CH
WIN_COLS = [0, 256, 512, 768] + [1536 + 256 * j for j in range(6)] + [3080, 3336]
N_WIN = len(WIN_COLS)
N_VO = 6
UP = FF // CH
DN_ROWS = [(0, 8), (8, 8), (16, 6)]
MLP_CH = 2 * UP + 4 * len(DN_ROWS)
MLP_POS = 36
POS_WIN = [2 * ADA_CH, 2 * ADA_CH + N_WIN + N_VO + MLP_POS]
POS_VO = [p + N_WIN for p in POS_WIN]
POS_MLP = [p + N_VO for p in POS_VO]

C_ID, C_TRI, C_TRIS, C_SAME, C_LEV = 0, 128, 256, 320, 384
C_SEQM = C_LEV + 7 * 128
C_LOW = C_SEQM + 8
C_ROW = C_LOW + 64
C_IOTA = C_ROW + 3
C_GRP = C_IOTA + NTOK
C_PAIR = C_GRP + 9
NC = C_PAIR + 2 * NSEQ // 2 * DSEQ
NPAIR = NSEQ // 2

CLASSES = [(128, [(0, 128)]), (224, [(0, 128), (128, 96)]), (NTOK, TILES)]


def constant_tables():
    c = np.zeros((P, NC), np.float32)
    j, i = np.arange(P)[:, None], np.arange(P)[None, :]
    c[:, C_ID:C_ID + P] = j == i
    c[:, C_TRI:C_TRI + P] = j <= i
    js, is_ = j[:NS], i[:, :NS]
    c[:NS, C_TRIS:C_TRIS + NS] = (js <= is_) & (js // DSEQ == is_ // DSEQ)
    c[:NS, C_SAME:C_SAME + NS] = js // DSEQ == is_ // DSEQ
    for n, s in enumerate(LEVELS):
        c[:, C_LEV + n * P:C_LEV + (n + 1) * P] = (i // (2 * s) == j // (2 * s)) & (i % (2 * s) >= s) & (j % (2 * s) < s)
    c[:NS, C_SEQM:C_SEQM + 8] = np.arange(NS)[:, None] // DSEQ == np.arange(8)[None, :]
    e, f = np.arange(8)[:, None], np.arange(8)[None, :]
    c[:, C_LOW:C_LOW + 64] = (f < e).astype(np.float32).reshape(1, 64)
    row = np.arange(P)
    rh, ra, rm, rt = row // 32, (row // 16) % 2, (row // 8) % 2, row % 8
    c[:, C_ROW] = [SLOPE[h] for h in rh]
    c[:, C_ROW + 1] = rm == 0
    c[:, C_ROW + 2] = rm == 1
    c[:, C_GRP:C_GRP + 9] = (row % 32)[:, None] == np.arange(9)[None, :]
    for a in range(2):
        c[:, C_PAIR + 32 * a:C_PAIR + 32 * (a + 1)] = (ra == a)[:, None] & ((8 * rh + rt)[:, None] == np.arange(32)[None, :])
    c[:, C_IOTA:C_IOTA + NTOK] = np.arange(1, NTOK + 1)[None, :]
    dp = np.full((P, 2, SEQ), NEG, np.float32)
    for qt in range(2):
        q, k = qt * P + np.arange(P)[:, None], np.arange(SEQ)[None, :]
        dp[:, qt] = np.where(q >= k, k - q, NEG)
    ds = (np.arange(PAST)[None, :] - (PAST + rt[:, None])).astype(np.float32)
    dn = np.full((P, NPAIR, NS), NEG, np.float32)
    for i in range(NPAIR):
        for u in range(NS):
            seen = (2 * i + ra == u // DSEQ) & (u % DSEQ <= rt)
            dn[:, i, u] = np.where(seen, u % DSEQ - rt, NEG)
    return c, dp.reshape(P, 2 * SEQ), ds, dn.reshape(P, NPAIR * NS)


REGION = 12512


class Chain:

    def __init__(self, eng, sem):
        self.eng, self.sem, self.n, self.extra, self.start = eng, sem, 0, 0, 0

    def __call__(self, ins):
        self.n += 1
        ins.then_inc(self.sem, 1)
        self.eng.wait_ge(self.sem, self.extra + self.n)

    def loop(self, reg, per):
        self.extra, self.start = reg * per, self.n

    def done(self, per, times):
        assert self.n - self.start == per, (self.n - self.start, per)
        self.extra, self.n = 0, self.start + per * times


def trunk_kernel(nc, x_p, x_s, cache_k, cache_v, st_conv, st_delta, ptab, c_p, c_s, w_in, w_out, lam_p,
                 subln, conv_w, a_log, dt_bias, norm_b, ada_w, ada_b, ln1_g, ln1_b, ln2_g, ln2_b,
                 dw_up, dw_dn, m_r, m_rb, mw_up, mw_dn, t_c, t_dp, t_ds, t_dn,
                 y_p, y_s, k_p, v_p, cv_p, dl_p, k_s, v_s, cv_s, dl_s):
    with ExitStack() as ctx:
        def sb(name, shape, dt=F32):
            return ctx.enter_context(nc.sbuf_tensor(name, shape, dt))

        def sem(name):
            return ctx.enter_context(nc.semaphore(name))

        ps = ctx.enter_context(nc.psum_tensor("ps", [P, 8, 512], F32))

        xT = sb("xT", [P, KT, NTOK])
        hT = sb("hT", [P, KT, NTOK])
        mixT = sb("mixT", [P, KT, NTOK])
        big = sb("big", [P, 12 * NTOK + 12 * PB])
        pA = big[:, 0:12 * NTOK].rearrange("p (f t) -> p f t", t=NTOK)
        pB = big[:, 12 * NTOK:].rearrange("p (f t) -> p f t", t=PB)
        pBs = pB[:, :, 3 + SEQ:3 + SEQ + 88].rearrange("p f (s r) -> p f s r", r=3 + DSEQ)
        xc = big[:, 0:KT * NTOK].rearrange("p (f t) -> p f t", t=NTOK)
        sq = big[:, KT * NTOK:2 * KT * NTOK].rearrange("p (f t) -> p f t", t=NTOK)
        ff = big[:, 0:FT * NTOK].rearrange("p (f t) -> p f t", t=NTOK)
        xrow = big[:, 0:3 * D].rearrange("p (a n) -> p a n", a=3)
        yrow = xrow
        va = sb("va", [P, 3, 512])
        ring = sb("ring", [P, RING, KT * CH])
        mod = sb("mod", [P, DEPTH, 48, 9])
        vrow = sb("vrow", [P, 4, P])
        vecT = sb("vecT", [P, 3, P])
        siluC = sb("siluC", [P, KT, 32])
        C = sb("C", [P, NC])
        dP = sb("dP", [P, 2, SEQ])
        dS = sb("dS", [P, PAST])
        dN = sb("dN", [P, NPAIR, NS])
        onesm = sb("onesm", [P, P])
        mean1 = sb("mean1", [P, P])
        cols = sb("cols", [P, 4])
        rstd = sb("rstd", [P, 2, NTOK])
        lnv = sb("lnv", [P, NTOK])
        wba = sb("wba", [P, DEPTH, KT, 8])
        wr = sb("wr", [P, KT, NE])
        small = sb("small", [P, 128])
        route = sb("route", [P, 3, 3, NE + 1])
        cls = sb("cls", [P, NE], I32)
        lamb = sb("lamb", [P, DEPTH, 256])
        lamw = sb("lamw", [P, 8])
        lamc = sb("lamc", [P, DEPTH, 2])
        adt = sb("adt", [P, 2, DEPTH, H])
        brb = sb("brb", [P, NE])
        pt_sb = sb("pt_sb", [1, NSEQ * NPG], I32)
        rowb = mixT[:, :, :].rearrange("p k t -> p (k t)")[0:27, 0:3 * 512]
        tail = sb("tail", [P, 12, 27])
        kst = sb("kst", [P, 3, 512])
        ctmp = sb("ctmp", [P, 2, NTOK])
        Sp = sb("Sp", [P, H, P])
        region = sb("region", [P, REGION])
        off = [0]

        def cut(n):
            off[0] += n
            assert off[0] <= REGION, off[0]
            return region[:, off[0] - n:off[0]]

        vring = cut(8 * 512).rearrange("p (a n) -> p a n", a=8)
        kring = cut(4 * 512).rearrange("p (a n) -> p a n", a=4)
        ktb = cut(2 * 512).rearrange("p (a n) -> p a n", a=2)
        scb = cut(2 * (PAST + NS)).rearrange("p (a n) -> p a n", a=2)
        ptb = cut(9 * P).rearrange("p (a n) -> p a n", a=9)
        qbd = cut(2 * H * 32).rearrange("p (a h n) -> p a h n", a=2, h=H)
        ob = cut(2 * P).rearrange("p (a n) -> p a n", a=2)
        oA = cut(H * NTOK).rearrange("p (h t) -> p h t", h=H)
        ptr = ptb[:, 0:4, :].rearrange("p a n -> p (a n)").rearrange("p (a n) -> p a n", a=2)
        off[0] = 0
        Ss = cut(NSEQ * H * P).rearrange("p (s h v) -> p s h v", s=NSEQ, h=H)
        g4 = lambda: cut(512)
        Gb_e, bbs, DT, LT, QK, LM, X, XT, PP, rT, rr, vn, kd, qd, oG, sG = [g4() for _ in range(16)]
        kdm = DT, LT
        off[0] = 0
        hrow = cut(3 * D).rearrange("p (a n) -> p a n", a=3)
        frow = cut(3 * D).rearrange("p (a n) -> p a n", a=3)
        Xe = cut(KT * NTOK).rearrange("p (k t) -> p k t", k=KT)
        Sel, SelG, GT = [cut(3 * NTOK).rearrange("p (a t) -> p a t", a=3) for _ in range(3)]
        sil = kst[:, :, :].rearrange("p a n -> p (a n)")[:, 0:4 * NTOK].rearrange("p (b a t) -> p b a t", b=2, a=2)

        ident = C[:, C_ID:C_ID + P]
        tri = C[:, C_TRI:C_TRI + P]

        def c3(t, a):
            return t.rearrange("p (h t) -> p h t", h=H)[:, :, 0:a]

        s_tab = sem("tables_loaded")
        s_pt = sem("page_table_loaded")
        s_ones = sem("ones_written")
        s_full = [sem(f"chunk_loaded_{i}") for i in range(RING)]
        s_chunk = sem("chunk_done")
        s_vecT = sem("vectors_transposed")
        s_vec = sem("vectors_copied")
        s_xt = sem("x_transposed")
        s_silc = sem("silu_c")
        s_adE = sem("mod_rows")
        s_adT = sem("mod_turned")
        s_modev = sem("mod_copied")
        s_mod = sem("mod_ready")
        s_lnin = sem("ln_input")
        s_mean = sem("ln_mean")
        s_xc = sem("ln_centered")
        s_sq = sem("ln_squared")
        s_var = sem("ln_var")
        s_rstd = sem("ln_rstd")
        s_xn = sem("ln_scaled")
        s_h = sem("h_prompt")
        s_hs = sem("h_sample")
        s_xa = sem("x_times_alpha")
        s_pev = sem("proj_copied")
        s_va = sem("v_rows")
        s_ba = sem("ba_done")
        s_bae = sem("ba_copied")
        s_hist = sem("history_loaded")
        s_histT = sem("history_transposed")
        s_histc = sem("history_placed")
        s_kT = sem("k_rows_psum")
        s_kst = sem("k_rows")
        s_tail = sem("tail_gathered")
        s_tailT = sem("tail_transposed")
        s_tailc = sem("tail_rows")
        s_conv = sem("conv_done")
        s_csil = sem("conv_silu")
        s_l2q = sem("l2_squared")
        s_l2s = sem("l2_summed")
        s_l2r = sem("l2_rinv")
        s_l2d = sem("l2_done")
        s_lam = sem("lambda_ready")
        s_pS = sem("p_scores")
        s_pM = sem("p_max")
        s_pE = sem("p_exp")
        s_pA = sem("p_probs")
        s_pT = sem("p_probsT_psum")
        s_pTc = sem("p_probsT")
        s_pV = sem("p_pv")
        s_pO = sem("p_out")
        s_qbz = sem("q_blocks_zero")
        s_qb = sem("q_blocks")
        s_kf = [sem(f"k_page_{i}") for i in range(4)]
        s_vf = [sem(f"v_page_{i}") for i in range(8)]
        s_kt = sem("k_page_transposed")
        s_ktA = sem("k_page_copied_act")
        s_kmm = sem("k_page_scored")
        s_sS = sem("s_scores")
        s_sM = sem("s_max")
        s_sE = sem("s_exp")
        s_sP = sem("s_probs")
        s_sT = sem("s_probsT_psum")
        s_sTc = sem("s_probsT")
        s_sTd = sem("s_probsT_last")
        s_vd = sem("v_page_used")
        s_ob = sem("s_pv_rows")
        s_oT = sem("s_pv_turned")
        s_sV = sem("s_pv")
        s_sO = sem("s_out")
        s_oq = sem("attn_squared")
        s_os = sem("attn_summed")
        s_or = sem("attn_rstd")
        s_mA = sem("attn_mixed")
        s_bt = sem("beta_g_ready")
        s_bta = sem("beta_g_act")
        s_btd = sem("beta_g_dve")
        s_S0 = sem("state_loaded")
        s_gG = sem("g_sums")
        s_gGc = sem("g_sums_copied")
        s_gE = sem("g_exp")
        s_gK = sem("g_kk_kq_k")
        s_gL = sem("g_L_ready")
        s_gkd = sem("g_kdec")
        s_lm = sem("g_level_mask")
        s_g1 = sem("g_level_P")
        s_g1c = sem("g_level_P_copied")
        s_g2 = sem("g_level_Q")
        s_g2c = sem("g_level_updated")
        s_gR = sem("g_kS")
        s_gRc = sem("g_rT")
        s_gRt = sem("g_r_psum")
        s_gr = sem("g_r")
        s_gV = sem("g_vnew_psum")
        s_gv = sem("g_vnew")
        s_gO = sem("g_o_psum")
        s_go = sem("g_o")
        s_gS = sem("g_state_psum")
        s_gSc = sem("g_state")
        s_gkm = sem("g_kdec_masked")
        s_goq = sem("g_o_squared")
        s_gos = sem("g_o_summed")
        s_gor = sem("g_o_rstd")
        s_mB = sem("gdn_mixed")
        s_res = sem("wout_added")
        s_rt = sem("router_logits")
        s_rtm = sem("router_max")
        s_rte = sem("router_exp")
        s_hrT = sem("h_rows_psum")
        s_hr = sem("h_rows")
        s_sel = sem("experts_chosen")
        s_pos = sem("slots_counted")
        s_route = sem("routing_ready")
        s_route2 = sem("counts_compared")
        s_prep = sem("selection_ready")
        s_gtT = sem("gate_selection_psum")
        s_gt = sem("gate_selection_turned")
        s_xeT = sem("packed_psum")
        s_xe = sem("packed")
        s_fr = sem("expert_rows")
        s_cb = sem("expert_sum_psum")
        s_fa = sem("expert_summed")
        s_sil = sem("gate_silu")
        s_ff = sem("ff_ready")
        s_turn = sem("values_begun")
        s_yT = sem("y_rows_psum")
        s_y = sem("y_rows")
        s_out = sem("outputs_stored")
        s_cd = sem("dve_chain")
        s_ca = sem("act_chain")
        s_cp = sem("pool_chain")
        N_OUT = [0]

        block = ctx.enter_context(nc.Block())

        def full(pos, e=0):
            return s_full[pos % RING], 16 * (pos // RING + 1) + e * (16 * MLP_POS // RING)

        def chunk(pos):
            return ring[:, pos % RING, :].rearrange("p (k n) -> p k n", n=CH)

        def wsrc(w, col):
            return w[:, bass.ds(col, CH)].rearrange("(k p) n -> p k n", p=P)

        N_TAB = [0]

        def tables(sp):
            def ld(dst, src):
                N_TAB[0] += 16
                sp.dma_start(dst, src).then_inc(s_tab, 16)

            ld(C[:], t_c)
            ld(vrow[0:96, 0, :], ada_b.rearrange("l (f p) -> (l f) p", p=P))
            ld(vrow[96:98, 0, :], subln)
            ld(vrow[98:100, 0, :], norm_b)
            ld(vrow[0:96, 1, :], conv_w.rearrange("l w (f p) -> (l w f) p", p=P))
            for n, v in enumerate((ln1_g, ln1_b, ln2_g, ln2_b)):
                ld(vrow[16 * n:16 * n + 16, 2, :], v.rearrange("l (f p) -> (l f) p", p=P))
            ld(vrow[0:8, 3, :], c_p.rearrange("a (f p) -> (a f) p", p=P))
            ld(vrow[8:72, 3, :], c_s.rearrange("a (f p) -> (a f) p", p=P))
            ld(xrow[:, 0:2, :], x_p[0].rearrange("(a p) n -> p a n", p=P))
            ld(xrow[0:NS, 2, :], x_s.rearrange("s t n -> (s t) n"))
            ld(dP[:], t_dp.rearrange("p (a n) -> p a n", a=2))
            ld(dS[:], t_ds)
            ld(dN[:], t_dn.rearrange("p (a n) -> p a n", a=NPAIR))
            for l in range(DEPTH):
                ld(wba[:, l, :, :], w_in[l][:, 3072:3080].rearrange("(k p) n -> p k n", p=P))
                ld(lamb[:, l, :], lam_p[l:l + 1].rearrange("o a b -> o (a b)").to_broadcast([P, 256]))
                ld(adt[:, 0, l, :], a_log[l:l + 1, :].to_broadcast([P, H]))
                ld(adt[:, 1, l, :], dt_bias[l:l + 1, :].to_broadcast([P, H]))
            ld(wr[:], m_r[0].rearrange("(k p) n -> p k n", p=P))
            ld(brb[:], m_rb[0:1, :].to_broadcast([P, NE]))

        N_TABLES = 16 * 26

        @block.sync
        def _(sp):
            tables(sp)
            assert N_TAB[0] == N_TABLES, N_TAB[0]
            sp.dma_start(pt_sb[:], ptab.rearrange("(o a) b -> o (a b)", o=1)).then_inc(s_pt, 16)

            def load(dst, src, pos, e=0, first=False):
                if not first:
                    sp.wait_ge(s_chunk, pos - RING + 1 + e * MLP_POS)
                sp.dma_start(dst, src).then_inc(full(pos)[0], 16)

            for c in range(RING):
                load(chunk(c), wsrc(ada_w[0], CH * c), c, first=True)
            for l in range(DEPTH):
                with sp.Fori(1 if l == 0 else 0, ADA_CH // RING) as i:
                    for c in range(RING):
                        sp.wait_ge(s_chunk, ADA_CH * l + c - RING + 1 + i * RING)
                        sp.dma_start(chunk(c), wsrc(ada_w[l], i * (RING * CH) + CH * c)).then_inc(s_full[c], 16)

            def mlp(w_up, w_dn, pos, e=0):
                for j in range(UP):
                    for part in range(2):
                        p = pos + 2 * j + part
                        load(chunk(p), wsrc(w_up, part * FF + CH * j), p, e)
                for d in range(4):
                    for n, (f0, nf) in enumerate(DN_ROWS):
                        p = pos + 2 * UP + 3 * d + n
                        load(chunk(p)[:, 0:nf, :],
                             w_dn[f0 * P:(f0 + nf) * P, CH * d:CH * (d + 1)].rearrange("(k p) n -> p k n", p=P), p, e)
                for p in range(pos + MLP_CH, pos + MLP_POS):
                    sp.wait_ge(s_chunk, p - RING + 1 + e * MLP_POS)
                    sp.sem_inc(full(p)[0], 16)

            for l in range(DEPTH):
                for c in range(N_WIN):
                    load(chunk(POS_WIN[l] + c), wsrc(w_in[l], WIN_COLS[c]), POS_WIN[l] + c)
                if l > 0:
                    sp.wait_ge(s_chunk, POS_VO[l - 1] + N_VO)
                sp.dma_start(rowb[0:24, :], st_conv[l].rearrange("s r n -> (s r) n")).then_inc(s_hist, 16)
                for c in range(2):
                    load(chunk(POS_VO[l] + c), wsrc(w_in[l], 1024 + CH * c), POS_VO[l] + c)
                for c in range(4):
                    load(chunk(POS_VO[l] + 2 + c), wsrc(w_out[l], CH * c), POS_VO[l] + 2 + c)
                if l == 0:
                    sp.wait_ge(s_pt, 16)
                else:
                    sp.wait_ge(s_mB, 3 * l)
                    sp.wait_ge(s_out, 16 * 8 * l)

                def v_pages(s):
                    for p in range(NPG):
                        pg = sp.value_load(pt_sb[0:1, bass.ds(s * NPG + p, 1)], min_val=0, max_val=NPOOL - 1)
                        if l or not isinstance(s, int):
                            sp.wait_ge(s_vd, 64 * l + s * NPG + p - 7)
                        sp.dma_start(vring[:, p, :], cache_v[l, bass.ds(pg, 1)].rearrange("o k h d -> (o k) (h d)")
                                     ).then_inc(s_vf[p], 16)

                v_pages(0)
                with sp.Fori(1, NSEQ) as s:
                    v_pages(s)
                if l == 0:
                    mlp(dw_up[0], dw_dn[0], POS_MLP[0])
                else:
                    with sp.Fori(0, NE) as e:
                        mlp(mw_up[0, bass.ds(e, 1)].rearrange("o a b -> (o a) b"),
                            mw_dn[0, bass.ds(e, 1)].rearrange("o a b -> (o a) b"), POS_MLP[1], e)

        @block.gpsimd
        def _(pool):
            link = Chain(pool, s_cp)
            nc.gpsimd.memset(onesm[:], 1.0).then_inc(s_ones, 1)
            nc.gpsimd.memset(mean1[:], 1.0 / D).then_inc(s_ones, 1)
            nc.gpsimd.memset(cols[:, 0:1], LN_EPS).then_inc(s_ones, 1)
            nc.gpsimd.memset(cols[:, 1:2], 1e-6).then_inc(s_ones, 1)
            nc.gpsimd.memset(cols[:, 2:3], -0.5 * math.log(P)).then_inc(s_ones, 1)
            nc.gpsimd.memset(cols[:, 3:4], 1.0).then_inc(s_ones, 1)
            nc.gpsimd.memset(small[:], 0.0).then_inc(s_ones, 1)
            nc.gpsimd.memset(siluC[:], 0.0).then_inc(s_ones, 1)
            pool.wait_ge(s_pt, 16)
            n_out = 0

            def store(dst, src):
                pool.dma_start(dst, src).then_inc(s_out, 16)

            for l in range(DEPTH):
                if l > 0:
                    pool.wait_ge(s_mB, 3 * l)
                    pool.wait_ge(s_out, 16 * 8 * l)
                nc.gpsimd.memset(qbd[:], 0.0).then_inc(s_qbz, 1)

                def pages(s):
                    for p in range(NPG):
                        pg = pool.value_load(pt_sb[0:1, bass.ds(s * NPG + p, 1)], min_val=0, max_val=NPOOL - 1)
                        if p >= 4 or not isinstance(s, int) or s > 0 or l > 0:
                            pool.wait_ge(s_kt, 64 * l + s * NPG + p - 3)
                        pool.dma_start(kring[:, p % 4, :], cache_k[l, bass.ds(pg, 1)].rearrange("o k h d -> (o k) (h d)")
                                       ).then_inc(s_kf[p % 4], 16)

                pages(0)
                with pool.Fori(1, NSEQ) as s:
                    pages(s)
                pool.wait_ge(s_va, 2 * (l + 1))
                store(v_p[l, 0].rearrange("(a p) h d -> p a (h d)", p=P), va[:, 0:2, :])
                store(v_s[l].rearrange("s t h d -> (s t) (h d)"), va[0:NS, 2, :])
                pool.wait_ge(s_kst, l + 1)
                store(k_p[l, 0].rearrange("(a p) h d -> p a (h d)", p=P), kst[:, 0:2, :])
                store(k_s[l].rearrange("s t h d -> (s t) (h d)"), kst[0:NS, 2, :])
                pool.wait_ge(s_tailc, l + 1)
                store(cv_p[l, 0], rowb[0:3, :])
                store(cv_s[l].rearrange("s r n -> (s r) n"), rowb[3:27, :])
                pool.wait_ge(s_mA, H * (l + 1))
                pool.dma_start(Ss, st_delta[l].rearrange("s h k v -> k s h v")).then_inc(s_S0, 16)
                pool.wait_ge(s_gSc, 34 * l + 2)
                store(dl_p[l, 0].rearrange("h k v -> k h v"), Sp[:])
                pool.wait_ge(s_gSc, 34 * l + 34)
                store(dl_s[l].rearrange("s h k v -> k s h v"), Ss)
            pool.wait_ge(s_y, 3)
            store(y_p[0].rearrange("(a p) n -> p a n", p=P), yrow[:, 0:2, :])
            store(y_s.rearrange("s t n -> (s t) n"), yrow[0:NS, 2, :])
            pool.wait_ge(s_out, 16 * 18)

        @block.tensor
        def _(pe):
            mm, tr = nc.tensor.matmul, nc.tensor.transpose

            def ln(n):
                for k in range(KT):
                    pe.wait_ge(s_lnin, KT * n + k + 1)
                    m = mm(ps[:, 0, 0:NTOK], mean1[:], xT[:, k, :], start=(k == 0), stop=(k == KT - 1))
                m.then_inc(s_mean, 1)
                for k in range(KT):
                    if k % 2 == 0:
                        pe.wait_ge(s_sq, 4 * n + k // 2 + 1)
                    m = mm(ps[:, 1, 0:NTOK], mean1[:], sq[:, k, :], start=(k == 0), stop=(k == KT - 1))
                m.then_inc(s_var, 1)

            def take(pos, e=0):
                pe.wait_ge(*full(pos, e))
                return chunk(pos)

            def two_tiles(w, b, rhs, n=NTOK, nk=KT, first=True, last=True):
                for o in range(2):
                    for k in range(nk):
                        m = mm(ps[:, b + o, 0:n], w[:, k, o * P:(o + 1) * P], rhs[:, k, 0:n],
                               start=(first and k == 0), stop=(last and k == nk - 1))
                return m

            def h_ready(m):
                pe.wait_ge(s_h, KT * (m + 1))
                pe.wait_ge(s_hs, m + 1)

            def up(pos, e, nff, rhs, n):
                for j in range(UP):
                    b = 4 * (j % 2)
                    if j >= 2:
                        pe.wait_ge(s_ff, nff + j - 1)
                    w = take(pos + 2 * j, e)
                    two_tiles(w, b, rhs, n).then_inc(s_chunk, 1)
                    w = take(pos + 2 * j + 1, e)
                    two_tiles(w, b + 2, rhs, n).then_inc(s_chunk, 1)
                pe.wait_ge(s_ff, nff + UP)

            def dense():
                up(POS_MLP[0], 0, 0, hT, NTOK)
                for d in range(4):
                    for i, (f0, nf) in enumerate(DN_ROWS):
                        w = take(POS_MLP[0] + 2 * UP + 3 * d + i)
                        for o in range(2):
                            for k in range(nf):
                                m = mm(ps[:, 2 * d + o, 0:NTOK], w[:, k, o * P:(o + 1) * P], ff[:, f0 + k, :],
                                       start=(i == 0 and k == 0), stop=(i == 2 and k == nf - 1))
                        m.then_inc(s_chunk, 1 + (MLP_POS - MLP_CH if d == 3 and i == 2 else 0))

            def expert(e, slots, rows):
                pos = POS_MLP[1]
                pe.wait_ge(s_prep, e + 1)
                for s_, (r0, nr) in enumerate(rows):
                    for t, (c0, nt) in enumerate(TILES):
                        m = tr(ps[0:nr, s_, c0:c0 + nt], SelG[0:nt, t, r0:r0 + nr], ident[0:nt, 0:nt])
                m.then_inc(s_gtT, 1)
                pe.wait_ge(s_fa, KT + e * KT)
                for k in range(KT):
                    if k >= 4:
                        pe.wait_ge(s_xe, e * KT + k - 3)
                    for t, (c0, nt) in enumerate(TILES):
                        m = mm(ps[:, 4 + k % 4, 0:slots], hrow[0:nt, t, k * P:(k + 1) * P], Sel[0:nt, t, 0:slots],
                               start=(t == 0), stop=(t == 2))
                    m.then_inc(s_xeT, 1)
                pe.wait_ge(s_xe, e * KT + KT)
                pe.wait_ge(s_gt, e + 1)
                up(pos, e, UP + e * UP, Xe, slots)
                for d in range(4):
                    if d >= 2:
                        pe.wait_ge(s_fr, e * 4 + d - 1)
                    for i, (f0, nf) in enumerate(DN_ROWS):
                        w = take(pos + 2 * UP + 3 * d + i, e)
                        for k in range(nf):
                            for s_, (r0, nr) in enumerate(rows):
                                m = mm(ps[0:nr, 3 * (d % 2) + s_, 0:CH], ff[:, f0 + k, r0:r0 + nr], w[:, k, :],
                                       start=(i == 0 and k == 0), stop=(i == 2 and k == nf - 1))
                        m.then_inc(s_chunk, 1 + (MLP_POS - MLP_CH if d == 3 and i == 2 else 0))
                pe.wait_ge(s_fr, e * 4 + 4)
                for k in range(KT):
                    if k >= 2:
                        pe.wait_ge(s_fa, KT + e * KT + k - 1)
                    for s_, (r0, nr) in enumerate(rows):
                        m = mm(ps[:, 6 + k % 2, 0:NTOK], frow[0:nr, s_, k * P:(k + 1) * P], GT[0:nr, s_, :],
                               start=(s_ == 0), stop=(s_ == len(rows) - 1))
                    m.then_inc(s_cb, 1)

            pe.wait_ge(s_tab, N_TABLES)
            pe.wait_ge(s_ones, 8)
            for b, n in enumerate((100, 96, 64, 72)):
                m = tr(ps[:, 0, b * P:b * P + n], vrow[0:n, b, :], ident[0:n, 0:n])
            m.then_inc(s_vecT, 1)
            for k in range(KT):
                if k >= 4:
                    pe.wait_ge(s_lnin, k - 3)
                for t, (c0, nt) in enumerate(TILES):
                    m = tr(ps[:, 1 + k % 4, c0:c0 + nt], xrow[0:nt, t, k * P:(k + 1) * P], ident[0:nt, 0:nt])
                m.then_inc(s_xt, 1)
            pe.wait_ge(s_silc, 1)
            def turn_mod(c, n):
                pe.wait_ge(s_adE, n + 1)
                if not (isinstance(n, int) and n < 2):
                    pe.wait_ge(s_modev, n - 1)
                for o in range(2):
                    m = mm(ps[:, 5 * (c % 2), 16 * o:16 * o + 9], kst[:, c % 2, o * P:(o + 1) * P], C[:, C_GRP:C_GRP + 9],
                           start=True, stop=True)
                m.then_inc(s_adT, 1)

            def ada(i):
                for c in range(RING):
                    n = i * RING + c
                    pe.wait_ge(s_full[c], 16 + 16 * i)
                    if c >= 2 or not isinstance(i, int):
                        pe.wait_ge(s_adE, n - 1)
                    for k in range(KT):
                        g = 32 * (k % 4)
                        m = mm(ps[g:g + 32, 6 + c % 2, 0:CH], siluC[:, k, :], chunk(c)[:, k, :], start=(k < 4), stop=(k >= 4))
                    m.then_inc(s_chunk, 1)
                    if c >= 1 or not isinstance(i, int):
                        turn_mod((c - 1) % RING, n - 1)

            ada(0)
            with pe.Fori(1, DEPTH * ADA_CH // RING) as i:
                ada(i)
            turn_mod(RING - 1, DEPTH * ADA_CH - 1)
            pe.wait_ge(s_modev, DEPTH * ADA_CH)

            for l in range(DEPTH):
                ln(4 * l)
                h_ready(2 * l)
                for c in range(N_WIN):
                    w = take(POS_WIN[l] + c)
                    if c >= 4:
                        pe.wait_ge(s_pev, N_WIN * l + c - 3)
                    two_tiles(w, 2 * (c % 4), hT).then_inc(s_chunk, 1)
                pe.wait_ge(s_pev, N_WIN * (l + 1))
                for t, (c0, nt) in enumerate(TILES):
                    for k in range(KT):
                        m = mm(ps[0:nt, 6, 8 * t:8 * t + 8], hT[:, k, c0:c0 + nt], wba[:, l, k, :],
                               start=(k == 0), stop=(k == KT - 1))
                m.then_inc(s_ba, 1)
                pe.wait_ge(s_hist, 16 * (l + 1))
                for f in range(12):
                    m = tr(ps[:, 7, 24 * f:24 * f + 24], rowb[0:24, f * P:(f + 1) * P], ident[0:24, 0:24])
                m.then_inc(s_histT, 1)
                for c in range(2):
                    w = take(POS_VO[l] + c)
                    for t, (c0, nt) in enumerate(TILES):
                        for k in range(KT):
                            m = mm(ps[0:nt, 3 * c + t, 0:CH], hT[:, k, c0:c0 + nt], w[:, k, :],
                                   start=(k == 0), stop=(k == KT - 1))
                    m.then_inc(s_chunk, 1)
                pe.wait_ge(s_va, 2 * (l + 1))
                for t, (c0, nt) in enumerate(TILES):
                    for h in range(H):
                        m = tr(ps[0:nt, t, h * P:(h + 1) * P], pA[:, 4 + h, c0:c0 + nt], ident)
                m.then_inc(s_kT, 1)
                pe.wait_ge(s_tail, l + 1)
                for f in range(12):
                    m = tr(ps[0:27, 3 + f // 4, (f % 4) * P:(f % 4 + 1) * P], tail[:, f, :], ident)
                m.then_inc(s_tailT, 1)
                pe.wait_ge(s_histc, l + 1)
                pe.wait_ge(s_bae, l + 1)
                for f in range(8):
                    pe.wait_ge(s_l2q, 8 * l + f + 1)
                    if f >= 2:
                        pe.wait_ge(s_l2r, 8 * l + f - 1)
                    mm(ps[:, 6 + f % 2, 0:NTOK], onesm[:], ctmp[:, f % 2, :], start=True, stop=True).then_inc(s_l2s, 1)

                units = [(h, qt) for h in range(H) for qt in range(2)]

                def scores(u):
                    h, qt = units[u]
                    nk = P * (qt + 1)
                    if u == 0:
                        pe.wait_ge(s_kst, l + 1)
                        pe.wait_ge(s_tailc, l + 1)
                        pe.wait_ge(s_l2r, 8 * (l + 1))
                    if u >= 2:
                        pe.wait_ge(s_pM, 8 * l + u - 1)
                    for m_ in range(2):
                        r = slice(64 * m_, 64 * m_ + 64)
                        m = mm(ps[:, 2 * (u % 2) + m_, 0:nk], pA[r, h, qt * P:(qt + 1) * P],
                               pA[r, 4 + h, 0:nk], start=True, stop=True)
                    m.then_inc(s_pS, 1)

                scores(0)
                for u, (h, qt) in enumerate(units):
                    if u + 1 < 8:
                        scores(u + 1)
                    pe.wait_ge(s_pA, 8 * l + u + 1)
                    if u >= 1:
                        pe.wait_ge(s_pTc, 8 * l + u)
                    for kb in range(qt + 1):
                        m = tr(ps[:, 4, kb * P:(kb + 1) * P], scb[:, u % 2, kb * P:(kb + 1) * P], ident)
                    m.then_inc(s_pT, 1)
                    pe.wait_ge(s_pTc, 8 * l + u + 1)
                    if u >= 2:
                        pe.wait_ge(s_pO, 8 * l + u - 1)
                    for kb in range(qt + 1):
                        m = mm(ps[:, 5 + u % 2, 0:P], va[:, kb, h * P:(h + 1) * P], ptr[:, u % 2, kb * P:(kb + 1) * P],
                               start=(kb == 0), stop=(kb == qt))
                    m.then_inc(s_pV, 1)

                pe.wait_ge(s_pO, 8 * (l + 1))

                def pair_scores(i):
                    g = NPAIR * l + i
                    early = l == 0 and isinstance(i, int) and i == 0

                    def turn(n):
                        pe.wait_ge(s_kf[n % 4], 16 * (4 * g + n // 4 + 1))
                        if not (early and n < 2):
                            pe.wait_ge(s_ktA, 16 * g + n - 1)
                        for h in range(H):
                            m = tr(ps[:, n % 2, h * P:(h + 1) * P], kring[:, n % 4, h * P:(h + 1) * P], ident)
                        m.then_inc(s_kt, 1)

                    turn(0)
                    for n in range(2 * NPG):
                        a, p = n // NPG, n % NPG
                        if n + 1 < 2 * NPG:
                            turn(n + 1)
                        if n == 0:
                            pe.wait_ge(s_qb, g + 1)
                            if not early:
                                pe.wait_ge(s_sM, g)
                        pe.wait_ge(s_ktA, 16 * g + n + 1)
                        for h in range(H):
                            m = mm(ps[32 * h:32 * h + 32, 2 + p // 4, (p % 4) * P:(p % 4 + 1) * P], qbd[:, a, h, :],
                                   ktb[:, n % 2, h * P:(h + 1) * P], start=(a == 0 and p % 4 == 0), stop=(a == 1 and p % 4 == 3))
                        m.then_inc(s_kmm, 1)
                    for a in range(2):
                        for h in range(H):
                            m = mm(ps[32 * h:32 * h + 32, 4, 0:NS], qbd[:, a, h, :], pA[:, 4 + h, SEQ:NTOK], start=(a == 0), stop=(a == 1))
                    m.then_inc(s_sS, 1)

                def pair_values(i):
                    g = NPAIR * l + i
                    early = l == 0 and isinstance(i, int) and i == 0
                    pe.wait_ge(s_sP, g + 1)
                    if not early:
                        pe.wait_ge(s_sO, g)
                    pe.sem_inc(s_turn, 1)
                    for p in range(NPG):
                        tr(ps[:, 5 + p // 4, (p % 4) * P:(p % 4 + 1) * P], scb[:, 0, p * P:(p + 1) * P], ident)
                    tr(ps[0:64, 4, P:2 * P], scb[:, 0, PAST:PAST + NS], ident).then_inc(s_sT, 1)
                    pe.wait_ge(s_sTc, g + 1)
                    pe.wait_ge(s_sTd, g + 1)
                    for a in range(2):
                        out = lambda h: ps[32 * h:32 * h + 32, 7 - 2 * a, 0:P]
                        for p in range(NPG):
                            pe.wait_ge(s_vf[p], 16 * (2 * g + a + 1))
                            for h in range(H):
                                m = mm(out(h), ptb[:, p, 32 * h:32 * h + 32], vring[:, p, h * P:(h + 1) * P], start=(p == 0), stop=False)
                            m.then_inc(s_vd, 1)
                        for h in range(H):
                            m = mm(out(h), ptb[0:NS, 8, 32 * h:32 * h + 32], va[0:NS, 2, h * P:(h + 1) * P], start=False, stop=True)
                        m.then_inc(s_sV, 1)
                    for a in range(2):
                        pe.wait_ge(s_ob, 2 * g + a + 1)
                        m = mm(ps[:, 6, 32 * a:32 * (a + 1)], ob[:, a, :], C[:, C_PAIR + 32 * a:C_PAIR + 32 * (a + 1)],
                               start=True, stop=True)
                    m.then_inc(s_oT, 1)

                def pair(i):
                    pair_scores(i + 1)
                    pair_values(i)

                pair_scores(0)
                pair(0)
                with pe.Fori(1, NPAIR - 1) as i:
                    pair(i)
                pair_values(NPAIR - 1)

                for h in range(H):
                    pe.wait_ge(s_oq, H * l + h + 1)
                    if h >= 2:
                        pe.wait_ge(s_or, H * l + h - 1)
                    mm(ps[:, h % 2, 0:NTOK], onesm[:], ctmp[:, h % 2, :], start=True, stop=True).then_inc(s_os, 1)

                pe.wait_ge(s_or, H * (l + 1))
                pe.wait_ge(s_bt, l + 1)
                pe.wait_ge(s_l2d, 8 * (l + 1))
                for T, (c0, nt) in enumerate(TILES):
                    n = 3 * l + T
                    smp = T == 2
                    lev = 3 if smp else 7
                    triT = C[0:nt, C_TRIS:C_TRIS + nt] if smp else tri
                    same = C[0:nt, C_SAME:C_SAME + nt] if smp else onesm[:]
                    if n > 0:
                        pe.wait_ge(s_mB, n)
                    gcol = small[0:nt, 24 + 4 * T:28 + 4 * T]
                    bcol = small[0:nt, 36 + 4 * T:40 + 4 * T]
                    mm(ps[0:nt, 0, 0:4], triT, gcol, start=True, stop=True)
                    mm(ps[0:nt, 0, 4:8], same, gcol, start=True, stop=True)
                    for h in range(H):
                        mm(ps[:, 1, h * P:h * P + nt], gcol[:, h:h + 1].to_broadcast([nt, P]), triT, start=True, stop=True)
                    for h in range(H):
                        m = mm(ps[:, 2, h * P:h * P + nt], bcol[:, h:h + 1].to_broadcast([nt, P]), ident[0:nt, 0:nt],
                               start=True, stop=True)
                    m.then_inc(s_gG, 1)
                    kT = pB[:, 4:8, c0:c0 + nt]
                    qT = pB[:, 0:4, c0:c0 + nt]
                    for h in range(H):
                        mm(ps[0:nt, 3, h * P:h * P + nt], kT[:, h, :], kT[:, h, :], start=True, stop=True)
                    for h in range(H):
                        mm(ps[0:nt, 4, h * P:h * P + nt], kT[:, h, :], qT[:, h, :], start=True, stop=True)
                    for h in range(H):
                        m = tr(ps[0:nt, 5, h * P:(h + 1) * P], kT[:, h, :], ident)
                    m.then_inc(s_gK, 1)
                    LM3, X3, XT3, PP3 = c3(LM, nt), c3(X, nt), c3(XT, nt), c3(PP, nt)
                    for v in range(lev):
                        i0 = 17 * l + 7 * T + v
                        pe.wait_ge(s_lm, i0 + 1)
                        for h in range(H):
                            m = mm(ps[0:nt, 6, h * P:h * P + nt], LM3[0:nt, h, :], X3[0:nt, h, :], start=True, stop=True)
                        m.then_inc(s_g1, 1)
                        pe.wait_ge(s_g1c, i0 + 1)
                        for h in range(H):
                            mm(ps[0:nt, 7, h * P:h * P + nt], XT3[0:nt, h, :], PP3[0:nt, h, :], start=True, stop=True)
                        if v == 0:
                            pe.wait_ge(s_gE, n + 1)
                        for h in range(H):
                            m = mm(ps[0:nt, 0, h * P:h * P + nt], PP3[0:nt, h, :], XT3[0:nt, h, :], start=True, stop=True)
                        m.then_inc(s_g2, 1)
                    if smp:
                        pe.wait_ge(s_S0, 16 * (l + 1))
                    if T == 1:
                        pe.wait_ge(s_gSc, 34 * l + 1)
                    for h in range(H):
                        if smp:
                            for s in range(NSEQ):
                                m = mm(ps[:, 1, h * P + 8 * s:h * P + 8 * s + 8], Ss[:, s, h, :], kT[:, h, 8 * s:8 * s + 8],
                                       start=True, stop=True)
                        else:
                            m = mm(ps[:, 1, h * P:h * P + nt], Sp[:, h, :], kT[:, h, :], start=True, stop=True)
                    m.then_inc(s_gR, 1)
                    pe.wait_ge(s_gRc, n + 1)
                    for h in range(H):
                        m = tr(ps[0:nt, 2, h * P:(h + 1) * P], c3(rT, nt)[:, h, :], ident)
                    m.then_inc(s_gRt, 1)
                    pe.wait_ge(s_gr, n + 1)
                    pe.wait_ge(s_g2c, 17 * l + 7 * T + lev)
                    for h in range(H):
                        m = mm(ps[0:nt, 3, h * P:(h + 1) * P], XT3[0:nt, h, :], c3(rr, P)[0:nt, h, :], start=True, stop=True)
                    m.then_inc(s_gV, 1)
                    pe.wait_ge(s_gv, n + 1)
                    for h in range(H):
                        mm(ps[:, 4, h * P:h * P + nt], c3(vn, P)[0:nt, h, :], c3(QK, nt)[0:nt, h, :], start=True, stop=False)
                        if smp:
                            for s in range(NSEQ):
                                m = mm(ps[:, 4, h * P + 8 * s:h * P + 8 * s + 8], Ss[:, s, h, :], c3(qd, nt)[:, h, 8 * s:8 * s + 8],
                                       start=False, stop=(s == NSEQ - 1))
                        else:
                            m = mm(ps[:, 4, h * P:h * P + nt], Sp[:, h, :], c3(qd, nt)[:, h, :], start=False, stop=True)
                    m.then_inc(s_gO, 1)
                    if smp:
                        for h in range(H):
                            pe.wait_ge(s_gkm, H * l + h + 1)
                            if h > 0:
                                pe.wait_ge(s_gSc, 34 * l + 2 + 8 * h)
                            for s in range(NSEQ):
                                m = mm(ps[:, 5 + s // 4, (s % 4) * P:(s % 4 + 1) * P], kdm[s // 4][0:nt, (s % 4) * P:(s % 4 + 1) * P],
                                       c3(vn, P)[0:nt, h, :], start=True, stop=True)
                            m.then_inc(s_gS, 1)
                    else:
                        pe.wait_ge(s_gkd, n + 1)
                        for h in range(H):
                            m = mm(ps[:, 5, h * P:(h + 1) * P], c3(kd, P)[0:nt, h, :], c3(vn, P)[0:nt, h, :], start=True, stop=True)
                        m.then_inc(s_gS, 1)
                    pe.wait_ge(s_goq, n + 1)
                    mm(ps[:, 7, 0:H * nt], onesm[:], sG[:, 0:H * nt], start=True, stop=True).then_inc(s_gos, 1)

                pe.wait_ge(s_mB, 3 * (l + 1))
                pe.wait_ge(s_mA, H * (l + 1))
                for c in range(4):
                    w = take(POS_VO[l] + 2 + c)
                    two_tiles(w, 2 * c, mixT).then_inc(s_chunk, 1)
                ln(4 * l + 1)
                ln(4 * l + 2)
                h_ready(2 * l + 1)
                if l == 0:
                    dense()
                else:
                    for t, (c0, nt) in enumerate(TILES):
                        for k in range(KT):
                            m = mm(ps[0:nt, 6, 8 * t:8 * t + 8], hT[:, k, c0:c0 + nt], wr[:, k, :], start=(k == 0), stop=(k == KT - 1))
                    m.then_inc(s_rt, 1)
                    for t, (c0, nt) in enumerate(TILES):
                        for k in range(KT):
                            m = tr(ps[0:nt, 2 * t + k // 4, (k % 4) * P:(k % 4 + 1) * P], hT[:, k, c0:c0 + nt], ident)
                    m.then_inc(s_hrT, 1)
                    pe.wait_ge(s_sel, 1)
                    for t, (c0, nt) in enumerate(TILES):
                        for u in range(t + 1):
                            nu = TILES[u][1]
                            mm(ps[0:nt, 7, 8 * t:8 * t + 8], onesm[0:nu, 0:nt] if u < t else tri[0:nt, 0:nt], route[0:nu, 0, u, 0:NE],
                               start=(u == 0), stop=(u == t))
                    for u, (c0, nu) in enumerate(TILES):
                        m = mm(ps[:, 7, 24:32], onesm[0:nu, :], route[0:nu, 0, u, 0:NE], start=(u == 0), stop=(u == 2))
                    m.then_inc(s_pos, 1)
                    pe.wait_ge(s_hr, 3)
                    pe.wait_ge(s_route, 1)
                    with pe.Fori(0, NE) as e:
                        c = pe.value_load(cls[0:1, bass.ds(e, 1)], min_val=0, max_val=2)
                        with pe.If(c < 1):
                            expert(e, *CLASSES[0])
                        with pe.Else():
                            with pe.If(c < 2):
                                expert(e, *CLASSES[1])
                            with pe.Else():
                                expert(e, *CLASSES[2])
                ln(4 * l + 3)
            pe.wait_ge(s_lnin, KT * 8 + KT)
            for t, (c0, nt) in enumerate(TILES):
                for k in range(KT):
                    m = tr(ps[0:nt, 2 * t + k // 4, (k % 4) * P:(k % 4 + 1) * P], xT[:, k, c0:c0 + nt], ident)
                m.then_inc(s_yT, 1)

        @block.scalar
        def _(act):
            A = nc.scalar.activation
            link = Chain(act, s_ca)

            def ln_stats(n):
                for p in range(4):
                    act.wait_ge(s_xc, 4 * n + p + 1)
                    A(sq[:, 2 * p:2 * p + 2, :], xc[:, 2 * p:2 * p + 2, :], ACT.Square).then_inc(s_sq, 1)
                act.wait_ge(s_var, n + 1)
                link(A(lnv[:], ps[:, 1, 0:NTOK], ACT.Ln, bias=cols[:, 0:1]))
                A(rstd[:, 0, :], lnv[:], ACT.Exp, scale=-0.5).then_inc(s_rstd, 1)

            def ln_mod(n, l, half):
                ln_stats(n)
                for k in range(KT):
                    act.wait_ge(s_xn, 4 * n + k // 2 + 1)
                    A(hT[:, k, 0:SEQ], xc[:, k, 0:SEQ], ACT.Identity, scale=mod[:, l, 24 * half + 8 + k, 0:1],
                      bias=mod[:, l, 24 * half + k, 0:1]).then_inc(s_h, 1)

            def ln_post(n, l, half):
                ln_stats(n)
                for k in range(KT):
                    act.wait_ge(s_xn, 4 * n + k // 2 + 1)
                    c = 32 * half + 8 * l + k
                    A(xT[:, k, :], xc[:, k, :], ACT.Identity, scale=vecT[:, 2, c:c + 1],
                      bias=vecT[:, 2, c + 16:c + 17]).then_inc(s_lnin, 1)

            def rinv(out, psum, scale, bias, last):
                act.wait_ge(*last)
                link(A(lnv[:, 0:psum.shape[-1]], psum, ACT.Ln, scale=scale, bias=cols[:, 1:2]))
                return A(out, lnv[:, 0:psum.shape[-1]], ACT.Exp, scale=-0.5, **({"bias": bias} if bias is not None else {}))

            act.wait_ge(s_vecT, 1)
            act.wait_ge(s_ones, 8)
            cps = ps[:, 0, 3 * P:3 * P + 72]
            A(vecT[:, 0, 0:100], ps[:, 0, 0:100], ACT.Copy).then_inc(s_vec, 1)
            A(vecT[:, 1, 0:96], ps[:, 0, P:P + 96], ACT.Copy).then_inc(s_vec, 1)
            A(vecT[:, 2, 0:64], ps[:, 0, 2 * P:2 * P + 64], ACT.Copy).then_inc(s_vec, 1)
            link(A(siluC[:, :, 0:1], cps[:, 0:8].rearrange("p (k o) -> p k o", o=1), ACT.Silu))
            A(siluC[:, :, 1:9], cps[:, 8:72].rearrange("p (s k) -> p k s", k=8), ACT.Silu).then_inc(s_silc, 1)

            def mod_rows(i):
                for c in range(RING):
                    n = i * RING + c
                    act.wait_ge(s_chunk, n + 1)
                    if c >= 2 or not isinstance(i, int):
                        act.wait_ge(s_adT, n - 1)
                    A(kst[:, c % 2, 0:CH], ps[:, 6 + c % 2, 0:CH], ACT.Copy).then_inc(s_adE, 1)

            mod_rows(0)
            with act.Fori(1, DEPTH * ADA_CH // RING) as i:
                mod_rows(i)

            for l in range(DEPTH):
                act.wait_ge(s_mod, 2 * (l + 1))
                act.wait_ge(s_vec, 3)
                act.wait_ge(s_lam, 3 * l + 1)
                A(lamw[:, 2:4], lamw[:, 0:2], ACT.Exp).then_inc(s_lam, 1)
                ln_mod(4 * l, l, 0)
                for c in range(N_WIN):
                    act.wait_ge(s_chunk, POS_WIN[l] + c + 1)
                    b = 2 * (c % 4)
                    if c < 4:
                        A(pA[:, 2 * c:2 * c + 2, :], ps[:, b:b + 2, 0:NTOK], ACT.Copy,
                          scale=DQK ** -0.5 if c < 2 else 1.0).then_inc(s_pev, 1)
                    elif c < 10:
                        f = 2 * (c - 4)
                        A(pB[:, f:f + 2, 3:3 + SEQ], ps[:, b:b + 2, 0:SEQ], ACT.Copy)
                        A(pBs[:, f:f + 2, :, 3:11], ps[:, b:b + 2, SEQ:NTOK].rearrange("p a (s r) -> p a s r", r=8),
                          ACT.Copy).then_inc(s_pev, 1)
                    else:
                        f = 8 + 2 * (c - 10)
                        A(pA[:, f:f + 2, :], ps[:, b:b + 2, 0:NTOK], ACT.Silu).then_inc(s_pev, 1)
                act.wait_ge(s_histT, l + 1)
                act.wait_ge(s_pev, N_WIN * (l + 1))
                A(pBs[:, :, :, 0:3], ps[:, 7, 0:288].rearrange("p (f s r) -> p f s r", f=12, r=3), ACT.Copy).then_inc(s_histc, 1)
                A(tail[:, :, 0:3], pB[:, :, SEQ:SEQ + 3], ACT.Copy)
                A(tail[:, :, 3:27].rearrange("p f (s r) -> p f s r", r=3), pBs[:, :, :, 8:11], ACT.Copy).then_inc(s_tail, 1)
                for f in range(12):
                    act.wait_ge(s_conv, 12 * l + f + 1)
                    A(pB[:, f, 0:NTOK], ctmp[:, f % 2, :], ACT.Silu).then_inc(s_csil, 1)
                act.wait_ge(s_csil, 12 * (l + 1))
                for f in range(9):
                    if f < 8:
                        if f >= 2:
                            act.wait_ge(s_l2s, 8 * l + f - 1)
                        A(ctmp[:, f % 2, :], pB[:, f, 0:NTOK], ACT.Square).then_inc(s_l2q, 1)
                    if f >= 1:
                        g = f - 1
                        act.wait_ge(s_l2s, 8 * l + g + 1)
                        if g >= 2:
                            act.wait_ge(s_l2d, 8 * l + g - 1)
                        rinv(rstd[:, g % 2, :], ps[:, 6 + g % 2, 0:NTOK], 1.0, cols[:, 2:3] if g < 4 else None, (s_l2r, 8 * l + g)).then_inc(s_l2r, 1)
                act.wait_ge(s_btd, l + 1)
                link(A(small[:, 48:60], small[:, 48:60], ACT.Exp, scale=-1.0))
                link(A(small[:, 48:60], small[:, 48:60], ACT.Ln, bias=cols[:, 3:4]))
                link(A(small[:, 60:64], adt[:, 0, l, :], ACT.Exp))
                A(small[:, 36:48].rearrange("p (t e) -> p t e", e=4), small[:, 0:24].rearrange("p (t e) -> p t e", e=8)[:, :, 0:4], ACT.Exp, scale=-1.0).then_inc(s_bta, 1)

                for u in range(8):
                    h, qt = u // 2, u % 2
                    nk = P * (qt + 1)
                    act.wait_ge(s_pM, 8 * l + u + 1)
                    for m_ in range(2):
                        m = A(scb[:, u % 2, 512 * m_:512 * m_ + nk], scb[:, u % 2, 512 * m_:512 * m_ + nk], ACT.Exp,
                              bias=small[:, 100 + 4 * (u % 2) + m_:101 + 4 * (u % 2) + m_],
                              accum_out=small[:, 102 + 4 * (u % 2) + m_:103 + 4 * (u % 2) + m_])
                        if m_ == 0:
                            link(m)
                    m.then_inc(s_pE, 1)
                    act.wait_ge(s_pT, 8 * l + u + 1)
                    if u >= 2:
                        act.wait_ge(s_pV, 8 * l + u - 1)
                    A(ptr[:, u % 2, 0:nk], ps[:, 4, 0:nk], ACT.Copy).then_inc(s_pTc, 1)
                    act.wait_ge(s_pV, 8 * l + u + 1)
                    A(oA[:, h, qt * P:(qt + 1) * P], ps[:, 5 + u % 2, 0:P], ACT.Copy).then_inc(s_pO, 1)

                act.wait_ge(s_qbz, l + 1)

                def pair_q(i):
                    if l or not (isinstance(i, int) and i == 0):
                        act.wait_ge(s_sS, NPAIR * l + i)
                    for a in range(2):
                        for m_ in range(2):
                            r = slice(64 * m_, 64 * m_ + 64)
                            m = A(qbd[r, a, :, 16 * a + 8 * m_:16 * a + 8 * m_ + 8],
                                  pA[r, 0:H, bass.ds(SEQ + a * DSEQ + i * (2 * DSEQ), DSEQ)], ACT.Copy)
                    m.then_inc(s_qb, 1)

                def pair_k(i, ns):
                    g = NPAIR * l + i
                    for n in ns:
                        act.wait_ge(s_kt, 16 * g + n + 1)
                        if not (l == 0 and isinstance(i, int) and i == 0 and n < 2):
                            act.wait_ge(s_kmm, 16 * g + n - 1)
                        A(ktb[:, n % 2, :], ps[:, n % 2, :], ACT.Copy).then_inc(s_ktA, 1)

                def pair_exp(i):
                    act.wait_ge(s_sM, NPAIR * l + i + 1)
                    A(scb[:, 0, :], scb[:, 0, :], ACT.Exp, bias=small[:, 108:109], accum_out=small[:, 110:111]).then_inc(s_sE, 1)

                def pair_out(i):
                    g = NPAIR * l + i
                    act.wait_ge(s_sT, g + 1)
                    if l or not (isinstance(i, int) and i == 0):
                        act.wait_ge(s_sV, 2 * g)
                    A(ptb[:, 0:4, :], ps[:, 5, :].rearrange("p (a n) -> p a n", a=4), ACT.Copy).then_inc(s_sTc, 1)
                    for a in range(2):
                        act.wait_ge(s_sV, 2 * g + a + 1)
                        A(ob[:, a, :], ps[:, 7 - 2 * a, 0:P], ACT.Copy).then_inc(s_ob, 1)
                    act.wait_ge(s_oT, g + 1)
                    A(oA[:, :, bass.ds(SEQ + i * (2 * DSEQ), 2 * DSEQ)].rearrange("p h (a t) -> p h a t", a=2),
                      ps[:, 6, 0:64].rearrange("p (a h t) -> p h a t", a=2, h=H), ACT.Copy).then_inc(s_sO, 1)

                def pair(i):
                    pair_q(i + 1)
                    pair_k(i + 1, range(0, 3))
                    pair_exp(i)
                    pair_k(i + 1, range(3, 2 * NPG))
                    pair_out(i)

                pair_q(0)
                pair_k(0, range(2 * NPG))
                pair(0)
                with act.Fori(1, NPAIR - 1) as i:
                    pair(i)
                pair_exp(NPAIR - 1)
                pair_out(NPAIR - 1)

                act.wait_ge(s_sO, NPAIR * (l + 1))
                act.wait_ge(s_l2d, 8 * (l + 1))
                for h in range(H + 1):
                    if h < H:
                        if h >= 2:
                            act.wait_ge(s_os, H * l + h - 1)
                        A(ctmp[:, h % 2, :], oA[:, h, :], ACT.Square).then_inc(s_oq, 1)
                    if h >= 1:
                        g = h - 1
                        act.wait_ge(s_os, H * l + g + 1)
                        if g >= 2:
                            act.wait_ge(s_mA, H * l + g - 1)
                        rinv(rstd[:, g % 2, :], ps[:, g % 2, 0:NTOK], 1.0 / P, None, (s_or, H * l + g)).then_inc(s_or, 1)

                for T, (c0, nt) in enumerate(TILES):
                    n = 3 * l + T
                    smp = T == 2
                    act.wait_ge(s_gG, n + 1)
                    act.wait_ge(s_gGc, n + 1)
                    act.wait_ge(s_mA, H * (l + 1))
                    link(A(c3(Gb_e, nt), c3(ps[:, 1, :], nt), ACT.Exp))
                    link(A(c3(DT, nt)[0:nt], c3(DT, nt)[0:nt], ACT.Exp))
                    A(small[0:nt, 120:124], small[0:nt, 120:124], ACT.Exp).then_inc(s_gE, 1)
                    act.wait_ge(s_gE, n + 1)
                    act.wait_ge(s_gK, n + 1)
                    for h in range(H):
                        m = A(c3(kd, P)[0:nt, h, :], ps[0:nt, 5, h * P:(h + 1) * P], ACT.Copy, scale=small[0:nt, 120 + h:121 + h])
                    m.then_inc(s_gkd, 1)
                    for v in range(3 if smp else 7):
                        i0 = 17 * l + 7 * T + v
                        act.wait_ge(s_g1, i0 + 1)
                        A(c3(PP, nt)[0:nt], c3(ps[0:nt, 6, :], nt), ACT.Copy).then_inc(s_g1c, 1)
                    act.wait_ge(s_gRt, n + 1)
                    A(rr[0:nt, :], ps[0:nt, 2, :], ACT.Copy).then_inc(s_gr, 1)
                    act.wait_ge(s_gV, n + 1)
                    A(vn[0:nt, :], ps[0:nt, 3, :], ACT.Copy).then_inc(s_gv, 1)
                    act.wait_ge(s_gO, n + 1)
                    link(A(c3(oG, nt), c3(ps[:, 4, :], nt), ACT.Copy))
                    A(sG[:, 0:H * nt].rearrange("p (h t) -> p h t", h=H), c3(oG, nt), ACT.Square).then_inc(s_goq, 1)
                    act.wait_ge(s_gos, n + 1)
                    link(A(sG[:, 0:H * nt], ps[:, 7, 0:H * nt], ACT.Ln, scale=1.0 / P, bias=cols[:, 1:2]))
                    A(sG[:, 0:H * nt], sG[:, 0:H * nt], ACT.Exp, scale=-0.5).then_inc(s_gor, 1)

                ln_post(4 * l + 1, l, 0)
                ln_mod(4 * l + 2, l, 1)

                def silu(pos, e, n0, n, first):
                    for j in range(UP):
                        act.wait_ge(s_chunk, pos + 2 * j + 1 + e * MLP_POS)
                        if j >= 2 or not first:
                            act.wait_ge(s_ff, n0 + j - 1)
                        A(sil[:, j % 2, :, 0:n], ps[:, 4 * (j % 2):4 * (j % 2) + 2, 0:n], ACT.Silu).then_inc(s_sil, 1)

                def expert(e, slots, rows):
                    for k in range(KT):
                        act.wait_ge(s_xeT, e * KT + k + 1)
                        A(Xe[:, k, 0:slots], ps[:, 4 + k % 4, 0:slots], ACT.Copy).then_inc(s_xe, 1)
                    silu(POS_MLP[1], e, UP + e * UP, slots, False)

                act.wait_ge(s_out, 16 * (8 * l + 6))
                if l == 0:
                    silu(POS_MLP[0], 0, 0, NTOK, True)
                else:
                    act.wait_ge(s_out, 16 * 8 * DEPTH)
                    act.wait_ge(s_hrT, 1)
                    for t, (c0, nt) in enumerate(TILES):
                        A(hrow[0:nt, t, :].rearrange("p (a n) -> p a n", a=2), ps[0:nt, 2 * t:2 * t + 2, :], ACT.Copy).then_inc(s_hr, 1)
                    act.wait_ge(s_rtm, 1)
                    A(small[:, 72:96], small[:, 72:96], ACT.Exp).then_inc(s_rte, 1)
                    act.wait_ge(s_route, 1)
                    with act.Fori(0, NE) as e:
                        c = act.value_load(cls[0:1, bass.ds(e, 1)], min_val=0, max_val=2)
                        with act.If(c < 1):
                            expert(e, *CLASSES[0])
                        with act.Else():
                            with act.If(c < 2):
                                expert(e, *CLASSES[1])
                            with act.Else():
                                expert(e, *CLASSES[2])
                ln_post(4 * l + 3, l, 1)
            for t, (c0, nt) in enumerate(TILES):
                act.wait_ge(s_yT, t + 1)
                A(yrow[0:nt, t, :].rearrange("p (a n) -> p a n", a=2), ps[0:nt, 2 * t:2 * t + 2, :], ACT.Copy).then_inc(s_y, 1)

        @block.vector
        def _(dve):
            V = nc.vector
            link = Chain(dve, s_cd)

            def ln(n):
                dve.wait_ge(s_mean, n + 1)
                for p in range(4):
                    V.tensor_tensor(xc[:, 2 * p:2 * p + 2, :], xT[:, 2 * p:2 * p + 2, :],
                                    ps[:, 0:1, 0:NTOK].to_broadcast([P, 2, NTOK]), ALU.subtract).then_inc(s_xc, 1)
                dve.wait_ge(s_rstd, n + 1)
                for p in range(4):
                    V.tensor_tensor(xc[:, 2 * p:2 * p + 2, :], xc[:, 2 * p:2 * p + 2, :],
                                    rstd[:, 0:1, :].to_broadcast([P, 2, NTOK]), ALU.mult).then_inc(s_xn, 1)

            def seqs(t):
                return t.rearrange("p k (s r) -> p k s r", r=DSEQ)

            def per_seq(l, f0, nf):
                m = mod[:, l, f0:f0 + nf, 1:9].rearrange("p k (s o) -> p k s o", o=1)
                return m.to_broadcast([P, nf, NSEQ, DSEQ])

            def ln_mod(n, l, half):
                ln(n)
                dve.wait_ge(s_xn, 4 * (n + 1))
                link(V.tensor_tensor(seqs(hT[:, :, SEQ:]), seqs(xc[:, :, SEQ:]), per_seq(l, 24 * half + 8, 8), ALU.mult))
                V.tensor_tensor(seqs(hT[:, :, SEQ:]), seqs(hT[:, :, SEQ:]), per_seq(l, 24 * half, 8), ALU.add).then_inc(s_hs, 1)
                V.tensor_scalar(xT[:], xT[:], ALPHA, None, ALU.mult).then_inc(s_xa, 1)

            def residual(src, k0, l, half):
                g0 = 24 * half + 16 + k0
                for o in range(2):
                    V.scalar_tensor_tensor(out=xT[:, k0 + o, 0:SEQ], in0=src[:, o, 0:SEQ], scalar=mod[:, l, g0 + o, 0:1],
                                           in1=xT[:, k0 + o, 0:SEQ], op0=ALU.mult, op1=ALU.add)
                t = seqs(ctmp[:, :, 0:NS])
                dve.wait_ge(s_lnin, KT * (4 * l + 2 * half + 1) + k0)
                link(V.tensor_tensor(t, seqs(src[:, :, SEQ:NTOK]), per_seq(l, g0, 2), ALU.mult))
                V.tensor_tensor(xT[:, k0:k0 + 2, SEQ:], xT[:, k0:k0 + 2, SEQ:], ctmp[:, :, 0:NS], ALU.add).then_inc(s_lnin, 2)

            for k in range(KT):
                dve.wait_ge(s_xt, k + 1)
                V.tensor_copy(xT[:, k, :], ps[:, 1 + k % 4, 0:NTOK]).then_inc(s_lnin, 1)
            dve.wait_ge(s_vec, 3)
            for l in range(DEPTH):
                with dve.Fori(0, ADA_CH // RING) as i:
                    for c in range(RING):
                        dve.wait_ge(s_adT, ADA_CH * l + c + 1 + i * RING)
                        b = vecT[:, 0, bass.ds(48 * l + 2 * c + i * (2 * RING), 2)].rearrange("p (a o) -> p a o", o=1)
                        V.tensor_tensor(mod[:, l, bass.ds(2 * c + i * (2 * RING), 2), :],
                                        ps[:, 5 * (c % 2), 0:32].rearrange("p (a n) -> p a n", a=2)[:, :, 0:9],
                                        b.to_broadcast([P, 2, 9]), ALU.add).then_inc(s_modev, 1)
                dve.wait_ge(s_modev, ADA_CH * (l + 1))
                for half in range(2):
                    f = 24 * half + 8
                    V.tensor_scalar(mod[:, l, f:f + 8, :], mod[:, l, f:f + 8, :], 1.0, None, ALU.add).then_inc(s_mod, 1)

            for l in range(DEPTH):
                for a in range(2):
                    link(V.tensor_tensor(ctmp[:, 0, 0:64], lamb[:, l, 128 * a:128 * a + 64], lamb[:, l, 128 * a + 64:128 * a + 128], ALU.mult))
                    m = V.tensor_reduce(lamw[:, a:a + 1], ctmp[:, 0, 0:64], AX.X, ALU.add)
                    if a == 0:
                        link(m)
                m.then_inc(s_lam, 1)
                dve.wait_ge(s_lam, 3 * l + 2)
                link(V.tensor_tensor(lamw[:, 4:5], lamw[:, 3:4], lamw[:, 2:3], ALU.subtract))
                link(V.tensor_scalar(lamc[:, l, 0:1], lamw[:, 4:5], -LAM_INIT[l], None, ALU.add))
                link(V.scalar_tensor_tensor(out=lamc[:, l, 1:2], in0=C[:, C_ROW + 2:C_ROW + 3], scalar=lamc[:, l, 0:1],
                                            in1=C[:, C_ROW + 1:C_ROW + 2], op0=ALU.mult, op1=ALU.add))
                V.tensor_scalar(lamw[:, 5:6], vecT[:, 0, 96 + l:97 + l], 1.0 - LAM_INIT[l], None, ALU.mult).then_inc(s_lam, 1)
                dve.wait_ge(s_lam, 3 * l + 3)
                dve.wait_ge(s_mod, 2 * (l + 1))
                ln_mod(4 * l, l, 0)

                dve.wait_ge(s_ba, l + 1)
                link(V.tensor_copy(small[:, 0:16], ps[:, 6, 0:16]))
                V.tensor_copy(small[0:NS, 16:24], ps[0:NS, 6, 16:24]).then_inc(s_bae, 1)
                dve.wait_ge(s_bae, l + 1)
                ba = small[:, 0:24].rearrange("p (t e) -> p t e", e=8)
                u = small[:, 24:36].rearrange("p (t e) -> p t e", e=4)
                t3 = lambda a: small[:, a:a + 12].rearrange("p (t e) -> p t e", e=4)
                bc3 = lambda t: t.rearrange("p (o e) -> p o e", o=1).to_broadcast([P, 3, H])
                link(V.tensor_tensor(u, ba[:, :, 4:8], bc3(adt[:, 1, l, :]), ALU.add))
                V.scalar_tensor_tensor(out=small[:, 48:60], in0=small[:, 24:36], scalar=-1.0, in1=small[:, 24:36],
                                       op0=ALU.mult, op1=ALU.max).then_inc(s_btd, 1)
                for c in range(2):
                    dve.wait_ge(s_chunk, POS_VO[l] + c + 1)
                    for t, (c0, nt) in enumerate(TILES):
                        m = V.tensor_copy(va[0:nt, t, CH * c:CH * (c + 1)], ps[0:nt, 3 * c + t, 0:CH])
                        if t < 2:
                            link(m)
                    m.then_inc(s_va, 1)
                dve.wait_ge(s_kT, l + 1)
                if l:
                    dve.wait_ge(s_ff, UP * l)
                link(V.tensor_copy(kst[:, 0:2, :], ps[:, 0:2, :]))
                V.tensor_copy(kst[0:NS, 2, :], ps[0:NS, 2, :]).then_inc(s_kst, 1)
                dve.wait_ge(s_tailT, l + 1)
                dve.wait_ge(s_histT, l + 1)
                V.tensor_copy(rowb[0:27, :].rearrange("p (a n) -> p a n", a=3), ps[0:27, 3:6, :]).then_inc(s_tailc, 1)
                dve.wait_ge(s_histc, l + 1)
                dve.wait_ge(s_tail, l + 1)
                link(V.memset(pB[:, :, 0:3], 0.0))
                for f in range(12):
                    if f >= 2:
                        dve.wait_ge(s_csil, 12 * l + f - 1)
                    smp = pB[:, f, 3 + SEQ:3 + SEQ + 88].rearrange("p (s r) -> p s r", r=11)
                    out_s = ctmp[:, f % 2, SEQ:].rearrange("p (s r) -> p s r", r=DSEQ)
                    out_p = ctmp[:, f % 2, 0:SEQ]
                    wc = lambda i: vecT[:, 1, 48 * l + 12 * i + f:48 * l + 12 * i + f + 1]
                    V.tensor_scalar(out_p, pB[:, f, 0:SEQ], wc(0), None, ALU.mult)
                    link(V.tensor_scalar(out_s, smp[:, :, 0:DSEQ], wc(0), None, ALU.mult))
                    for i in range(1, CW):
                        m = V.scalar_tensor_tensor(out=out_p, in0=pB[:, f, i:i + SEQ], scalar=wc(i), in1=out_p, op0=ALU.mult, op1=ALU.add)
                        m = V.scalar_tensor_tensor(out=out_s, in0=smp[:, :, i:i + DSEQ], scalar=wc(i), in1=out_s, op0=ALU.mult, op1=ALU.add)
                        if i < CW - 1:
                            link(m)
                    m.then_inc(s_conv, 1)
                for f in range(8):
                    dve.wait_ge(s_l2r, 8 * l + f + 1)
                    V.tensor_tensor(pB[:, f, 0:NTOK], pB[:, f, 0:NTOK], rstd[:, f % 2, :], ALU.mult).then_inc(s_l2d, 1)
                dve.wait_ge(s_bta, l + 1)
                link(V.tensor_scalar(small[:, 36:48], small[:, 36:48], 1.0, None, ALU.add))
                link(V.reciprocal(small[:, 36:48], small[:, 36:48]))
                link(V.scalar_tensor_tensor(out=small[:, 24:36], in0=small[:, 24:36], scalar=0.0, in1=small[:, 48:60],
                                            op0=ALU.max, op1=ALU.add))
                link(V.tensor_tensor(u, u, bc3(small[:, 60:64]), ALU.mult))
                V.tensor_scalar(small[:, 24:36], small[:, 24:36], -1.0, None, ALU.mult).then_inc(s_bt, 1)

                def p_max(uu):
                    h, qt = uu // 2, uu % 2
                    nk = P * (qt + 1)
                    dve.wait_ge(s_pS, 8 * l + uu + 1)
                    if uu >= 2:
                        dve.wait_ge(s_pT, 8 * l + uu - 1)
                    for m_ in range(2):
                        m = V.scalar_tensor_tensor(out=scb[:, uu % 2, 512 * m_:512 * m_ + nk], in0=dP[:, qt, 0:nk], scalar=SLOPE[h],
                                                   in1=ps[:, 2 * (uu % 2) + m_, 0:nk], op0=ALU.mult, op1=ALU.add)
                    link(m)
                    V.tensor_reduce(small[:, 100 + 4 * (uu % 2):102 + 4 * (uu % 2)],
                                    scb[:, uu % 2, 0:1024].rearrange("p (a n) -> p a n", a=2)[:, :, 0:nk],
                                    AX.X, ALU.max, negate=True).then_inc(s_pM, 1)

                def p_probs(uu):
                    nk = P * (uu % 2 + 1)
                    b = 102 + 4 * (uu % 2)
                    dve.wait_ge(s_pE, 8 * l + uu + 1)
                    link(V.reciprocal(small[:, b:b + 2], small[:, b:b + 2]))
                    link(V.tensor_scalar(small[:, b + 1:b + 2], small[:, b + 1:b + 2], lamc[:, l, 0:1], None, ALU.mult))
                    p1, p2 = scb[:, uu % 2, 0:nk], scb[:, uu % 2, 512:512 + nk]
                    link(V.tensor_scalar(p1, p1, small[:, b:b + 1], None, ALU.mult))
                    V.scalar_tensor_tensor(out=p1, in0=p2, scalar=small[:, b + 1:b + 2], in1=p1, op0=ALU.mult, op1=ALU.add).then_inc(s_pA, 1)

                p_max(0)
                for uu in range(8):
                    if uu + 1 < 8:
                        p_max(uu + 1)
                    p_probs(uu)

                def pair(i):
                    g = NPAIR * l + i
                    dve.wait_ge(s_sS, g + 1)
                    if l or not (isinstance(i, int) and i == 0):
                        dve.wait_ge(s_sT, g)
                    V.scalar_tensor_tensor(out=scb[:, 0, 0:PAST], in0=dS[:], scalar=C[:, C_ROW:C_ROW + 1],
                                           in1=ps[:, 2:4, :].rearrange("p a n -> p (a n)"), op0=ALU.mult, op1=ALU.add)
                    link(V.scalar_tensor_tensor(out=scb[:, 0, PAST:PAST + NS], in0=dN[:, bass.ds(i, 1), :].rearrange("p o n -> p (o n)"),
                                                scalar=C[:, C_ROW:C_ROW + 1], in1=ps[:, 4, 0:NS], op0=ALU.mult, op1=ALU.add))
                    V.tensor_reduce(small[:, 108:109], scb[:, 0, :], AX.X, ALU.max, negate=True).then_inc(s_sM, 1)
                    dve.wait_ge(s_sE, g + 1)
                    link(V.reciprocal(small[:, 110:111], small[:, 110:111]))
                    V.tensor_scalar(scb[:, 0, :], scb[:, 0, :], small[:, 110:111], lamc[:, l, 1:2], ALU.mult, ALU.mult).then_inc(s_sP, 1)
                    dve.wait_ge(s_sT, g + 1)
                    if l or not (isinstance(i, int) and i == 0):
                        dve.wait_ge(s_sV, 2 * g)
                    V.tensor_copy(ptb[0:64, 8, :], ps[0:64, 4, P:2 * P])
                    V.tensor_copy(ptb[:, 4:8, :], ps[:, 6, :].rearrange("p (a n) -> p a n", a=4)).then_inc(s_sTd, 1)

                DVE_PAIR = 2
                pair(0)
                with dve.Fori(1, NPAIR) as i:
                    link.loop(i - 1, DVE_PAIR)
                    pair(i)
                link.done(DVE_PAIR, NPAIR - 1)

                dve.wait_ge(s_out, 16 * (8 * l + 6))
                for h in range(H):
                    dve.wait_ge(s_or, H * l + h + 1)
                    V.scalar_tensor_tensor(out=mixT[:, h, :], in0=oA[:, h, :], scalar=lamw[:, 5:6], in1=rstd[:, h % 2, :],
                                           op0=ALU.mult, op1=ALU.mult).then_inc(s_mA, 1)

                dve.wait_ge(s_mA, H * (l + 1))
                if l > 0:
                    dve.wait_ge(s_out, 16 * 8 * l)
                V.memset(Sp[:], 0.0)
                for T, (c0, nt) in enumerate(TILES):
                    n = 3 * l + T
                    smp = T == 2
                    lev = 3 if smp else 7
                    mask = (C[0:nt, C_TRIS:C_TRIS + nt] if smp else tri).rearrange("p (o t) -> p o t", o=1).to_broadcast([nt, H, nt])
                    dve.wait_ge(s_gG, n + 1)
                    link(V.tensor_copy(small[0:nt, 112:120], ps[0:nt, 0, 0:8]))
                    V.tensor_copy(c3(bbs, nt), c3(ps[:, 2, :], nt))
                    for h in range(H):
                        V.tensor_scalar(c3(DT, nt)[0:nt, h, :], ps[0:nt, 1, h * P:h * P + nt], small[0:nt, 112 + h:113 + h], 0.0,
                                        ALU.subtract, ALU.min)
                    V.tensor_tensor(small[0:nt, 120:124], small[0:nt, 116:120], small[0:nt, 112:116], ALU.subtract).then_inc(s_gGc, 1)
                    dve.wait_ge(s_gE, n + 1)
                    V.tensor_tensor(c3(qd, nt), pB[:, 0:4, c0:c0 + nt], c3(Gb_e, nt), ALU.mult)
                    link(V.tensor_tensor(c3(DT, nt)[0:nt], c3(DT, nt)[0:nt], mask, ALU.mult))
                    dve.wait_ge(s_gK, n + 1)
                    V.tensor_tensor(c3(QK, nt)[0:nt], c3(ps[0:nt, 4, :], nt), c3(DT, nt)[0:nt], ALU.mult)
                    link(V.tensor_tensor(c3(LT, nt)[0:nt], c3(ps[0:nt, 3, :], nt), c3(DT, nt)[0:nt], ALU.mult))
                    idb = ident[0:nt, 0:nt].rearrange("p (o t) -> p o t", o=1).to_broadcast([nt, H, nt])
                    V.tensor_copy(c3(X, nt)[0:nt], idb)
                    V.tensor_copy(c3(XT, nt)[0:nt], idb)
                    link(V.tensor_tensor(c3(LT, nt)[0:nt], c3(LT, nt)[0:nt], c3(bbs, nt)[0:nt], ALU.mult))
                    for v in range(lev):
                        i0 = 17 * l + 7 * T + v
                        lm = C[0:nt, C_LEV + v * P:C_LEV + v * P + nt].rearrange("p (o t) -> p o t", o=1).to_broadcast([nt, H, nt])
                        V.tensor_tensor(c3(LM, nt)[0:nt], c3(LT, nt)[0:nt], lm, ALU.mult).then_inc(s_lm, 1)
                        dve.wait_ge(s_g2, i0 + 1)
                        V.tensor_tensor(c3(X, nt)[0:nt], c3(X, nt)[0:nt], c3(ps[0:nt, 7, :], nt), ALU.subtract)
                        V.tensor_tensor(c3(XT, nt)[0:nt], c3(XT, nt)[0:nt], c3(ps[0:nt, 0, :], nt), ALU.subtract).then_inc(s_g2c, 1)
                    dve.wait_ge(s_gR, n + 1)
                    link(V.tensor_tensor(c3(rT, nt), c3(ps[:, 1, :], nt), c3(Gb_e, nt), ALU.mult))
                    link(V.tensor_tensor(c3(rT, nt), pB[:, 8:12, c0:c0 + nt], c3(rT, nt), ALU.subtract))
                    V.tensor_tensor(c3(rT, nt), c3(rT, nt), c3(bbs, nt), ALU.mult).then_inc(s_gRc, 1)
                    if smp:
                        dve.wait_ge(s_gO, n + 1)
                        dve.wait_ge(s_gkd, n + 1)
                        for h in range(H):
                            if h > 0:
                                dve.wait_ge(s_gS, 6 * l + 2 + h)
                            for half in range(2):
                                m = V.tensor_tensor(kdm[half][0:nt, :].rearrange("p (s k) -> p s k", s=4),
                                                    c3(kd, P)[0:nt, h:h + 1, :].to_broadcast([nt, 4, P]),
                                                    C[0:nt, C_SEQM + 4 * half:C_SEQM + 4 * half + 4].rearrange("p (s o) -> p s o", o=1).to_broadcast([nt, 4, P]),
                                                    ALU.mult)
                            m.then_inc(s_gkm, 1)
                            dve.wait_ge(s_gS, 6 * l + 3 + h)
                            for s in range(NSEQ):
                                V.scalar_tensor_tensor(out=Ss[:, s, h, :], in0=Ss[:, s, h, :], scalar=c3(Gb_e, nt)[:, h, 8 * s + 7:8 * s + 8],
                                                       in1=ps[:, 5 + s // 4, (s % 4) * P:(s % 4 + 1) * P], op0=ALU.mult, op1=ALU.add
                                                       ).then_inc(s_gSc, 1)
                    else:
                        dve.wait_ge(s_gS, 6 * l + T + 1)
                        for h in range(H):
                            m = V.scalar_tensor_tensor(out=Sp[:, h, :], in0=Sp[:, h, :], scalar=c3(Gb_e, nt)[:, h, nt - 1:nt],
                                                       in1=ps[:, 5, h * P:(h + 1) * P], op0=ALU.mult, op1=ALU.add)
                        m.then_inc(s_gSc, 1)
                    dve.wait_ge(s_gor, n + 1)
                    g3 = sG[:, 0:H * nt].rearrange("p (h t) -> p h t", h=H)
                    link(V.tensor_tensor(c3(oG, nt), c3(oG, nt), g3, ALU.mult))
                    V.scalar_tensor_tensor(out=mixT[:, 4:8, c0:c0 + nt], in0=c3(oG, nt), scalar=vecT[:, 0, 98 + l:99 + l],
                                           in1=pA[:, 8:12, c0:c0 + nt], op0=ALU.mult, op1=ALU.mult).then_inc(s_mB, 1)

                for c in range(4):
                    dve.wait_ge(s_chunk, POS_VO[l] + 2 + c + 1)
                    if c == 0:
                        dve.wait_ge(s_xa, 2 * l + 1)
                    residual(ps[:, 2 * c:2 * c + 2, :], 2 * c, l, 0)
                ln(4 * l + 1)
                ln_mod(4 * l + 2, l, 1)
                dve.wait_ge(s_xa, 2 * l + 2)

                def swiglu(pos, e, n0, n, js):
                    for j in js:
                        dve.wait_ge(s_sil, n0 + j + 1)
                        dve.wait_ge(s_chunk, pos + 2 * j + 2 + e * MLP_POS)
                        b = 4 * (j % 2) + 2
                        V.tensor_tensor(ff[:, 2 * j:2 * j + 2, 0:n], sil[:, j % 2, :, 0:n], ps[:, b:b + 2, 0:n], ALU.mult).then_inc(s_ff, 1)

                def select(e):
                    col = lambda what, t, nt: route[0:nt, what, t, bass.ds(e, 1)]
                    for t, (c0, nt) in enumerate(TILES):
                        V.tensor_scalar(Sel[0:nt, t, :], C[0:nt, C_IOTA:C_IOTA + NTOK], col(2, t, nt), col(0, t, nt), ALU.is_equal, ALU.mult)
                        m = V.tensor_scalar(SelG[0:nt, t, :], C[0:nt, C_IOTA:C_IOTA + NTOK], col(2, t, nt), col(1, t, nt), ALU.is_equal, ALU.mult)
                    m.then_inc(s_prep, 1)

                def expert(e, slots, rows):
                    dve.wait_ge(s_gtT, e + 1)
                    for s_, (r0, nr) in enumerate(rows):
                        m = V.tensor_copy(GT[0:nr, s_, :], ps[0:nr, s_, 0:NTOK])
                    m.then_inc(s_gt, 1)
                    dve.wait_ge(s_xeT, e * KT + KT)
                    select(e + 1)
                    swiglu(POS_MLP[1], e, UP + e * UP, slots, range(UP))
                    for d in range(4):
                        dve.wait_ge(s_chunk, POS_MLP[1] + 2 * UP + 3 * d + 3 + e * MLP_POS)
                        for s_, (r0, nr) in enumerate(rows):
                            m = V.tensor_copy(frow[0:nr, s_, CH * d:CH * (d + 1)], ps[0:nr, 3 * (d % 2) + s_, 0:CH])
                        m.then_inc(s_fr, 1)
                    dve.wait_ge(s_fa, KT + e * KT)
                    for k in range(KT):
                        dve.wait_ge(s_cb, e * KT + k + 1)
                        V.tensor_tensor(mixT[:, k, :], mixT[:, k, :], ps[:, 6 + k % 2, 0:NTOK], ALU.add).then_inc(s_fa, 1)

                if l == 0:
                    swiglu(POS_MLP[0], 0, 0, NTOK, range(UP))
                    for d in range(4):
                        dve.wait_ge(s_chunk, POS_MLP[0] + 2 * UP + 3 * d + 3)
                        residual(ps[:, 2 * d:2 * d + 2, :], 2 * d, l, 1)
                else:
                    dve.wait_ge(s_rt, 1)
                    lg = small[:, 72:96].rearrange("p (t e) -> p t e", e=8)
                    V.memset(route[:], 0.0)
                    link(V.memset(small[:, 64:96], 0.0))
                    V.tensor_tensor(lg[:, 0:2, :], ps[:, 6, 0:16].rearrange("p (t e) -> p t e", e=8),
                                    brb[:].rearrange("p (o e) -> p o e", o=1).to_broadcast([P, 2, 8]), ALU.add)
                    link(V.tensor_tensor(small[0:NS, 88:96], ps[0:NS, 6, 16:24], brb[0:NS, :], ALU.add))
                    sel = route[:, 0, :, 0:NE]
                    pw = ctmp[:, 0, 0:64].rearrange("p (i j) -> p i j", i=8)
                    pw2 = ctmp[:, 1, 0:64].rearrange("p (i j) -> p i j", i=8)
                    low = C[:, C_LOW:C_LOW + 64].rearrange("p (i j) -> p i j", i=8)
                    for t in range(3):
                        lj = lg[:, t:t + 1, :].to_broadcast([P, 8, 8])
                        li = small[:, 72 + 8 * t:80 + 8 * t].rearrange("p (i o) -> p i o", o=1).to_broadcast([P, 8, 8])
                        V.tensor_tensor(pw, lj, li, ALU.is_equal)
                        link(V.tensor_tensor(pw2, lj, li, ALU.is_gt))
                        link(V.tensor_tensor(pw, pw, low, ALU.mult))
                        link(V.tensor_tensor(pw, pw, pw2, ALU.add))
                        link(V.tensor_reduce(sel[:, t, :], pw, AX.X, ALU.add))
                    V.tensor_scalar(sel, sel, 2.0, None, ALU.is_lt).then_inc(s_sel, 1)
                    dve.wait_ge(s_sel, 1)
                    link(V.tensor_reduce(small[:, 64:67], lg, AX.X, ALU.max))
                    mx = small[:, 64:67].rearrange("p (t o) -> p t o", o=1).to_broadcast([P, 3, 8])
                    V.tensor_tensor(lg, lg, mx, ALU.subtract).then_inc(s_rtm, 1)
                    dve.wait_ge(s_rte, 1)
                    link(V.tensor_tensor(lg, lg, sel, ALU.mult))
                    link(V.tensor_reduce(small[:, 64:67], lg, AX.X, ALU.add))
                    link(V.reciprocal(small[:, 64:67], small[:, 64:67]))
                    link(V.tensor_tensor(route[:, 1, :, 0:NE], lg, mx, ALU.mult))
                    dve.wait_ge(s_pos, 1)
                    V.tensor_copy(route[:, 2, 0:2, 0:NE], ps[:, 7, 0:16].rearrange("p (t e) -> p t e", e=8))
                    V.tensor_copy(route[0:NS, 2, 2, 0:NE], ps[0:NS, 7, 16:24])
                    link(V.tensor_scalar(small[:, 0:8], ps[:, 7, 24:32], float(CLASSES[0][0]), None, ALU.is_gt))
                    V.tensor_scalar(small[:, 8:16], ps[:, 7, 24:32], float(CLASSES[1][0]), None, ALU.is_gt).then_inc(s_route2, 1)
                    dve.wait_ge(s_route2, 1)
                    V.tensor_tensor(cls[:], small[:, 0:8], small[:, 8:16], ALU.add).then_inc(s_route, 1)
                    dve.wait_ge(s_out, 16 * 8 * DEPTH)
                    select(0)
                    V.memset(mixT[:], 0.0).then_inc(s_fa, KT)
                    dve.wait_ge(s_route, 1)
                    with dve.Fori(0, NE) as e:
                        c = dve.value_load(cls[0:1, bass.ds(e, 1)], min_val=0, max_val=2)
                        with dve.If(c < 1):
                            expert(e, *CLASSES[0])
                        with dve.Else():
                            with dve.If(c < 2):
                                expert(e, *CLASSES[1])
                            with dve.Else():
                                expert(e, *CLASSES[2])
                    dve.wait_ge(s_fa, KT * (NE + 1))
                    for d in range(4):
                        residual(mixT[:, 2 * d:2 * d + 2, :], 2 * d, l, 1)
                ln(4 * l + 3)


_INS = ['x_prompt', 'x_sample', 'cache_k', 'cache_v', 'state_conv', 'state_delta', 'page_table', 'c_prompt', 'c_sample',
        'w_in', 'w_out', 'lam_params', 'subln_a', 'conv_w', 'a_log', 'dt_bias', 'norm_b', 'ada_w', 'ada_b',
        'ln1_g', 'ln1_b', 'ln2_g', 'ln2_b', 'dense_w_up', 'dense_w_down', 'moe_router', 'moe_router_b', 'moe_w_up', 'moe_w_down']
_OUTS = [(1, SEQ, D), (NSEQ, DSEQ, D), (DEPTH, 1, SEQ, H, P), (DEPTH, 1, SEQ, H, P), (DEPTH, 1, 3, 1536), (DEPTH, 1, H, P, P),
         (DEPTH, NSEQ, DSEQ, H, P), (DEPTH, NSEQ, DSEQ, H, P), (DEPTH, NSEQ, 3, 1536), (DEPTH, NSEQ, H, P, P)]


def kernel(**inputs):
    import concourse.bacc as _bacc
    from concourse.bass_utils import run_bass_kernel_spmd as _run

    nc = _bacc.Bacc("TRN2", target_bir_lowering=False, num_devices=1)
    arrays, args = {}, []
    host = [(n, np.ascontiguousarray(inputs[n])) for n in _INS]
    host += list(zip(("table_c", "table_dp", "table_ds", "table_dn"), constant_tables()))
    for name, a in host:
        arrays[f"in_{name}_dram"] = a
        args.append(nc.dram_tensor(f"in_{name}_dram", a.shape, mybir.dt.from_np(a.dtype), kind="ExternalInput").ap())
    for i, shape in enumerate(_OUTS):
        args.append(nc.dram_tensor(f"out_{i}_dram", shape, F32, kind="ExternalOutput").ap())
    trunk_kernel(nc, *args)
    r = _run(nc, [arrays], core_ids=[0])
    return tuple(r.results[0][f"out_{i}_dram"] for i in range(len(_OUTS)))
```

```python
from contextlib import ExitStack
import math

import numpy as np

import concourse.bass as bass
from concourse import mybir

ALU = mybir.AluOpType
ACT = mybir.ActivationFunctionType
AX = mybir.AxisListType
F32 = mybir.dt.float32
I32 = mybir.dt.int32

P = 128
D = 1024
KT = D // P
SEQ = 256
NSEQ = 8
DSEQ = 8
NS = NSEQ * DSEQ
NTOK = SEQ + NS
DEPTH = 2
H = 4
DQK = 64
PAST = 1024
PAGE = 128
NPG = PAST // PAGE
NPOOL = 80
FF = 2816
FT = FF // P
NE = 8
CW = 4
D_IN = 3592
PB = 3 + SEQ + NSEQ * (3 + DSEQ) + 1
ALPHA = (2 * DEPTH) ** 0.25
LN_EPS = 1e-5
NEG = -1e30
LAM_INIT = [0.8 - 0.6 * math.exp(-0.3 * l) for l in range(DEPTH)]
SLOPE = [2.0 ** (-8.0 * (h + 1) / H) for h in range(H)]
LEVELS = [1, 2, 4, 8, 16, 32, 64]
TILES = [(0, 128), (128, 128), (256, 64)]

RING = 6
CH = 256
ADA_CH = 6 * D // CH
WIN_COLS = [0, 256, 512, 768] + [1536 + 256 * j for j in range(6)] + [3080, 3336]
N_WIN = len(WIN_COLS)
N_VO = 6
UP = FF // CH
DN_ROWS = [(0, 8), (8, 8), (16, 6)]
MLP_CH = 2 * UP + 4 * len(DN_ROWS)
MLP_POS = 36
POS_WIN = [2 * ADA_CH, 2 * ADA_CH + N_WIN + N_VO + MLP_POS]
POS_VO = [p + N_WIN for p in POS_WIN]
POS_MLP = [p + N_VO for p in POS_VO]

C_ID, C_TRI, C_TRIS, C_SAME, C_LEV = 0, 128, 256, 320, 384
C_SEQM = C_LEV + 7 * 128
C_LOW = C_SEQM + 8
C_ROW = C_LOW + 64
C_IOTA = C_ROW + 3
C_GRP = C_IOTA + NTOK
C_PAIR = C_GRP + 9
C_KQ = C_PAIR + 64
NC = C_KQ + 64
NPAIR = NSEQ // 2

CLASSES = [(128, [(0, 128)]), (224, [(0, 128), (128, 96)]), (NTOK, TILES)]


def constant_tables():
    c = np.zeros((P, NC), np.float32)
    j, i = np.arange(P)[:, None], np.arange(P)[None, :]
    c[:, C_ID:C_ID + P] = j == i
    c[:, C_TRI:C_TRI + P] = j <= i
    js, is_ = j[:NS], i[:, :NS]
    c[:NS, C_TRIS:C_TRIS + NS] = (js <= is_) & (js // DSEQ == is_ // DSEQ)
    c[:NS, C_SAME:C_SAME + NS] = js // DSEQ == is_ // DSEQ
    for n, s in enumerate(LEVELS):
        c[:, C_LEV + n * P:C_LEV + (n + 1) * P] = (i // (2 * s) == j // (2 * s)) & (i % (2 * s) >= s) & (j % (2 * s) < s)
    c[:NS, C_SEQM:C_SEQM + 8] = np.arange(NS)[:, None] // DSEQ == np.arange(8)[None, :]
    e, f = np.arange(8)[:, None], np.arange(8)[None, :]
    c[:, C_LOW:C_LOW + 64] = (f < e).astype(np.float32).reshape(1, 64)
    row = np.arange(P)
    rh, ra, rm, rt = row // 32, (row // 16) % 2, (row // 8) % 2, row % 8
    c[:, C_ROW] = [SLOPE[h] for h in rh]
    c[:, C_ROW + 1] = rm == 0
    c[:, C_ROW + 2] = rm == 1
    c[:, C_GRP:C_GRP + 9] = (row % 32)[:, None] == np.arange(9)[None, :]
    for a in range(2):
        c[:, C_PAIR + 32 * a:C_PAIR + 32 * (a + 1)] = (ra == a)[:, None] & ((8 * rh + rt)[:, None] == np.arange(32)[None, :])
    c[:, C_KQ:C_KQ + 64] = (row % 32 < 16)[:, None] & ((32 * ((row // 8) % 2) + 8 * rh + rt)[:, None] == np.arange(64)[None, :])
    c[:, C_IOTA:C_IOTA + NTOK] = np.arange(1, NTOK + 1)[None, :]
    dp = np.full((P, 2, SEQ), NEG, np.float32)
    for qt in range(2):
        q, k = qt * P + np.arange(P)[:, None], np.arange(SEQ)[None, :]
        dp[:, qt] = np.where(q >= k, k - q, NEG)
    ds = (np.arange(PAST)[None, :] - (PAST + rt[:, None])).astype(np.float32)
    dn = np.full((P, NPAIR, NS), NEG, np.float32)
    for i in range(NPAIR):
        for u in range(NS):
            seen = (2 * i + ra == u // DSEQ) & (u % DSEQ <= rt)
            dn[:, i, u] = np.where(seen, u % DSEQ - rt, NEG)
    return c, dp.reshape(P, 2 * SEQ), ds, dn.reshape(P, NPAIR * NS)


REGION = 12512


class Chain:

    def __init__(self, eng, sem):
        self.eng, self.sem, self.n, self.extra, self.start = eng, sem, 0, 0, 0

    def __call__(self, ins):
        self.n += 1
        ins.then_inc(self.sem, 1)
        self.eng.wait_ge(self.sem, self.extra + self.n)

    def loop(self, reg, per):
        self.extra, self.start = reg * per, self.n

    def done(self, per, times):
        assert self.n - self.start == per, (self.n - self.start, per)
        self.extra, self.n = 0, self.start + per * times


def trunk_kernel(nc, x_p, x_s, cache_k, cache_v, st_conv, st_delta, ptab, c_p, c_s, w_in, w_out, lam_p,
                 subln, conv_w, a_log, dt_bias, norm_b, ada_w, ada_b, ln1_g, ln1_b, ln2_g, ln2_b,
                 dw_up, dw_dn, m_r, m_rb, mw_up, mw_dn, t_c, t_dp, t_ds, t_dn,
                 y_p, y_s, k_p, v_p, cv_p, dl_p, k_s, v_s, cv_s, dl_s):
    with ExitStack() as ctx:
        def sb(name, shape, dt=F32):
            return ctx.enter_context(nc.sbuf_tensor(name, shape, dt))

        def sem(name):
            return ctx.enter_context(nc.semaphore(name))

        ps = ctx.enter_context(nc.psum_tensor("ps", [P, 8, 512], F32))

        xT = sb("xT", [P, KT, NTOK])
        hT = sb("hT", [P, KT, NTOK])
        mixT = sb("mixT", [P, KT, NTOK])
        big = sb("big", [P, 12 * NTOK + 12 * PB])
        pA = big[:, 0:12 * NTOK].rearrange("p (f t) -> p f t", t=NTOK)
        pB = big[:, 12 * NTOK:].rearrange("p (f t) -> p f t", t=PB)
        pBs = pB[:, :, 3 + SEQ:3 + SEQ + 88].rearrange("p f (s r) -> p f s r", r=3 + DSEQ)
        xc = big[:, 0:KT * NTOK].rearrange("p (f t) -> p f t", t=NTOK)
        sq = big[:, KT * NTOK:2 * KT * NTOK].rearrange("p (f t) -> p f t", t=NTOK)
        ff = big[:, 0:FT * NTOK].rearrange("p (f t) -> p f t", t=NTOK)
        xrow = big[:, 0:3 * D].rearrange("p (a n) -> p a n", a=3)
        yrow = xrow
        va = sb("va", [P, 3, 512])
        ring = sb("ring", [P, RING, KT * CH])
        mod = sb("mod", [P, DEPTH, 48, 9])
        vrow = sb("vrow", [P, 4, P])
        vecT = sb("vecT", [P, 3, P])
        siluC = sb("siluC", [P, KT, 32])
        C = sb("C", [P, NC])
        dP = sb("dP", [P, 2, SEQ])
        dS = sb("dS", [P, PAST])
        dN = sb("dN", [P, NPAIR, NS])
        onesm = sb("onesm", [P, P])
        mean1 = sb("mean1", [P, P])
        cols = sb("cols", [P, 4])
        rstd = sb("rstd", [P, 2, NTOK])
        lnv = sb("lnv", [P, NTOK])
        wba = sb("wba", [P, DEPTH * KT + 3, 8])
        wr = sb("wr", [P, KT + 3, NE])
        small = sb("small", [P, 128])
        route = sb("route", [P, 3, 3, NE + 1])
        cls = sb("cls", [P, NE], I32)
        lamb = sb("lamb", [P, DEPTH, 256])
        lamw = sb("lamw", [P, 8])
        lamc = sb("lamc", [P, DEPTH, 2])
        adt = sb("adt", [P, 2, DEPTH, H])
        brb = sb("brb", [P, NE])
        pt_sb = sb("pt_sb", [1, NSEQ * NPG], I32)
        rowb = mixT[:, :, :].rearrange("p k t -> p (k t)")[0:27, 0:3 * 512]
        tail = sb("tail", [P, 12, 27])
        kst = sb("kst", [P, 3, 512])
        ctmp = sb("ctmp", [P, 2, NTOK])
        Sp = sb("Sp", [P, H, P])
        region = sb("region", [P, REGION])
        off = [0]

        def cut(n):
            off[0] += n
            assert off[0] <= REGION, off[0]
            return region[:, off[0] - n:off[0]]

        vring = cut(8 * 512).rearrange("p (a n) -> p a n", a=8)
        kring = cut(4 * 512).rearrange("p (a n) -> p a n", a=4)
        ktb = cut(2 * 512).rearrange("p (a n) -> p a n", a=2)
        scb = cut(2 * (PAST + NS)).rearrange("p (a n) -> p a n", a=2)
        ptb = cut(9 * P).rearrange("p (a n) -> p a n", a=9)
        qbd = cut(2 * H * 32).rearrange("p (a h n) -> p a h n", a=2, h=H)
        ob = cut(2 * P).rearrange("p (a n) -> p a n", a=2)
        oA = cut(H * NTOK).rearrange("p (h t) -> p h t", h=H)
        ptr = ptb[:, 0:4, :].rearrange("p a n -> p (a n)").rearrange("p (a n) -> p a n", a=2)
        off[0] = 0
        Ss = cut(NSEQ * H * P).rearrange("p (s h v) -> p s h v", s=NSEQ, h=H)
        g4 = lambda: cut(512)
        Gb_e, bbs, DT, LT, QK, LM, X, XT, PP, rT, rr, vn, kd, qd, oG, sG = [g4() for _ in range(16)]
        off[0] = 0
        Gb_e1, bbs1, QK1, XT1, qd1, kd1 = [g4() for _ in range(6)]
        PREP = [(Gb_e, bbs, QK, XT, qd, kd, DT, LT, LM, X, PP), (Gb_e1, bbs1, QK1, XT1, qd1, kd1, rT, rr, vn, oG, sG),
                (Gb_e, bbs, QK, XT, qd, kd, DT, LT, LM, X, PP)]
        LEVEL_BANKS = [(6, 7, 0), (1, 2, 3), (6, 7, 0)]
        kdm = (DT, LT), (LM, X)
        base = NSEQ * H * P + 2 * 512
        kqp = region[:, base:base + H * 144].rearrange("p (h s j) -> p h s j", h=H, s=9)
        Rsb = region[:, base + 3 * 512:base + 5 * 512]
        off[0] = 0
        hrow = cut(3 * D).rearrange("p (a n) -> p a n", a=3)
        frow = cut(3 * D).rearrange("p (a n) -> p a n", a=3)
        Xe = cut(KT * NTOK).rearrange("p (k t) -> p k t", k=KT)
        Sel, SelG, GT = [cut(3 * NTOK).rearrange("p (a t) -> p a t", a=3) for _ in range(3)]
        sil = kst[:, :, :].rearrange("p a n -> p (a n)")[:, 0:4 * NTOK].rearrange("p (b a t) -> p b a t", b=2, a=2)

        ident = C[:, C_ID:C_ID + P]
        tri = C[:, C_TRI:C_TRI + P]

        def c3(t, a):
            return t.rearrange("p (h t) -> p h t", h=H)[:, :, 0:a]

        s_tab = sem("tables_loaded")
        s_pt = sem("page_table_loaded")
        s_ones = sem("ones_written")
        s_full = [sem(f"chunk_loaded_{i}") for i in range(RING)]
        s_chunk = sem("chunk_done")
        s_vecT = sem("vectors_transposed")
        s_vec = sem("vectors_copied")
        s_xt = sem("x_transposed")
        s_silc = sem("silu_c")
        s_adE = sem("mod_rows")
        s_adT = sem("mod_turned")
        s_modev = sem("mod_copied")
        s_mod = sem("mod_ready")
        s_lnin = sem("ln_input")
        s_mean = sem("ln_mean")
        s_xc = sem("ln_centered")
        s_sq = sem("ln_squared")
        s_var = sem("ln_var")
        s_rstd = sem("ln_rstd")
        s_xn = sem("ln_scaled")
        s_h = sem("h_prompt")
        s_hs = sem("h_sample")
        s_xa = sem("x_times_alpha")
        s_pev = sem("proj_copied")
        s_va = sem("v_rows")
        s_ba = sem("ba_done")
        s_nar = sem("narrow_products_psum")
        s_narc = sem("narrow_products")
        s_bae = sem("ba_copied")
        s_hist = sem("history_loaded")
        s_histT = sem("history_transposed")
        s_histc = sem("history_placed")
        s_kT = sem("k_rows_psum")
        s_kst = sem("k_rows")
        s_tailT = sem("tail_transposed")
        s_tailc = sem("tail_rows")
        s_conv = sem("conv_done")
        s_csil = sem("conv_silu")
        s_l2q = sem("l2_squared")
        s_l2s = sem("l2_summed")
        s_l2r = sem("l2_rinv")
        s_l2d = sem("l2_done")
        s_lam = sem("lambda_ready")
        s_pS = sem("p_scores")
        s_pM = sem("p_max")
        s_pE = sem("p_exp")
        s_pA = sem("p_probs")
        s_pT = sem("p_probsT_psum")
        s_pTc = sem("p_probsT")
        s_pV = sem("p_pv")
        s_pO = sem("p_out")
        s_qbz = sem("q_blocks_zero")
        s_qb = sem("q_blocks")
        s_kf = [sem(f"k_page_{i}") for i in range(4)]
        s_vf = [sem(f"v_page_{i}") for i in range(8)]
        s_kt = sem("k_page_transposed")
        s_ktA = sem("k_page_copied_act")
        s_kmm = sem("k_page_scored")
        s_sS = sem("s_scores")
        s_sM = sem("s_max")
        s_sE = sem("s_exp")
        s_sP = sem("s_probs")
        s_sT = sem("s_probsT_psum")
        s_sTc = sem("s_probsT")
        s_sTd = sem("s_probsT_last")
        s_vd = sem("v_page_used")
        s_ob = sem("s_pv_rows")
        s_oT = sem("s_pv_turned")
        s_sV = sem("s_pv")
        s_sO = sem("s_out")
        s_oq = sem("attn_squared")
        s_os = sem("attn_summed")
        s_or = sem("attn_rstd")
        s_mA = sem("attn_mixed")
        s_bt = sem("beta_g_ready")
        s_bta = sem("beta_g_act")
        s_btd = sem("beta_g_dve")
        s_S0 = sem("state_loaded")
        s_gG = sem("g_sums")
        s_gGc = sem("g_sums_copied")
        s_gE = sem("g_exp")
        s_gK = sem("g_kk_kq_k")
        s_gkd = sem("g_kdec")
        s_lm = sem("g_level_mask")
        s_g1 = sem("g_level_P")
        s_g1c = sem("g_level_P_copied")
        s_g2 = sem("g_level_Q")
        s_g2c = sem("g_level_updated")
        s_gR = sem("g_kS")
        s_gRc = sem("g_rT")
        s_gRt = sem("g_r_psum")
        s_gr = sem("g_r")
        s_gV = sem("g_vnew_psum")
        s_gv = sem("g_vnew")
        s_gO = sem("g_o_psum")
        s_gS = sem("g_state_psum")
        s_gSc = sem("g_state")
        s_gkm = sem("g_kdec_masked")
        s_kq = sem("g_kq_packed")
        s_kqS = sem("g_kq_states")
        s_kqc = sem("g_kq_states_copied")
        s_goa = sem("g_o_added")
        s_goq = sem("g_o_squared")
        s_gos = sem("g_o_summed")
        s_gor = sem("g_o_rstd")
        s_mB = sem("gdn_mixed")
        s_rt = sem("router_logits")
        s_rtm = sem("router_max")
        s_rte = sem("router_exp")
        s_hrT = sem("h_rows_psum")
        s_hr = sem("h_rows")
        s_sel = sem("experts_chosen")
        s_pos = sem("slots_counted")
        s_route = sem("routing_ready")
        s_route2 = sem("counts_compared")
        s_prep = sem("selection_ready")
        s_gtT = sem("gate_selection_psum")
        s_gt = sem("gate_selection_turned")
        s_xeT = sem("packed_psum")
        s_xe = sem("packed")
        s_fr = sem("expert_rows")
        s_cb = sem("expert_sum_psum")
        s_fa = sem("expert_summed")
        s_sil = sem("gate_silu")
        s_ff = sem("ff_ready")
        s_turn = sem("values_begun")
        s_yT = sem("y_rows_psum")
        s_y = sem("y_rows")
        s_out = sem("outputs_stored")
        s_cd = sem("dve_chain")
        s_ca = sem("act_chain")
        s_cp = sem("pool_chain")

        block = ctx.enter_context(nc.Block())

        def full(pos, e=0):
            return s_full[pos % RING], 16 * (pos // RING + 1) + e * (16 * MLP_POS // RING)

        def chunk(pos):
            return ring[:, pos % RING, :].rearrange("p (k n) -> p k n", n=CH)

        def wsrc(w, col):
            return w[:, bass.ds(col, CH)].rearrange("(k p) n -> p k n", p=P)

        N_TAB = [0]

        def tables(sp):
            def ld(dst, src):
                N_TAB[0] += 16
                sp.dma_start(dst, src).then_inc(s_tab, 16)

            ld(C[:], t_c)
            ld(vrow[0:96, 0, :], ada_b.rearrange("l (f p) -> (l f) p", p=P))
            ld(vrow[96:98, 0, :], subln)
            ld(vrow[98:100, 0, :], norm_b)
            ld(vrow[0:96, 1, :], conv_w.rearrange("l w (f p) -> (l w f) p", p=P))
            for n, v in enumerate((ln1_g, ln1_b, ln2_g, ln2_b)):
                ld(vrow[16 * n:16 * n + 16, 2, :], v.rearrange("l (f p) -> (l f) p", p=P))
            ld(vrow[0:8, 3, :], c_p.rearrange("a (f p) -> (a f) p", p=P))
            ld(vrow[8:72, 3, :], c_s.rearrange("a (f p) -> (a f) p", p=P))
            ld(xrow[:, 0:2, :], x_p[0].rearrange("(a p) n -> p a n", p=P))
            ld(xrow[0:NS, 2, :], x_s.rearrange("s t n -> (s t) n"))
            ld(dP[:], t_dp.rearrange("p (a n) -> p a n", a=2))
            ld(dS[:], t_ds)
            ld(dN[:], t_dn.rearrange("p (a n) -> p a n", a=NPAIR))
            for l in range(DEPTH):
                ld(wba[:, l * KT:(l + 1) * KT, :], w_in[l][:, 3072:3080].rearrange("(k p) n -> p k n", p=P))
                ld(lamb[:, l, :], lam_p[l:l + 1].rearrange("o a b -> o (a b)").to_broadcast([P, 256]))
                ld(adt[:, 0, l, :], a_log[l:l + 1, :].to_broadcast([P, H]))
                ld(adt[:, 1, l, :], dt_bias[l:l + 1, :].to_broadcast([P, H]))
            ld(wr[:, 0:KT, :], m_r[0].rearrange("(k p) n -> p k n", p=P))
            ld(brb[:], m_rb[0:1, :].to_broadcast([P, NE]))

        N_TABLES = 16 * 26

        @block.sync
        def _(sp):
            tables(sp)
            assert N_TAB[0] == N_TABLES, N_TAB[0]
            sp.dma_start(pt_sb[:], ptab.rearrange("(o a) b -> o (a b)", o=1)).then_inc(s_pt, 16)

            def load(dst, src, pos, e=0, first=False):
                if not first:
                    sp.wait_ge(s_chunk, pos - RING + 1 + e * MLP_POS)
                sp.dma_start(dst, src).then_inc(full(pos)[0], 16)

            for c in range(RING):
                load(chunk(c), wsrc(ada_w[0], CH * c), c, first=True)
            for l in range(DEPTH):
                with sp.Fori(1 if l == 0 else 0, ADA_CH // RING) as i:
                    for c in range(RING):
                        sp.wait_ge(s_chunk, ADA_CH * l + c - RING + 1 + i * RING)
                        sp.dma_start(chunk(c), wsrc(ada_w[l], i * (RING * CH) + CH * c)).then_inc(s_full[c], 16)

            def mlp(w_up, w_dn, pos, e=0):
                for j in range(UP):
                    for part in range(2):
                        p = pos + 2 * j + part
                        load(chunk(p), wsrc(w_up, part * FF + CH * j), p, e)
                for d in range(4):
                    for n, (f0, nf) in enumerate(DN_ROWS):
                        p = pos + 2 * UP + 3 * d + n
                        load(chunk(p)[:, 0:nf, :],
                             w_dn[f0 * P:(f0 + nf) * P, CH * d:CH * (d + 1)].rearrange("(k p) n -> p k n", p=P), p, e)
                for p in range(pos + MLP_CH, pos + MLP_POS):
                    sp.wait_ge(s_chunk, p - RING + 1 + e * MLP_POS)
                    sp.sem_inc(full(p)[0], 16)

            for l in range(DEPTH):
                if l > 0:
                    sp.wait_ge(s_chunk, POS_VO[l - 1] + N_VO)
                sp.dma_start(rowb[0:24, :], st_conv[l].rearrange("s r n -> (s r) n")).then_inc(s_hist, 16)
                for c in range(N_WIN):
                    load(chunk(POS_WIN[l] + c), wsrc(w_in[l], WIN_COLS[c]), POS_WIN[l] + c)
                for c in range(2):
                    load(chunk(POS_VO[l] + c), wsrc(w_in[l], 1024 + CH * c), POS_VO[l] + c)
                for c in range(4):
                    load(chunk(POS_VO[l] + 2 + c), wsrc(w_out[l], CH * c), POS_VO[l] + 2 + c)
                if l == 0:
                    sp.wait_ge(s_pt, 16)
                else:
                    sp.wait_ge(s_mB, 3 * l)
                    sp.wait_ge(s_out, 16 * 8 * l)

                def v_pages(s):
                    for p in range(NPG):
                        pg = sp.value_load(pt_sb[0:1, bass.ds(s * NPG + p, 1)], min_val=0, max_val=NPOOL - 1)
                        if l or not isinstance(s, int):
                            sp.wait_ge(s_vd, 64 * l + s * NPG + p - 7)
                        sp.dma_start(vring[:, p, :], cache_v[l, bass.ds(pg, 1)].rearrange("o k h d -> (o k) (h d)")
                                     ).then_inc(s_vf[p], 16)

                v_pages(0)
                with sp.Fori(1, NSEQ) as s:
                    v_pages(s)
                if l == 0:
                    mlp(dw_up[0], dw_dn[0], POS_MLP[0])
                else:
                    with sp.Fori(0, NE) as e:
                        mlp(mw_up[0, bass.ds(e, 1)].rearrange("o a b -> (o a) b"),
                            mw_dn[0, bass.ds(e, 1)].rearrange("o a b -> (o a) b"), POS_MLP[1], e)

        @block.gpsimd
        def _(pool):
            link = Chain(pool, s_cp)
            nc.gpsimd.memset(onesm[:], 1.0).then_inc(s_ones, 1)
            nc.gpsimd.memset(mean1[:], 1.0 / D).then_inc(s_ones, 1)
            nc.gpsimd.memset(cols[:, 0:1], LN_EPS).then_inc(s_ones, 1)
            nc.gpsimd.memset(cols[:, 1:2], 1e-6).then_inc(s_ones, 1)
            nc.gpsimd.memset(cols[:, 2:3], -0.5 * math.log(P)).then_inc(s_ones, 1)
            nc.gpsimd.memset(cols[:, 3:4], 1.0).then_inc(s_ones, 1)
            nc.gpsimd.memset(small[:], 0.0).then_inc(s_ones, 1)
            nc.gpsimd.memset(siluC[:], 0.0).then_inc(s_ones, 1)
            nc.gpsimd.memset(wba[:, DEPTH * KT:, :], 0.0).then_inc(s_ones, 1)
            nc.gpsimd.memset(wr[:, KT:, :], 0.0).then_inc(s_ones, 1)
            pool.wait_ge(s_pt, 16)

            def store(dst, src):
                pool.dma_start(dst, src).then_inc(s_out, 16)

            for l in range(DEPTH):
                if l > 0:
                    pool.wait_ge(s_mB, 3 * l)
                    pool.wait_ge(s_out, 16 * 8 * l)
                nc.gpsimd.memset(qbd[:], 0.0).then_inc(s_qbz, 1)

                def pages(s):
                    for p in range(NPG):
                        pg = pool.value_load(pt_sb[0:1, bass.ds(s * NPG + p, 1)], min_val=0, max_val=NPOOL - 1)
                        if p >= 4 or not isinstance(s, int) or s > 0 or l > 0:
                            pool.wait_ge(s_kt, 64 * l + s * NPG + p - 3)
                        pool.dma_start(kring[:, p % 4, :], cache_k[l, bass.ds(pg, 1)].rearrange("o k h d -> (o k) (h d)")
                                       ).then_inc(s_kf[p % 4], 16)

                pages(0)
                with pool.Fori(1, NSEQ) as s:
                    pages(s)
                pool.wait_ge(s_va, 2 * (l + 1))
                store(v_p[l, 0].rearrange("(a p) h d -> p a (h d)", p=P), va[:, 0:2, :])
                store(v_s[l].rearrange("s t h d -> (s t) (h d)"), va[0:NS, 2, :])
                pool.wait_ge(s_kst, l + 1)
                store(k_p[l, 0].rearrange("(a p) h d -> p a (h d)", p=P), kst[:, 0:2, :])
                store(k_s[l].rearrange("s t h d -> (s t) (h d)"), kst[0:NS, 2, :])
                pool.wait_ge(s_tailc, l + 1)
                store(cv_p[l, 0], rowb[0:3, :])
                store(cv_s[l].rearrange("s r n -> (s r) n"), rowb[3:27, :])
                pool.wait_ge(s_gor, 3 * l + 2)
                pool.wait_ge(s_mB, 3 * l + 2)
                pool.dma_start(Ss, st_delta[l].rearrange("s h k v -> k s h v")).then_inc(s_S0, 16)
                pool.wait_ge(s_gSc, 34 * l + 2)
                store(dl_p[l, 0].rearrange("h k v -> k h v"), Sp[:])
                pool.wait_ge(s_gSc, 34 * l + 34)
                store(dl_s[l].rearrange("s h k v -> k s h v"), Ss)
            pool.wait_ge(s_y, 3)
            store(y_p[0].rearrange("(a p) n -> p a n", p=P), yrow[:, 0:2, :])
            store(y_s.rearrange("s t n -> (s t) n"), yrow[0:NS, 2, :])
            pool.wait_ge(s_out, 16 * 18)

        @block.tensor
        def _(pe):
            mm, tr = nc.tensor.matmul, nc.tensor.transpose

            def ln(n):
                for k in range(KT):
                    pe.wait_ge(s_lnin, KT * n + k + 1)
                    m = mm(ps[:, 0, 0:NTOK], mean1[:], xT[:, k, :], start=(k == 0), stop=(k == KT - 1))
                m.then_inc(s_mean, 1)
                for k in range(KT):
                    if k % 2 == 0:
                        pe.wait_ge(s_sq, 4 * n + k // 2 + 1)
                    m = mm(ps[:, 1, 0:NTOK], mean1[:], sq[:, k, :], start=(k == 0), stop=(k == KT - 1))
                m.then_inc(s_var, 1)

            def take(pos, e=0):
                pe.wait_ge(*full(pos, e))
                return chunk(pos)

            def two_tiles(w, b, rhs, n=NTOK, nk=KT, first=True, last=True):
                for o in range(2):
                    for k in range(nk):
                        m = mm(ps[:, b + o, 0:n], w[:, k, o * P:(o + 1) * P], rhs[:, k, 0:n],
                               start=(first and k == 0), stop=(last and k == nk - 1))
                return m

            def narrow(w, b):
                for k in range(KT):
                    g = 32 * (k % 4)
                    m = mm(ps[g:g + 32, b, 0:NTOK], w[:, k:k + 4, :].rearrange("p k n -> p (k n)"), hT[:, k, :],
                           start=(k < 4), stop=(k >= 4))
                m.then_inc(s_nar, 1)

            def narrow_rows(n, b):
                pe.wait_ge(s_narc, n + 1)
                for t, (c0, nt) in enumerate(TILES):
                    m = mm(ps[0:nt, b, 8 * t:8 * t + 8], lnv[:, c0:c0 + nt], C[:, C_GRP:C_GRP + 8], start=True, stop=True)
                return m

            def h_ready(m):
                pe.wait_ge(s_h, KT * (m + 1))
                pe.wait_ge(s_hs, m + 1)

            def up(pos, e, nff, rhs, n):
                for j in range(UP):
                    b = 4 * (j % 2)
                    if j >= 2:
                        pe.wait_ge(s_ff, nff + j - 1)
                    w = take(pos + 2 * j, e)
                    two_tiles(w, b, rhs, n).then_inc(s_chunk, 1)
                    w = take(pos + 2 * j + 1, e)
                    two_tiles(w, b + 2, rhs, n).then_inc(s_chunk, 1)
                pe.wait_ge(s_ff, nff + UP)

            def dense():
                up(POS_MLP[0], 0, 0, hT, NTOK)
                for d in range(4):
                    for i, (f0, nf) in enumerate(DN_ROWS):
                        w = take(POS_MLP[0] + 2 * UP + 3 * d + i)
                        for o in range(2):
                            for k in range(nf):
                                m = mm(ps[:, 2 * d + o, 0:NTOK], w[:, k, o * P:(o + 1) * P], ff[:, f0 + k, :],
                                       start=(i == 0 and k == 0), stop=(i == 2 and k == nf - 1))
                        m.then_inc(s_chunk, 1 + (MLP_POS - MLP_CH if d == 3 and i == 2 else 0))

            def expert(e, slots, rows):
                pos = POS_MLP[1]
                pe.wait_ge(s_prep, e + 1)
                for s_, (r0, nr) in enumerate(rows):
                    for t, (c0, nt) in enumerate(TILES):
                        m = tr(ps[0:nr, s_, c0:c0 + nt], SelG[0:nt, t, r0:r0 + nr], ident[0:nt, 0:nt])
                m.then_inc(s_gtT, 1)
                pe.wait_ge(s_fa, KT + e * KT)
                for k in range(KT):
                    if k >= 4:
                        pe.wait_ge(s_xe, e * KT + k - 3)
                    for t, (c0, nt) in enumerate(TILES):
                        m = mm(ps[:, 4 + k % 4, 0:slots], hrow[0:nt, t, k * P:(k + 1) * P], Sel[0:nt, t, 0:slots],
                               start=(t == 0), stop=(t == 2))
                    m.then_inc(s_xeT, 1)
                pe.wait_ge(s_xe, e * KT + KT)
                pe.wait_ge(s_gt, e + 1)
                up(pos, e, UP + e * UP, Xe, slots)
                for d in range(4):
                    if d >= 2:
                        pe.wait_ge(s_fr, e * 4 + d - 1)
                    for i, (f0, nf) in enumerate(DN_ROWS):
                        w = take(pos + 2 * UP + 3 * d + i, e)
                        for k in range(nf):
                            for s_, (r0, nr) in enumerate(rows):
                                m = mm(ps[0:nr, 3 * (d % 2) + s_, 0:CH], ff[:, f0 + k, r0:r0 + nr], w[:, k, :],
                                       start=(i == 0 and k == 0), stop=(i == 2 and k == nf - 1))
                        m.then_inc(s_chunk, 1 + (MLP_POS - MLP_CH if d == 3 and i == 2 else 0))
                pe.wait_ge(s_fr, e * 4 + 4)
                for k in range(KT):
                    if k >= 2:
                        pe.wait_ge(s_fa, KT + e * KT + k - 1)
                    for s_, (r0, nr) in enumerate(rows):
                        m = mm(ps[:, 6 + k % 2, 0:NTOK], frow[0:nr, s_, k * P:(k + 1) * P], GT[0:nr, s_, :],
                               start=(s_ == 0), stop=(s_ == len(rows) - 1))
                    m.then_inc(s_cb, 1)

            pe.wait_ge(s_tab, N_TABLES)
            pe.wait_ge(s_ones, 10)
            for b, n in enumerate((100, 96, 64, 72)):
                m = tr(ps[:, 0, b * P:b * P + n], vrow[0:n, b, :], ident[0:n, 0:n])
            m.then_inc(s_vecT, 1)
            for k in range(KT):
                if k >= 4:
                    pe.wait_ge(s_lnin, k - 3)
                for t, (c0, nt) in enumerate(TILES):
                    m = tr(ps[:, 1 + k % 4, c0:c0 + nt], xrow[0:nt, t, k * P:(k + 1) * P], ident[0:nt, 0:nt])
                m.then_inc(s_xt, 1)
            pe.wait_ge(s_silc, 1)
            def turn_mod(c, n):
                pe.wait_ge(s_adE, n + 1)
                if not (isinstance(n, int) and n < 2):
                    pe.wait_ge(s_modev, n - 1)
                for o in range(2):
                    m = mm(ps[:, 5 * (c % 2), 16 * o:16 * o + 9], kst[:, c % 2, o * P:(o + 1) * P], C[:, C_GRP:C_GRP + 9],
                           start=True, stop=True)
                m.then_inc(s_adT, 1)

            def ada(i):
                for c in range(RING):
                    n = i * RING + c
                    pe.wait_ge(s_full[c], 16 + 16 * i)
                    if c >= 2 or not isinstance(i, int):
                        pe.wait_ge(s_adE, n - 1)
                    for k in range(KT):
                        g = 32 * (k % 4)
                        m = mm(ps[g:g + 32, 6 + c % 2, 0:CH], siluC[:, k, :], chunk(c)[:, k, :], start=(k < 4), stop=(k >= 4))
                    m.then_inc(s_chunk, 1)
                    if c >= 1 or not isinstance(i, int):
                        turn_mod((c - 1) % RING, n - 1)

            ada(0)
            with pe.Fori(1, DEPTH * ADA_CH // RING) as i:
                ada(i)
            turn_mod(RING - 1, DEPTH * ADA_CH - 1)
            pe.wait_ge(s_modev, DEPTH * ADA_CH)

            for l in range(DEPTH):
                ln(4 * l)
                h_ready(2 * l)
                pe.wait_ge(s_hist, 16 * (l + 1))
                for f in range(12):
                    m = tr(ps[:, 7, 24 * f:24 * f + 24], rowb[0:24, f * P:(f + 1) * P], ident[0:24, 0:24])
                m.then_inc(s_histT, 1)
                for c in range(N_WIN):
                    w = take(POS_WIN[l] + c)
                    if c == 3:
                        pe.wait_ge(s_histc, l + 1)
                    if c >= 4:
                        pe.wait_ge(s_pev, N_WIN * l + c - 3)
                    two_tiles(w, 2 * (c % 4), hT).then_inc(s_chunk, 1)
                pe.wait_ge(s_pev, N_WIN * (l + 1))
                narrow(wba[:, l * KT:, :], 6)
                for c in range(2):
                    w = take(POS_VO[l] + c)
                    for t, (c0, nt) in enumerate(TILES):
                        for k in range(KT):
                            m = mm(ps[0:nt, 3 * c + t, 0:CH], hT[:, k, c0:c0 + nt], w[:, k, :],
                                   start=(k == 0), stop=(k == KT - 1))
                    m.then_inc(s_chunk, 1)
                    if c == 0:
                        narrow_rows(l, 7).then_inc(s_ba, 1)
                pe.wait_ge(s_va, 2 * (l + 1))
                for t, (c0, nt) in enumerate(TILES):
                    for h in range(H):
                        m = tr(ps[0:nt, t, h * P:(h + 1) * P], pA[:, 4 + h, c0:c0 + nt], ident)
                m.then_inc(s_kT, 1)
                pe.wait_ge(s_pev, N_WIN * (l + 1))
                for f in range(12):
                    m = tr(ps[0:27, 3 + f // 4, (f % 4) * P:(f % 4 + 1) * P], tail[:, f, :], ident)
                m.then_inc(s_tailT, 1)
                pe.wait_ge(s_histc, l + 1)
                pe.wait_ge(s_bae, l + 1)
                for b in range(4):
                    pe.wait_ge(s_l2q, 4 * l + b + 1)
                    if b == 1:
                        pe.wait_ge(s_tailc, l + 1)
                    if b >= 2:
                        pe.wait_ge(s_l2r, 4 * l + b - 1)
                    for o in range(2):
                        m = mm(ps[:, 6 - 2 * (b % 2) + o, 0:NTOK], onesm[:], ctmp[:, o, :], start=True, stop=True)
                    m.then_inc(s_l2s, 1)

                units = [(h, qt) for h in range(H) for qt in range(2)]

                def scores(u):
                    h, qt = units[u]
                    nk = P * (qt + 1)
                    if u == 0:
                        pe.wait_ge(s_kst, l + 1)
                        pe.wait_ge(s_tailc, l + 1)
                        pe.wait_ge(s_l2r, 4 * (l + 1))
                    if u >= 2:
                        pe.wait_ge(s_pM, 8 * l + u - 1)
                    for m_ in range(2):
                        r = slice(64 * m_, 64 * m_ + 64)
                        m = mm(ps[:, 2 * (u % 2) + m_, 0:nk], pA[r, h, qt * P:(qt + 1) * P],
                               pA[r, 4 + h, 0:nk], start=True, stop=True)
                    m.then_inc(s_pS, 1)

                scores(0)
                for u, (h, qt) in enumerate(units):
                    if u + 1 < 8:
                        scores(u + 1)
                    pe.wait_ge(s_pA, 8 * l + u + 1)
                    if u >= 1:
                        pe.wait_ge(s_pTc, 8 * l + u)
                    for kb in range(qt + 1):
                        m = tr(ps[:, 4, kb * P:(kb + 1) * P], scb[:, u % 2, kb * P:(kb + 1) * P], ident)
                    m.then_inc(s_pT, 1)
                    pe.wait_ge(s_pTc, 8 * l + u + 1)
                    if u >= 2:
                        pe.wait_ge(s_pO, 8 * l + u - 1)
                    for kb in range(qt + 1):
                        m = mm(ps[:, 5 + u % 2, 0:P], va[:, kb, h * P:(h + 1) * P], ptr[:, u % 2, kb * P:(kb + 1) * P],
                               start=(kb == 0), stop=(kb == qt))
                    m.then_inc(s_pV, 1)

                pe.wait_ge(s_pO, 8 * (l + 1))

                def pair_scores(i):
                    g = NPAIR * l + i
                    early = l == 0 and isinstance(i, int) and i == 0

                    def turn(n):
                        pe.wait_ge(s_kf[n % 4], 16 * (4 * g + n // 4 + 1))
                        if not (early and n < 2):
                            pe.wait_ge(s_ktA, 16 * g + n - 1)
                        for h in range(H):
                            m = tr(ps[:, n % 2, h * P:(h + 1) * P], kring[:, n % 4, h * P:(h + 1) * P], ident)
                        m.then_inc(s_kt, 1)

                    turn(0)
                    for n in range(2 * NPG):
                        a, p = n // NPG, n % NPG
                        if n + 1 < 2 * NPG:
                            turn(n + 1)
                        if n == 0:
                            pe.wait_ge(s_qb, g + 1)
                            if not early:
                                pe.wait_ge(s_sM, g)
                        pe.wait_ge(s_ktA, 16 * g + n + 1)
                        for h in range(H):
                            m = mm(ps[32 * h:32 * h + 32, 2 + p // 4, (p % 4) * P:(p % 4 + 1) * P], qbd[:, a, h, :],
                                   ktb[:, n % 2, h * P:(h + 1) * P], start=(a == 0 and p % 4 == 0), stop=(a == 1 and p % 4 == 3))
                        m.then_inc(s_kmm, 1)
                    for a in range(2):
                        for h in range(H):
                            m = mm(ps[32 * h:32 * h + 32, 4, 0:NS], qbd[:, a, h, :], pA[:, 4 + h, SEQ:NTOK], start=(a == 0), stop=(a == 1))
                    m.then_inc(s_sS, 1)

                def pair_values(i):
                    g = NPAIR * l + i
                    early = l == 0 and isinstance(i, int) and i == 0
                    pe.wait_ge(s_sP, g + 1)
                    if not early:
                        pe.wait_ge(s_sO, g)
                    pe.sem_inc(s_turn, 1)
                    for p in range(NPG):
                        tr(ps[:, 5 + p // 4, (p % 4) * P:(p % 4 + 1) * P], scb[:, 0, p * P:(p + 1) * P], ident)
                    tr(ps[0:64, 4, P:2 * P], scb[:, 0, PAST:PAST + NS], ident).then_inc(s_sT, 1)
                    pe.wait_ge(s_sTc, g + 1)
                    pe.wait_ge(s_sTd, g + 1)
                    for a in range(2):
                        out = lambda h: ps[32 * h:32 * h + 32, 7 - 2 * a, 0:P]
                        for p in range(NPG):
                            pe.wait_ge(s_vf[p], 16 * (2 * g + a + 1))
                            for h in range(H):
                                m = mm(out(h), ptb[:, p, 32 * h:32 * h + 32], vring[:, p, h * P:(h + 1) * P], start=(p == 0), stop=False)
                            m.then_inc(s_vd, 1)
                        for h in range(H):
                            m = mm(out(h), ptb[0:NS, 8, 32 * h:32 * h + 32], va[0:NS, 2, h * P:(h + 1) * P], start=False, stop=True)
                        m.then_inc(s_sV, 1)
                    for a in range(2):
                        pe.wait_ge(s_ob, 2 * g + a + 1)
                        m = mm(ps[:, 6, 32 * a:32 * (a + 1)], ob[:, a, :], C[:, C_PAIR + 32 * a:C_PAIR + 32 * (a + 1)],
                               start=True, stop=True)
                    m.then_inc(s_oT, 1)

                def pair(i):
                    pair_scores(i + 1)
                    pair_values(i)

                pair_scores(0)
                pair(0)
                with pe.Fori(1, NPAIR - 1) as i:
                    pair(i)
                pair_values(NPAIR - 1)

                for h in range(H):
                    pe.wait_ge(s_oq, H * l + h + 1)
                    if h >= 2:
                        pe.wait_ge(s_or, H * l + h - 1)
                    mm(ps[:, h % 2, 0:NTOK], onesm[:], ctmp[:, h % 2, :], start=True, stop=True).then_inc(s_os, 1)

                pe.wait_ge(s_or, H * (l + 1))
                pe.wait_ge(s_bt, l + 1)
                pe.wait_ge(s_l2d, 4 * (l + 1))

                def prepare(T):
                    c0, nt = TILES[T]
                    smp = T == 2
                    triT = C[0:nt, C_TRIS:C_TRIS + nt] if smp else tri
                    same = C[0:nt, C_SAME:C_SAME + nt] if smp else onesm[:]
                    gcol = small[0:nt, 24 + 4 * T:28 + 4 * T]
                    bcol = small[0:nt, 36 + 4 * T:40 + 4 * T]
                    mm(ps[0:nt, 0, 0:4], triT, gcol, start=True, stop=True)
                    mm(ps[0:nt, 0, 4:8], same, gcol, start=True, stop=True)
                    for h in range(H):
                        mm(ps[:, 1, h * P:h * P + nt], gcol[:, h:h + 1].to_broadcast([nt, P]), triT, start=True, stop=True)
                    for h in range(H):
                        m = mm(ps[:, 2, h * P:h * P + nt], bcol[:, h:h + 1].to_broadcast([nt, P]), ident[0:nt, 0:nt],
                               start=True, stop=True)
                    m.then_inc(s_gG, 1)
                    kT = pB[:, 4:8, c0:c0 + nt]
                    qT = pB[:, 0:4, c0:c0 + nt]
                    for h in range(H):
                        mm(ps[0:nt, 3, h * P:h * P + nt], kT[:, h, :], kT[:, h, :], start=True, stop=True)
                    for h in range(H):
                        mm(ps[0:nt, 4, h * P:h * P + nt], kT[:, h, :], qT[:, h, :], start=True, stop=True)
                    for h in range(H):
                        m = tr(ps[0:nt, 5, h * P:(h + 1) * P], kT[:, h, :], ident)
                    m.then_inc(s_gK, 1)

                def levels(tiles):
                    nt = TILES[tiles[0]][1]
                    lev = 3 if tiles[0] == 2 else 7
                    w = len(tiles)
                    for v in range(lev):
                        for x, T in enumerate(tiles):
                            i0 = 17 * l + (14 if T == 2 else 0) + w * v + x
                            LM_, X_ = c3(PREP[T][8], nt), c3(PREP[T][9], nt)
                            pe.wait_ge(s_lm, i0 + 1)
                            if v == 0:
                                pe.wait_ge(s_gE, 3 * l + T + 1)
                            else:
                                pe.wait_ge(s_g2c, i0 - w + 1)
                            for h in range(H):
                                m = mm(ps[0:nt, LEVEL_BANKS[T][0], h * P:h * P + nt], LM_[0:nt, h, :], X_[0:nt, h, :],
                                       start=True, stop=True)
                            m.then_inc(s_g1, 1)
                        for x, T in enumerate(tiles):
                            i0 = 17 * l + (14 if T == 2 else 0) + w * v + x
                            XT_, PP_ = c3(PREP[T][3], nt), c3(PREP[T][10], nt)
                            pe.wait_ge(s_g1c, i0 + 1)
                            if v < lev - 1:
                                for h in range(H):
                                    mm(ps[0:nt, LEVEL_BANKS[T][1], h * P:h * P + nt], XT_[0:nt, h, :], PP_[0:nt, h, :],
                                       start=True, stop=True)
                            for h in range(H):
                                m = mm(ps[0:nt, LEVEL_BANKS[T][2], h * P:h * P + nt], PP_[0:nt, h, :], XT_[0:nt, h, :],
                                       start=True, stop=True)
                            m.then_inc(s_g2, 1)

                def outputs(T):
                    c0, nt = TILES[T]
                    n = 3 * l + T
                    smp = T == 2
                    Gb_, bbs_, QK_, XT_, qd_, kd_ = PREP[T][:6]
                    kT = pB[:, 4:8, c0:c0 + nt]
                    if smp:
                        pe.wait_ge(s_S0, 16 * (l + 1))
                        pe.wait_ge(s_kq, l + 1)
                        for h in range(H):
                            for s in range(NSEQ):
                                g = 32 * (s % 4)
                                m = mm(ps[g:g + 32, 1 + s // 4, h * P:(h + 1) * P],
                                       kqp[:, h, s:s + 2, :].rearrange("p s j -> p (s j)"), Ss[:, s, h, :], start=True, stop=True)
                        m.then_inc(s_kqS, 1)
                        pe.wait_ge(s_kqc, l + 1)
                        for h in range(H):
                            for b in range(2):
                                m = mm(ps[:, 6, h * P + 64 * b:h * P + 64 * b + 64], Rsb[:, 512 * b + h * P:512 * b + (h + 1) * P],
                                       C[:, C_KQ:C_KQ + 64], start=True, stop=True)
                    else:
                        if T == 1:
                            pe.wait_ge(s_gSc, 34 * l + 1)
                        for h in range(H):
                            m = mm(ps[:, 1, h * P:h * P + nt], Sp[:, h, :], kT[:, h, :], start=True, stop=True)
                    m.then_inc(s_gR, 1)
                    pe.wait_ge(s_gRc, n + 1)
                    for h in range(H):
                        m = tr(ps[0:nt, 2, h * P:(h + 1) * P], c3(rT, nt)[:, h, :], ident)
                    m.then_inc(s_gRt, 1)
                    pe.wait_ge(s_gr, n + 1)
                    for h in range(H):
                        m = mm(ps[0:nt, 3, h * P:(h + 1) * P], c3(XT_, nt)[0:nt, h, :], c3(rr, P)[0:nt, h, :], start=True, stop=True)
                    m.then_inc(s_gV, 1)
                    pe.wait_ge(s_gv, n + 1)
                    if not smp:
                        pe.wait_ge(s_gkd, n + 1)
                        for h in range(H):
                            m = mm(ps[:, 5, h * P:(h + 1) * P], c3(kd_, P)[0:nt, h, :], c3(vn, P)[0:nt, h, :], start=True, stop=True)
                        m.then_inc(s_gS, 1)
                    for h in range(H):
                        m = mm(ps[:, 4, h * P:h * P + nt], c3(vn, P)[0:nt, h, :], c3(QK_, nt)[0:nt, h, :], start=True, stop=smp)
                        if not smp:
                            m = mm(ps[:, 4, h * P:h * P + nt], Sp[:, h, :], c3(qd_, nt)[:, h, :], start=False, stop=True)
                    m.then_inc(s_gO, 1)
                    if smp:
                        for h in range(H):
                            pe.wait_ge(s_gkm, H * l + h + 1)
                            if h >= 2:
                                pe.wait_ge(s_gSc, 34 * l + 2 + 8 * (h - 1))
                            for s in range(NSEQ):
                                m = mm(ps[:, (5, 2)[h % 2] + s // 4, (s % 4) * P:(s % 4 + 1) * P],
                                       kdm[h % 2][s // 4][0:nt, (s % 4) * P:(s % 4 + 1) * P],
                                       c3(vn, P)[0:nt, h, :], start=True, stop=True)
                            m.then_inc(s_gS, 1)
                    pe.wait_ge(s_goq, n + 1)
                    mm(ps[:, 7, 0:H * nt], onesm[:], sG[:, 0:H * nt], start=True, stop=True).then_inc(s_gos, 1)

                prepare(0)
                pe.wait_ge(s_lm, 17 * l + 1)
                pe.wait_ge(s_gkd, 3 * l + 1)
                prepare(1)
                levels((0, 1))
                pe.wait_ge(s_g2c, 17 * l + 14)
                outputs(0)
                outputs(1)
                pe.wait_ge(s_mB, 3 * l + 2)
                prepare(2)
                levels((2,))
                pe.wait_ge(s_g2c, 17 * l + 17)
                outputs(2)

                pe.wait_ge(s_mB, 3 * (l + 1))
                pe.wait_ge(s_mA, H * (l + 1))
                for c in range(4):
                    w = take(POS_VO[l] + 2 + c)
                    two_tiles(w, 2 * c, mixT).then_inc(s_chunk, 1)
                ln(4 * l + 1)
                ln(4 * l + 2)
                h_ready(2 * l + 1)
                if l == 0:
                    dense()
                else:
                    narrow(wr, 7)
                    narrow_rows(DEPTH, 6).then_inc(s_rt, 1)
                    for t, (c0, nt) in enumerate(TILES):
                        for k in range(KT):
                            m = tr(ps[0:nt, 2 * t + k // 4, (k % 4) * P:(k % 4 + 1) * P], hT[:, k, c0:c0 + nt], ident)
                    m.then_inc(s_hrT, 1)
                    pe.wait_ge(s_sel, 1)
                    for t, (c0, nt) in enumerate(TILES):
                        for u in range(t + 1):
                            nu = TILES[u][1]
                            mm(ps[0:nt, 7, 8 * t:8 * t + 8], onesm[0:nu, 0:nt] if u < t else tri[0:nt, 0:nt], route[0:nu, 0, u, 0:NE],
                               start=(u == 0), stop=(u == t))
                    for u, (c0, nu) in enumerate(TILES):
                        m = mm(ps[:, 7, 24:32], onesm[0:nu, :], route[0:nu, 0, u, 0:NE], start=(u == 0), stop=(u == 2))
                    m.then_inc(s_pos, 1)
                    pe.wait_ge(s_hr, 3)
                    pe.wait_ge(s_route, 1)
                    with pe.Fori(0, NE) as e:
                        c = pe.value_load(cls[0:1, bass.ds(e, 1)], min_val=0, max_val=2)
                        with pe.If(c < 1):
                            expert(e, *CLASSES[0])
                        with pe.Else():
                            with pe.If(c < 2):
                                expert(e, *CLASSES[1])
                            with pe.Else():
                                expert(e, *CLASSES[2])
                ln(4 * l + 3)
            pe.wait_ge(s_lnin, KT * 8 + KT)
            for t, (c0, nt) in enumerate(TILES):
                for k in range(KT):
                    m = tr(ps[0:nt, 2 * t + k // 4, (k % 4) * P:(k % 4 + 1) * P], xT[:, k, c0:c0 + nt], ident)
                m.then_inc(s_yT, 1)

        @block.scalar
        def _(act):
            A = nc.scalar.activation
            link = Chain(act, s_ca)

            def ln_stats(n):
                for p in range(4):
                    act.wait_ge(s_xc, 4 * n + p + 1)
                    A(sq[:, 2 * p:2 * p + 2, :], xc[:, 2 * p:2 * p + 2, :], ACT.Square).then_inc(s_sq, 1)
                act.wait_ge(s_var, n + 1)
                link(A(lnv[:], ps[:, 1, 0:NTOK], ACT.Ln, bias=cols[:, 0:1]))
                A(rstd[:, 0, :], lnv[:], ACT.Exp, scale=-0.5).then_inc(s_rstd, 1)

            def ln_mod(n, l, half):
                ln_stats(n)
                for k in range(KT):
                    act.wait_ge(s_xn, 4 * n + k // 2 + 1)
                    A(hT[:, k, 0:SEQ], xc[:, k, 0:SEQ], ACT.Identity, scale=mod[:, l, 24 * half + 8 + k, 0:1],
                      bias=mod[:, l, 24 * half + k, 0:1]).then_inc(s_h, 1)

            def ln_post(n, l, half):
                ln_stats(n)
                for k in range(KT):
                    act.wait_ge(s_xn, 4 * n + k // 2 + 1)
                    c = 32 * half + 8 * l + k
                    A(xT[:, k, :], xc[:, k, :], ACT.Identity, scale=vecT[:, 2, c:c + 1],
                      bias=vecT[:, 2, c + 16:c + 17]).then_inc(s_lnin, 1)

            def rinv(out, psum, scale, bias, last):
                act.wait_ge(*last)
                link(A(lnv[:, 0:psum.shape[-1]], psum, ACT.Ln, scale=scale, bias=cols[:, 1:2]))
                return A(out, lnv[:, 0:psum.shape[-1]], ACT.Exp, scale=-0.5, **({"bias": bias} if bias is not None else {}))

            act.wait_ge(s_vecT, 1)
            act.wait_ge(s_ones, 10)
            cps = ps[:, 0, 3 * P:3 * P + 72]
            A(vecT[:, 0, 0:100], ps[:, 0, 0:100], ACT.Copy).then_inc(s_vec, 1)
            A(vecT[:, 1, 0:96], ps[:, 0, P:P + 96], ACT.Copy).then_inc(s_vec, 1)
            A(vecT[:, 2, 0:64], ps[:, 0, 2 * P:2 * P + 64], ACT.Copy).then_inc(s_vec, 1)
            link(A(siluC[:, :, 0:1], cps[:, 0:8].rearrange("p (k o) -> p k o", o=1), ACT.Silu))
            A(siluC[:, :, 1:9], cps[:, 8:72].rearrange("p (s k) -> p k s", k=8), ACT.Silu).then_inc(s_silc, 1)

            def mod_rows(i):
                for c in range(RING):
                    n = i * RING + c
                    act.wait_ge(s_chunk, n + 1)
                    if c >= 2 or not isinstance(i, int):
                        act.wait_ge(s_adT, n - 1)
                    A(kst[:, c % 2, 0:CH], ps[:, 6 + c % 2, 0:CH], ACT.Copy).then_inc(s_adE, 1)

            mod_rows(0)
            with act.Fori(1, DEPTH * ADA_CH // RING) as i:
                mod_rows(i)

            for l in range(DEPTH):
                act.wait_ge(s_mod, 2 * (l + 1))
                act.wait_ge(s_vec, 3)
                act.wait_ge(s_lam, 3 * l + 1)
                A(lamw[:, 2:4], lamw[:, 0:2], ACT.Exp).then_inc(s_lam, 1)
                ln_mod(4 * l, l, 0)
                act.wait_ge(s_histT, l + 1)
                A(pBs[:, :, :, 0:3], ps[:, 7, 0:288].rearrange("p (f s r) -> p f s r", f=12, r=3), ACT.Copy).then_inc(s_histc, 1)

                def conv_silu(f):
                    act.wait_ge(s_conv, 12 * l + f + 1)
                    A(pB[:, f, 0:NTOK], ctmp[:, f % 2, :], ACT.Silu).then_inc(s_csil, 1)

                for c in range(N_WIN):
                    act.wait_ge(s_chunk, POS_WIN[l] + c + 1)
                    b = 2 * (c % 4)
                    if c < 4:
                        A(pA[:, 2 * c:2 * c + 2, :], ps[:, b:b + 2, 0:NTOK], ACT.Copy,
                          scale=DQK ** -0.5 if c < 2 else 1.0).then_inc(s_pev, 1)
                    elif c < 10:
                        f = 2 * (c - 4)
                        A(pB[:, f:f + 2, 3:3 + SEQ], ps[:, b:b + 2, 0:SEQ], ACT.Copy)
                        link(A(pBs[:, f:f + 2, :, 3:11], ps[:, b:b + 2, SEQ:NTOK].rearrange("p a (s r) -> p a s r", r=8), ACT.Copy))
                        A(tail[:, f:f + 2, 0:3], pB[:, f:f + 2, SEQ:SEQ + 3], ACT.Copy)
                        A(tail[:, f:f + 2, 3:27].rearrange("p f (s r) -> p f s r", r=3), pBs[:, f:f + 2, :, 8:11], ACT.Copy
                          ).then_inc(s_pev, 1)
                    else:
                        f = 8 + 2 * (c - 10)
                        A(pA[:, f:f + 2, :], ps[:, b:b + 2, 0:NTOK], ACT.Silu).then_inc(s_pev, 1)
                    if 5 <= c <= 10:
                        conv_silu(2 * (c - 5))
                        conv_silu(2 * (c - 5) + 1)
                act.wait_ge(s_csil, 12 * (l + 1))
                for b in range(5):
                    if b < 4:
                        if b >= 1:
                            act.wait_ge(s_l2s, 4 * l + b)
                        A(ctmp[:], pB[:, 2 * b:2 * b + 2, 0:NTOK], ACT.Square).then_inc(s_l2q, 1)
                    if b >= 1:
                        g = b - 1
                        act.wait_ge(s_l2s, 4 * l + g + 1)
                        if g >= 1:
                            act.wait_ge(s_l2d, 4 * l + g)
                        link(A(rstd[:], ps[:, 6 - 2 * (g % 2):8 - 2 * (g % 2), 0:NTOK], ACT.Ln, bias=cols[:, 1:2]))
                        A(rstd[:], rstd[:], ACT.Exp, scale=-0.5, **({"bias": cols[:, 2:3]} if g < 2 else {})).then_inc(s_l2r, 1)
                act.wait_ge(s_btd, l + 1)
                link(A(small[:, 48:60], small[:, 48:60], ACT.Exp, scale=-1.0))
                link(A(small[:, 48:60], small[:, 48:60], ACT.Ln, bias=cols[:, 3:4]))
                link(A(small[:, 60:64], adt[:, 0, l, :], ACT.Exp))
                A(small[:, 36:48].rearrange("p (t e) -> p t e", e=4), small[:, 0:24].rearrange("p (t e) -> p t e", e=8)[:, :, 0:4], ACT.Exp, scale=-1.0).then_inc(s_bta, 1)

                for u in range(8):
                    h, qt = u // 2, u % 2
                    nk = P * (qt + 1)
                    act.wait_ge(s_pM, 8 * l + u + 1)
                    for m_ in range(2):
                        m = A(scb[:, u % 2, 512 * m_:512 * m_ + nk], scb[:, u % 2, 512 * m_:512 * m_ + nk], ACT.Exp,
                              bias=small[:, 100 + 4 * (u % 2) + m_:101 + 4 * (u % 2) + m_],
                              accum_out=small[:, 102 + 4 * (u % 2) + m_:103 + 4 * (u % 2) + m_])
                        if m_ == 0:
                            link(m)
                    m.then_inc(s_pE, 1)
                    act.wait_ge(s_pT, 8 * l + u + 1)
                    if u >= 2:
                        act.wait_ge(s_pV, 8 * l + u - 1)
                    A(ptr[:, u % 2, 0:nk], ps[:, 4, 0:nk], ACT.Copy).then_inc(s_pTc, 1)
                    act.wait_ge(s_pV, 8 * l + u + 1)
                    A(oA[:, h, qt * P:(qt + 1) * P], ps[:, 5 + u % 2, 0:P], ACT.Copy).then_inc(s_pO, 1)

                act.wait_ge(s_qbz, l + 1)

                def pair_q(i):
                    if l or not (isinstance(i, int) and i == 0):
                        act.wait_ge(s_sS, NPAIR * l + i)
                    for a in range(2):
                        for m_ in range(2):
                            r = slice(64 * m_, 64 * m_ + 64)
                            m = A(qbd[r, a, :, 16 * a + 8 * m_:16 * a + 8 * m_ + 8],
                                  pA[r, 0:H, bass.ds(SEQ + a * DSEQ + i * (2 * DSEQ), DSEQ)], ACT.Copy)
                    m.then_inc(s_qb, 1)

                def pair_k(i, ns):
                    g = NPAIR * l + i
                    for n in ns:
                        act.wait_ge(s_kt, 16 * g + n + 1)
                        if not (l == 0 and isinstance(i, int) and i == 0 and n < 2):
                            act.wait_ge(s_kmm, 16 * g + n - 1)
                        A(ktb[:, n % 2, :], ps[:, n % 2, :], ACT.Copy).then_inc(s_ktA, 1)

                def pair_exp(i):
                    act.wait_ge(s_sM, NPAIR * l + i + 1)
                    A(scb[:, 0, :], scb[:, 0, :], ACT.Exp, bias=small[:, 108:109], accum_out=small[:, 110:111]).then_inc(s_sE, 1)

                def pair_out(i):
                    g = NPAIR * l + i
                    act.wait_ge(s_sT, g + 1)
                    if l or not (isinstance(i, int) and i == 0):
                        act.wait_ge(s_sV, 2 * g)
                    A(ptb[:, 0:4, :], ps[:, 5, :].rearrange("p (a n) -> p a n", a=4), ACT.Copy).then_inc(s_sTc, 1)
                    for a in range(2):
                        act.wait_ge(s_sV, 2 * g + a + 1)
                        A(ob[:, a, :], ps[:, 7 - 2 * a, 0:P], ACT.Copy).then_inc(s_ob, 1)
                    act.wait_ge(s_oT, g + 1)
                    A(oA[:, :, bass.ds(SEQ + i * (2 * DSEQ), 2 * DSEQ)].rearrange("p h (a t) -> p h a t", a=2),
                      ps[:, 6, 0:64].rearrange("p (a h t) -> p h a t", a=2, h=H), ACT.Copy).then_inc(s_sO, 1)

                def pair(i):
                    pair_q(i + 1)
                    pair_k(i + 1, range(0, 3))
                    pair_exp(i)
                    pair_k(i + 1, range(3, 2 * NPG))
                    pair_out(i)

                pair_q(0)
                pair_k(0, range(2 * NPG))
                pair(0)
                with act.Fori(1, NPAIR - 1) as i:
                    pair(i)
                pair_exp(NPAIR - 1)
                pair_out(NPAIR - 1)

                act.wait_ge(s_sO, NPAIR * (l + 1))
                act.wait_ge(s_l2d, 4 * (l + 1))
                for h in range(H + 1):
                    if h < H:
                        if h >= 2:
                            act.wait_ge(s_os, H * l + h - 1)
                        A(ctmp[:, h % 2, :], oA[:, h, :], ACT.Square).then_inc(s_oq, 1)
                    if h >= 1:
                        g = h - 1
                        act.wait_ge(s_os, H * l + g + 1)
                        if g >= 2:
                            act.wait_ge(s_mA, H * l + g - 1)
                        rinv(rstd[:, g % 2, :], ps[:, g % 2, 0:NTOK], 1.0 / P, None, (s_or, H * l + g)).then_inc(s_or, 1)

                def prepare(T):
                    c0, nt = TILES[T]
                    n = 3 * l + T
                    Gb_, kd_, DT_ = PREP[T][0], PREP[T][5], PREP[T][6]
                    act.wait_ge(s_gG, n + 1)
                    act.wait_ge(s_gGc, n + 1)
                    act.wait_ge(s_mA, H * (l + 1))
                    link(A(c3(Gb_, nt), c3(ps[:, 1, :], nt), ACT.Exp))
                    link(A(c3(DT_, nt)[0:nt], c3(DT_, nt)[0:nt], ACT.Exp))
                    A(small[0:nt, 120:124], small[0:nt, 120:124], ACT.Exp).then_inc(s_gE, 1)
                    act.wait_ge(s_gE, n + 1)
                    act.wait_ge(s_gK, n + 1)
                    for h in range(H):
                        m = A(c3(kd_, P)[0:nt, h, :], ps[0:nt, 5, h * P:(h + 1) * P], ACT.Copy, scale=small[0:nt, 120 + h:121 + h])
                    m.then_inc(s_gkd, 1)

                def levels(tiles):
                    nt = TILES[tiles[0]][1]
                    for v in range(3 if tiles[0] == 2 else 7):
                        for x, T in enumerate(tiles):
                            i0 = 17 * l + (14 if T == 2 else 0) + len(tiles) * v + x
                            act.wait_ge(s_g1, i0 + 1)
                            A(c3(PREP[T][10], nt)[0:nt], c3(ps[0:nt, LEVEL_BANKS[T][0], :], nt), ACT.Copy).then_inc(s_g1c, 1)

                def outputs(T):
                    c0, nt = TILES[T]
                    n = 3 * l + T
                    smp = T == 2
                    if smp:
                        act.wait_ge(s_kqS, l + 1)
                        act.wait_ge(s_g2c, 17 * l + 17)
                        A(Rsb, ps[:, 1:3, :].rearrange("p b n -> p (b n)"), ACT.Copy).then_inc(s_kqc, 1)
                    act.wait_ge(s_gRt, n + 1)
                    if smp:
                        act.wait_ge(s_kq, l + 1)
                        A(c3(qd, nt).rearrange("p h (b n) -> p h b n", b=2),
                          ps[:, 6, :].rearrange("p (h b q n) -> p h b q n", h=H, b=2, q=2)[:, :, :, 1, :], ACT.Copy)
                    A(rr[0:nt, :], ps[0:nt, 2, :], ACT.Copy).then_inc(s_gr, 1)
                    act.wait_ge(s_gV, n + 1)
                    A(vn[0:nt, :], ps[0:nt, 3, :], ACT.Copy).then_inc(s_gv, 1)
                    if T > 0:
                        act.wait_ge(s_mB, n)
                    if smp:
                        act.wait_ge(s_goa, l + 1)
                    else:
                        act.wait_ge(s_gO, n + 1)
                        link(A(c3(oG, nt), c3(ps[:, 4, :], nt), ACT.Copy))
                    A(sG[:, 0:H * nt].rearrange("p (h t) -> p h t", h=H), c3(oG, nt), ACT.Square).then_inc(s_goq, 1)
                    act.wait_ge(s_gos, n + 1)
                    link(A(sG[:, 0:H * nt], ps[:, 7, 0:H * nt], ACT.Ln, scale=1.0 / P, bias=cols[:, 1:2]))
                    A(sG[:, 0:H * nt], sG[:, 0:H * nt], ACT.Exp, scale=-0.5).then_inc(s_gor, 1)

                prepare(0)
                prepare(1)
                levels((0, 1))
                outputs(0)
                outputs(1)
                prepare(2)
                levels((2,))
                outputs(2)

                ln_post(4 * l + 1, l, 0)
                ln_mod(4 * l + 2, l, 1)

                def silu(pos, e, n0, n, first):
                    for j in range(UP):
                        act.wait_ge(s_chunk, pos + 2 * j + 1 + e * MLP_POS)
                        if j >= 2 or not first:
                            act.wait_ge(s_ff, n0 + j - 1)
                        A(sil[:, j % 2, :, 0:n], ps[:, 4 * (j % 2):4 * (j % 2) + 2, 0:n], ACT.Silu).then_inc(s_sil, 1)

                def expert(e, slots, rows):
                    for k in range(KT):
                        act.wait_ge(s_xeT, e * KT + k + 1)
                        A(Xe[:, k, 0:slots], ps[:, 4 + k % 4, 0:slots], ACT.Copy).then_inc(s_xe, 1)
                    silu(POS_MLP[1], e, UP + e * UP, slots, False)

                act.wait_ge(s_out, 16 * (8 * l + 6))
                if l == 0:
                    silu(POS_MLP[0], 0, 0, NTOK, True)
                else:
                    act.wait_ge(s_out, 16 * 8 * DEPTH)
                    act.wait_ge(s_hrT, 1)
                    for t, (c0, nt) in enumerate(TILES):
                        A(hrow[0:nt, t, :].rearrange("p (a n) -> p a n", a=2), ps[0:nt, 2 * t:2 * t + 2, :], ACT.Copy).then_inc(s_hr, 1)
                    act.wait_ge(s_rtm, 1)
                    A(small[:, 72:96], small[:, 72:96], ACT.Exp).then_inc(s_rte, 1)
                    act.wait_ge(s_route, 1)
                    with act.Fori(0, NE) as e:
                        c = act.value_load(cls[0:1, bass.ds(e, 1)], min_val=0, max_val=2)
                        with act.If(c < 1):
                            expert(e, *CLASSES[0])
                        with act.Else():
                            with act.If(c < 2):
                                expert(e, *CLASSES[1])
                            with act.Else():
                                expert(e, *CLASSES[2])
                ln_post(4 * l + 3, l, 1)
            for t, (c0, nt) in enumerate(TILES):
                act.wait_ge(s_yT, t + 1)
                A(yrow[0:nt, t, :].rearrange("p (a n) -> p a n", a=2), ps[0:nt, 2 * t:2 * t + 2, :], ACT.Copy).then_inc(s_y, 1)

        @block.vector
        def _(dve):
            V = nc.vector
            link = Chain(dve, s_cd)

            def ln(n):
                dve.wait_ge(s_mean, n + 1)
                for p in range(4):
                    V.tensor_tensor(xc[:, 2 * p:2 * p + 2, :], xT[:, 2 * p:2 * p + 2, :],
                                    ps[:, 0:1, 0:NTOK].to_broadcast([P, 2, NTOK]), ALU.subtract).then_inc(s_xc, 1)
                dve.wait_ge(s_rstd, n + 1)
                for p in range(4):
                    V.tensor_tensor(xc[:, 2 * p:2 * p + 2, :], xc[:, 2 * p:2 * p + 2, :],
                                    rstd[:, 0:1, :].to_broadcast([P, 2, NTOK]), ALU.mult).then_inc(s_xn, 1)

            def seqs(t):
                return t.rearrange("p k (s r) -> p k s r", r=DSEQ)

            def per_seq(l, f0, nf):
                m = mod[:, l, f0:f0 + nf, 1:9].rearrange("p k (s o) -> p k s o", o=1)
                return m.to_broadcast([P, nf, NSEQ, DSEQ])

            def ln_mod(n, l, half):
                ln(n)
                dve.wait_ge(s_xn, 4 * (n + 1))
                link(V.tensor_tensor(seqs(hT[:, :, SEQ:]), seqs(xc[:, :, SEQ:]), per_seq(l, 24 * half + 8, 8), ALU.mult))
                V.tensor_tensor(seqs(hT[:, :, SEQ:]), seqs(hT[:, :, SEQ:]), per_seq(l, 24 * half, 8), ALU.add).then_inc(s_hs, 1)
                V.tensor_scalar(xT[:], xT[:], ALPHA, None, ALU.mult).then_inc(s_xa, 1)

            def residual(src, k0, l, half):
                g0 = 24 * half + 16 + k0
                for o in range(2):
                    V.scalar_tensor_tensor(out=xT[:, k0 + o, 0:SEQ], in0=src[:, o, 0:SEQ], scalar=mod[:, l, g0 + o, 0:1],
                                           in1=xT[:, k0 + o, 0:SEQ], op0=ALU.mult, op1=ALU.add)
                t = seqs(ctmp[:, :, 0:NS])
                dve.wait_ge(s_lnin, KT * (4 * l + 2 * half + 1) + k0)
                link(V.tensor_tensor(t, seqs(src[:, :, SEQ:NTOK]), per_seq(l, g0, 2), ALU.mult))
                V.tensor_tensor(xT[:, k0:k0 + 2, SEQ:], xT[:, k0:k0 + 2, SEQ:], ctmp[:, :, 0:NS], ALU.add).then_inc(s_lnin, 2)

            for k in range(KT):
                dve.wait_ge(s_xt, k + 1)
                V.tensor_copy(xT[:, k, :], ps[:, 1 + k % 4, 0:NTOK]).then_inc(s_lnin, 1)
            dve.wait_ge(s_vec, 3)
            for l in range(DEPTH):
                with dve.Fori(0, ADA_CH // RING) as i:
                    for c in range(RING):
                        dve.wait_ge(s_adT, ADA_CH * l + c + 1 + i * RING)
                        b = vecT[:, 0, bass.ds(48 * l + 2 * c + i * (2 * RING), 2)].rearrange("p (a o) -> p a o", o=1)
                        V.tensor_tensor(mod[:, l, bass.ds(2 * c + i * (2 * RING), 2), :],
                                        ps[:, 5 * (c % 2), 0:32].rearrange("p (a n) -> p a n", a=2)[:, :, 0:9],
                                        b.to_broadcast([P, 2, 9]), ALU.add).then_inc(s_modev, 1)
                dve.wait_ge(s_modev, ADA_CH * (l + 1))
                for half in range(2):
                    f = 24 * half + 8
                    V.tensor_scalar(mod[:, l, f:f + 8, :], mod[:, l, f:f + 8, :], 1.0, None, ALU.add).then_inc(s_mod, 1)

            for l in range(DEPTH):
                for a in range(2):
                    link(V.tensor_tensor(ctmp[:, 0, 0:64], lamb[:, l, 128 * a:128 * a + 64], lamb[:, l, 128 * a + 64:128 * a + 128], ALU.mult))
                    m = V.tensor_reduce(lamw[:, a:a + 1], ctmp[:, 0, 0:64], AX.X, ALU.add)
                    if a == 0:
                        link(m)
                m.then_inc(s_lam, 1)
                dve.wait_ge(s_lam, 3 * l + 2)
                link(V.tensor_tensor(lamw[:, 4:5], lamw[:, 3:4], lamw[:, 2:3], ALU.subtract))
                link(V.tensor_scalar(lamc[:, l, 0:1], lamw[:, 4:5], -LAM_INIT[l], None, ALU.add))
                link(V.scalar_tensor_tensor(out=lamc[:, l, 1:2], in0=C[:, C_ROW + 2:C_ROW + 3], scalar=lamc[:, l, 0:1],
                                            in1=C[:, C_ROW + 1:C_ROW + 2], op0=ALU.mult, op1=ALU.add))
                V.tensor_scalar(lamw[:, 5:6], vecT[:, 0, 96 + l:97 + l], 1.0 - LAM_INIT[l], None, ALU.mult).then_inc(s_lam, 1)
                dve.wait_ge(s_lam, 3 * l + 3)
                dve.wait_ge(s_mod, 2 * (l + 1))
                ln_mod(4 * l, l, 0)

                dve.wait_ge(s_histc, l + 1)
                link(V.memset(pB[:, :, 0:3], 0.0))
                for f in range(12):
                    dve.wait_ge(s_pev, N_WIN * l + 5 + f // 2)
                    if f >= 2:
                        dve.wait_ge(s_csil, 12 * l + f - 1)
                    smp = pB[:, f, 3 + SEQ:3 + SEQ + 88].rearrange("p (s r) -> p s r", r=11)
                    out_s = ctmp[:, f % 2, SEQ:].rearrange("p (s r) -> p s r", r=DSEQ)
                    out_p = ctmp[:, f % 2, 0:SEQ]
                    wc = lambda i: vecT[:, 1, 48 * l + 12 * i + f:48 * l + 12 * i + f + 1]
                    V.tensor_scalar(out_p, pB[:, f, 0:SEQ], wc(0), None, ALU.mult)
                    link(V.tensor_scalar(out_s, smp[:, :, 0:DSEQ], wc(0), None, ALU.mult))
                    for i in range(1, CW):
                        m = V.scalar_tensor_tensor(out=out_p, in0=pB[:, f, i:i + SEQ], scalar=wc(i), in1=out_p, op0=ALU.mult, op1=ALU.add)
                        m = V.scalar_tensor_tensor(out=out_s, in0=smp[:, :, i:i + DSEQ], scalar=wc(i), in1=out_s, op0=ALU.mult, op1=ALU.add)
                        if i < CW - 1:
                            link(m)
                    m.then_inc(s_conv, 1)
                dve.wait_ge(s_nar, l + 1)
                V.tensor_copy(lnv[:], ps[:, 6, 0:NTOK]).then_inc(s_narc, 1)
                dve.wait_ge(s_ba, l + 1)
                link(V.tensor_copy(small[:, 0:16], ps[:, 7, 0:16]))
                V.tensor_copy(small[0:NS, 16:24], ps[0:NS, 7, 16:24]).then_inc(s_bae, 1)
                dve.wait_ge(s_bae, l + 1)
                ba = small[:, 0:24].rearrange("p (t e) -> p t e", e=8)
                u = small[:, 24:36].rearrange("p (t e) -> p t e", e=4)
                t3 = lambda a: small[:, a:a + 12].rearrange("p (t e) -> p t e", e=4)
                bc3 = lambda t: t.rearrange("p (o e) -> p o e", o=1).to_broadcast([P, 3, H])
                link(V.tensor_tensor(u, ba[:, :, 4:8], bc3(adt[:, 1, l, :]), ALU.add))
                V.scalar_tensor_tensor(out=small[:, 48:60], in0=small[:, 24:36], scalar=-1.0, in1=small[:, 24:36],
                                       op0=ALU.mult, op1=ALU.max).then_inc(s_btd, 1)
                for c in range(2):
                    dve.wait_ge(s_chunk, POS_VO[l] + c + 1)
                    for t, (c0, nt) in enumerate(TILES):
                        m = V.tensor_copy(va[0:nt, t, CH * c:CH * (c + 1)], ps[0:nt, 3 * c + t, 0:CH])
                        if t < 2:
                            link(m)
                    m.then_inc(s_va, 1)
                dve.wait_ge(s_kT, l + 1)
                if l:
                    dve.wait_ge(s_ff, UP * l)
                link(V.tensor_copy(kst[:, 0:2, :], ps[:, 0:2, :]))
                V.tensor_copy(kst[0:NS, 2, :], ps[0:NS, 2, :]).then_inc(s_kst, 1)
                dve.wait_ge(s_tailT, l + 1)
                dve.wait_ge(s_histT, l + 1)
                V.tensor_copy(rowb[0:27, :].rearrange("p (a n) -> p a n", a=3), ps[0:27, 3:6, :]).then_inc(s_tailc, 1)
                for b in range(4):
                    dve.wait_ge(s_l2r, 4 * l + b + 1)
                    V.tensor_tensor(pB[:, 2 * b:2 * b + 2, 0:NTOK], pB[:, 2 * b:2 * b + 2, 0:NTOK], rstd[:], ALU.mult).then_inc(s_l2d, 1)
                dve.wait_ge(s_bta, l + 1)
                link(V.tensor_scalar(small[:, 36:48], small[:, 36:48], 1.0, None, ALU.add))
                link(V.reciprocal(small[:, 36:48], small[:, 36:48]))
                link(V.scalar_tensor_tensor(out=small[:, 24:36], in0=small[:, 24:36], scalar=0.0, in1=small[:, 48:60],
                                            op0=ALU.max, op1=ALU.add))
                link(V.tensor_tensor(u, u, bc3(small[:, 60:64]), ALU.mult))
                V.tensor_scalar(small[:, 24:36], small[:, 24:36], -1.0, None, ALU.mult).then_inc(s_bt, 1)

                def p_max(uu):
                    h, qt = uu // 2, uu % 2
                    nk = P * (qt + 1)
                    dve.wait_ge(s_pS, 8 * l + uu + 1)
                    if uu >= 2:
                        dve.wait_ge(s_pT, 8 * l + uu - 1)
                    for m_ in range(2):
                        m = V.scalar_tensor_tensor(out=scb[:, uu % 2, 512 * m_:512 * m_ + nk], in0=dP[:, qt, 0:nk], scalar=SLOPE[h],
                                                   in1=ps[:, 2 * (uu % 2) + m_, 0:nk], op0=ALU.mult, op1=ALU.add)
                    link(m)
                    V.tensor_reduce(small[:, 100 + 4 * (uu % 2):102 + 4 * (uu % 2)],
                                    scb[:, uu % 2, 0:1024].rearrange("p (a n) -> p a n", a=2)[:, :, 0:nk],
                                    AX.X, ALU.max, negate=True).then_inc(s_pM, 1)

                def p_probs(uu):
                    nk = P * (uu % 2 + 1)
                    b = 102 + 4 * (uu % 2)
                    dve.wait_ge(s_pE, 8 * l + uu + 1)
                    link(V.reciprocal(small[:, b:b + 2], small[:, b:b + 2]))
                    link(V.tensor_scalar(small[:, b + 1:b + 2], small[:, b + 1:b + 2], lamc[:, l, 0:1], None, ALU.mult))
                    p1, p2 = scb[:, uu % 2, 0:nk], scb[:, uu % 2, 512:512 + nk]
                    link(V.tensor_scalar(p1, p1, small[:, b:b + 1], None, ALU.mult))
                    V.scalar_tensor_tensor(out=p1, in0=p2, scalar=small[:, b + 1:b + 2], in1=p1, op0=ALU.mult, op1=ALU.add).then_inc(s_pA, 1)

                p_max(0)
                for uu in range(8):
                    if uu + 1 < 8:
                        p_max(uu + 1)
                    p_probs(uu)

                def pair(i):
                    g = NPAIR * l + i
                    dve.wait_ge(s_sS, g + 1)
                    if l or not (isinstance(i, int) and i == 0):
                        dve.wait_ge(s_sT, g)
                    V.scalar_tensor_tensor(out=scb[:, 0, 0:PAST], in0=dS[:], scalar=C[:, C_ROW:C_ROW + 1],
                                           in1=ps[:, 2:4, :].rearrange("p a n -> p (a n)"), op0=ALU.mult, op1=ALU.add)
                    link(V.scalar_tensor_tensor(out=scb[:, 0, PAST:PAST + NS], in0=dN[:, bass.ds(i, 1), :].rearrange("p o n -> p (o n)"),
                                                scalar=C[:, C_ROW:C_ROW + 1], in1=ps[:, 4, 0:NS], op0=ALU.mult, op1=ALU.add))
                    V.tensor_reduce(small[:, 108:109], scb[:, 0, :], AX.X, ALU.max, negate=True).then_inc(s_sM, 1)
                    dve.wait_ge(s_sE, g + 1)
                    link(V.reciprocal(small[:, 110:111], small[:, 110:111]))
                    V.tensor_scalar(scb[:, 0, :], scb[:, 0, :], small[:, 110:111], lamc[:, l, 1:2], ALU.mult, ALU.mult).then_inc(s_sP, 1)
                    dve.wait_ge(s_sT, g + 1)
                    if l or not (isinstance(i, int) and i == 0):
                        dve.wait_ge(s_sV, 2 * g)
                    V.tensor_copy(ptb[0:64, 8, :], ps[0:64, 4, P:2 * P])
                    V.tensor_copy(ptb[:, 4:8, :], ps[:, 6, :].rearrange("p (a n) -> p a n", a=4)).then_inc(s_sTd, 1)

                DVE_PAIR = 2
                pair(0)
                with dve.Fori(1, NPAIR) as i:
                    link.loop(i - 1, DVE_PAIR)
                    pair(i)
                link.done(DVE_PAIR, NPAIR - 1)

                dve.wait_ge(s_out, 16 * (8 * l + 6))
                for h in range(H):
                    dve.wait_ge(s_or, H * l + h + 1)
                    V.scalar_tensor_tensor(out=mixT[:, h, :], in0=oA[:, h, :], scalar=lamw[:, 5:6], in1=rstd[:, h % 2, :],
                                           op0=ALU.mult, op1=ALU.mult).then_inc(s_mA, 1)

                dve.wait_ge(s_mA, H * (l + 1))
                if l > 0:
                    dve.wait_ge(s_out, 16 * 8 * l)
                V.memset(Sp[:], 0.0)
                def level_mask(T, v):
                    nt = TILES[T][1]
                    lm = C[0:nt, C_LEV + v * P:C_LEV + v * P + nt].rearrange("p (o t) -> p o t", o=1).to_broadcast([nt, H, nt])
                    V.tensor_tensor(c3(PREP[T][8], nt)[0:nt], c3(PREP[T][7], nt)[0:nt], lm, ALU.mult).then_inc(s_lm, 1)

                def prepare(T):
                    c0, nt = TILES[T]
                    n = 3 * l + T
                    Gb_, bbs_, QK_, XT_, qd_, kd_, DT_, LT_, LM_, X_, PP_ = PREP[T]
                    mask = (C[0:nt, C_TRIS:C_TRIS + nt] if T == 2 else tri).rearrange("p (o t) -> p o t", o=1).to_broadcast([nt, H, nt])
                    dve.wait_ge(s_gG, n + 1)
                    if T > 0:
                        dve.wait_ge(s_gkd, n)
                    link(V.tensor_copy(small[0:nt, 112:120], ps[0:nt, 0, 0:8]))
                    V.tensor_copy(c3(bbs_, nt), c3(ps[:, 2, :], nt))
                    for h in range(H):
                        V.tensor_scalar(c3(DT_, nt)[0:nt, h, :], ps[0:nt, 1, h * P:h * P + nt], small[0:nt, 112 + h:113 + h], 0.0,
                                        ALU.subtract, ALU.min)
                    V.tensor_tensor(small[0:nt, 120:124], small[0:nt, 116:120], small[0:nt, 112:116], ALU.subtract).then_inc(s_gGc, 1)
                    dve.wait_ge(s_gE, n + 1)
                    V.tensor_tensor(c3(qd_, nt), pB[:, 0:4, c0:c0 + nt], c3(Gb_, nt), ALU.mult)
                    link(V.tensor_tensor(c3(DT_, nt)[0:nt], c3(DT_, nt)[0:nt], mask, ALU.mult))
                    dve.wait_ge(s_gK, n + 1)
                    V.tensor_tensor(c3(QK_, nt)[0:nt], c3(ps[0:nt, 4, :], nt), c3(DT_, nt)[0:nt], ALU.mult)
                    link(V.tensor_tensor(c3(LT_, nt)[0:nt], c3(ps[0:nt, 3, :], nt), c3(DT_, nt)[0:nt], ALU.mult))
                    idb = ident[0:nt, 0:nt].rearrange("p (o t) -> p o t", o=1).to_broadcast([nt, H, nt])
                    V.tensor_copy(c3(X_, nt)[0:nt], idb)
                    V.tensor_copy(c3(XT_, nt)[0:nt], idb)
                    link(V.tensor_tensor(c3(LT_, nt)[0:nt], c3(LT_, nt)[0:nt], c3(bbs_, nt)[0:nt], ALU.mult))
                    level_mask(T, 0)

                def levels(tiles):
                    nt = TILES[tiles[0]][1]
                    lev = 3 if tiles[0] == 2 else 7
                    for v in range(lev):
                        for x, T in enumerate(tiles):
                            i0 = 17 * l + (14 if T == 2 else 0) + len(tiles) * v + x
                            X_, XT_ = c3(PREP[T][9], nt)[0:nt], c3(PREP[T][3], nt)[0:nt]
                            if v + 1 < lev:
                                dve.wait_ge(s_g1c, i0 + 1)
                                level_mask(T, v + 1)
                            dve.wait_ge(s_g2, i0 + 1)
                            if v + 1 < lev:
                                V.tensor_tensor(X_, X_, c3(ps[0:nt, LEVEL_BANKS[T][1], :], nt), ALU.subtract)
                            V.tensor_tensor(XT_, XT_, c3(ps[0:nt, LEVEL_BANKS[T][2], :], nt), ALU.subtract).then_inc(s_g2c, 1)

                def right_side(T):
                    c0, nt = TILES[T]
                    Gb_, bbs_ = PREP[T][:2]
                    dve.wait_ge(s_gR, 3 * l + T + 1)
                    if T == 2:
                        kS = ps[:, 6, :].rearrange("p (h b q n) -> p h b q n", h=H, b=2, q=2)[:, :, :, 0, :]
                        halves = lambda t: t.rearrange("p h (b n) -> p h b n", b=2)
                        link(V.tensor_tensor(halves(c3(rT, nt)), kS, halves(c3(Gb_, nt)), ALU.mult))
                    else:
                        link(V.tensor_tensor(c3(rT, nt), c3(ps[:, 1, :], nt), c3(Gb_, nt), ALU.mult))
                    link(V.tensor_tensor(c3(rT, nt), pB[:, 8:12, c0:c0 + nt], c3(rT, nt), ALU.subtract))
                    V.tensor_tensor(c3(rT, nt), c3(rT, nt), c3(bbs_, nt), ALU.mult).then_inc(s_gRc, 1)

                def prompt_state(T):
                    nt = P
                    dve.wait_ge(s_gS, 6 * l + T + 1)
                    dve.wait_ge(s_gO, 3 * l + T + 1)
                    for h in range(H):
                        m = V.scalar_tensor_tensor(out=Sp[:, h, :], in0=Sp[:, h, :], scalar=c3(PREP[T][0], nt)[:, h, nt - 1:nt],
                                                   in1=ps[:, 5, h * P:(h + 1) * P], op0=ALU.mult, op1=ALU.add)
                    m.then_inc(s_gSc, 1)

                def sample_states():
                    nt = NS

                    def masked_keys(h):
                        for half in range(2):
                            m = V.tensor_tensor(kdm[h % 2][half][0:nt, :].rearrange("p (s k) -> p s k", s=4),
                                                c3(kd, P)[0:nt, h:h + 1, :].to_broadcast([nt, 4, P]),
                                                C[0:nt, C_SEQM + 4 * half:C_SEQM + 4 * half + 4].rearrange("p (s o) -> p s o", o=1).to_broadcast([nt, 4, P]),
                                                ALU.mult)
                        m.then_inc(s_gkm, 1)

                    dve.wait_ge(s_gR, 3 * l + 3)
                    dve.wait_ge(s_gkd, 3 * l + 3)
                    masked_keys(0)
                    masked_keys(1)
                    dve.wait_ge(s_gO, 3 * l + 3)
                    V.tensor_tensor(c3(oG, nt), c3(ps[:, 4, :], nt), c3(qd, nt), ALU.add).then_inc(s_goa, 1)
                    for h in range(H):
                        dve.wait_ge(s_gS, 6 * l + 3 + h)
                        for s in range(NSEQ):
                            V.scalar_tensor_tensor(out=Ss[:, s, h, :], in0=Ss[:, s, h, :], scalar=c3(Gb_e, nt)[:, h, 8 * s + 7:8 * s + 8],
                                                   in1=ps[:, (5, 2)[h % 2] + s // 4, (s % 4) * P:(s % 4 + 1) * P], op0=ALU.mult, op1=ALU.add
                                                   ).then_inc(s_gSc, 1)
                        if h + 2 < H:
                            masked_keys(h + 2)

                def mix(T):
                    c0, nt = TILES[T]
                    dve.wait_ge(s_gor, 3 * l + T + 1)
                    g3 = sG[:, 0:H * nt].rearrange("p (h t) -> p h t", h=H)
                    link(V.tensor_tensor(c3(oG, nt), c3(oG, nt), g3, ALU.mult))
                    V.scalar_tensor_tensor(out=mixT[:, 4:8, c0:c0 + nt], in0=c3(oG, nt), scalar=vecT[:, 0, 98 + l:99 + l],
                                           in1=pA[:, 8:12, c0:c0 + nt], op0=ALU.mult, op1=ALU.mult).then_inc(s_mB, 1)

                prepare(0)
                prepare(1)
                levels((0, 1))
                right_side(0)
                prompt_state(0)
                right_side(1)
                mix(0)
                prompt_state(1)
                mix(1)
                prepare(2)
                levels((2,))
                kT = pB[:, 4:8, SEQ:NTOK]
                dve.wait_ge(s_g2c, 17 * l + 17)
                V.memset(kqp[:, :, NSEQ:NSEQ + 1, :], 0.0)
                for h in range(H):
                    V.tensor_copy(kqp[:, h, 0:NSEQ, 0:8], kT[:, h, :].rearrange("p (s t) -> p s t", t=DSEQ))
                    m = V.tensor_copy(kqp[:, h, 0:NSEQ, 8:16], c3(qd, NS)[:, h, :].rearrange("p (s t) -> p s t", t=DSEQ))
                m.then_inc(s_kq, 1)
                right_side(2)
                sample_states()
                mix(2)

                for c in range(4):
                    dve.wait_ge(s_chunk, POS_VO[l] + 2 + c + 1)
                    if c == 0:
                        dve.wait_ge(s_xa, 2 * l + 1)
                    residual(ps[:, 2 * c:2 * c + 2, :], 2 * c, l, 0)
                ln(4 * l + 1)
                ln_mod(4 * l + 2, l, 1)
                dve.wait_ge(s_xa, 2 * l + 2)

                def swiglu(pos, e, n0, n, js):
                    for j in js:
                        dve.wait_ge(s_sil, n0 + j + 1)
                        dve.wait_ge(s_chunk, pos + 2 * j + 2 + e * MLP_POS)
                        b = 4 * (j % 2) + 2
                        V.tensor_tensor(ff[:, 2 * j:2 * j + 2, 0:n], sil[:, j % 2, :, 0:n], ps[:, b:b + 2, 0:n], ALU.mult).then_inc(s_ff, 1)

                def select(e):
                    col = lambda what, t, nt: route[0:nt, what, t, bass.ds(e, 1)]
                    for t, (c0, nt) in enumerate(TILES):
                        V.tensor_scalar(Sel[0:nt, t, :], C[0:nt, C_IOTA:C_IOTA + NTOK], col(2, t, nt), col(0, t, nt), ALU.is_equal, ALU.mult)
                        m = V.tensor_scalar(SelG[0:nt, t, :], C[0:nt, C_IOTA:C_IOTA + NTOK], col(2, t, nt), col(1, t, nt), ALU.is_equal, ALU.mult)
                    m.then_inc(s_prep, 1)

                def expert(e, slots, rows):
                    dve.wait_ge(s_gtT, e + 1)
                    for s_, (r0, nr) in enumerate(rows):
                        m = V.tensor_copy(GT[0:nr, s_, :], ps[0:nr, s_, 0:NTOK])
                    m.then_inc(s_gt, 1)
                    dve.wait_ge(s_xeT, e * KT + KT)
                    select(e + 1)
                    swiglu(POS_MLP[1], e, UP + e * UP, slots, range(UP))
                    for d in range(4):
                        dve.wait_ge(s_chunk, POS_MLP[1] + 2 * UP + 3 * d + 3 + e * MLP_POS)
                        for s_, (r0, nr) in enumerate(rows):
                            m = V.tensor_copy(frow[0:nr, s_, CH * d:CH * (d + 1)], ps[0:nr, 3 * (d % 2) + s_, 0:CH])
                        m.then_inc(s_fr, 1)
                    dve.wait_ge(s_fa, KT + e * KT)
                    for k in range(KT):
                        dve.wait_ge(s_cb, e * KT + k + 1)
                        V.tensor_tensor(mixT[:, k, :], mixT[:, k, :], ps[:, 6 + k % 2, 0:NTOK], ALU.add).then_inc(s_fa, 1)

                if l == 0:
                    swiglu(POS_MLP[0], 0, 0, NTOK, range(UP))
                    for d in range(4):
                        dve.wait_ge(s_chunk, POS_MLP[0] + 2 * UP + 3 * d + 3)
                        residual(ps[:, 2 * d:2 * d + 2, :], 2 * d, l, 1)
                else:
                    dve.wait_ge(s_nar, DEPTH + 1)
                    V.tensor_copy(lnv[:], ps[:, 7, 0:NTOK]).then_inc(s_narc, 1)
                    dve.wait_ge(s_rt, 1)
                    lg = small[:, 72:96].rearrange("p (t e) -> p t e", e=8)
                    V.memset(route[:], 0.0)
                    link(V.memset(small[:, 64:96], 0.0))
                    V.tensor_tensor(lg[:, 0:2, :], ps[:, 6, 0:16].rearrange("p (t e) -> p t e", e=8),
                                    brb[:].rearrange("p (o e) -> p o e", o=1).to_broadcast([P, 2, 8]), ALU.add)
                    link(V.tensor_tensor(small[0:NS, 88:96], ps[0:NS, 6, 16:24], brb[0:NS, :], ALU.add))
                    sel = route[:, 0, :, 0:NE]
                    pw = ctmp[:, 0, 0:64].rearrange("p (i j) -> p i j", i=8)
                    pw2 = ctmp[:, 1, 0:64].rearrange("p (i j) -> p i j", i=8)
                    low = C[:, C_LOW:C_LOW + 64].rearrange("p (i j) -> p i j", i=8)
                    for t in range(3):
                        lj = lg[:, t:t + 1, :].to_broadcast([P, 8, 8])
                        li = small[:, 72 + 8 * t:80 + 8 * t].rearrange("p (i o) -> p i o", o=1).to_broadcast([P, 8, 8])
                        V.tensor_tensor(pw, lj, li, ALU.is_equal)
                        link(V.tensor_tensor(pw2, lj, li, ALU.is_gt))
                        link(V.tensor_tensor(pw, pw, low, ALU.mult))
                        link(V.tensor_tensor(pw, pw, pw2, ALU.add))
                        link(V.tensor_reduce(sel[:, t, :], pw, AX.X, ALU.add))
                    V.tensor_scalar(sel, sel, 2.0, None, ALU.is_lt).then_inc(s_sel, 1)
                    dve.wait_ge(s_sel, 1)
                    link(V.tensor_reduce(small[:, 64:67], lg, AX.X, ALU.max))
                    mx = small[:, 64:67].rearrange("p (t o) -> p t o", o=1).to_broadcast([P, 3, 8])
                    V.tensor_tensor(lg, lg, mx, ALU.subtract).then_inc(s_rtm, 1)
                    dve.wait_ge(s_rte, 1)
                    link(V.tensor_tensor(lg, lg, sel, ALU.mult))
                    link(V.tensor_reduce(small[:, 64:67], lg, AX.X, ALU.add))
                    link(V.reciprocal(small[:, 64:67], small[:, 64:67]))
                    link(V.tensor_tensor(route[:, 1, :, 0:NE], lg, mx, ALU.mult))
                    dve.wait_ge(s_pos, 1)
                    V.tensor_copy(route[:, 2, 0:2, 0:NE], ps[:, 7, 0:16].rearrange("p (t e) -> p t e", e=8))
                    V.tensor_copy(route[0:NS, 2, 2, 0:NE], ps[0:NS, 7, 16:24])
                    link(V.tensor_scalar(small[:, 0:8], ps[:, 7, 24:32], float(CLASSES[0][0]), None, ALU.is_gt))
                    V.tensor_scalar(small[:, 8:16], ps[:, 7, 24:32], float(CLASSES[1][0]), None, ALU.is_gt).then_inc(s_route2, 1)
                    dve.wait_ge(s_route2, 1)
                    V.tensor_tensor(cls[:], small[:, 0:8], small[:, 8:16], ALU.add).then_inc(s_route, 1)
                    dve.wait_ge(s_out, 16 * 8 * DEPTH)
                    select(0)
                    V.memset(mixT[:], 0.0).then_inc(s_fa, KT)
                    dve.wait_ge(s_route, 1)
                    with dve.Fori(0, NE) as e:
                        c = dve.value_load(cls[0:1, bass.ds(e, 1)], min_val=0, max_val=2)
                        with dve.If(c < 1):
                            expert(e, *CLASSES[0])
                        with dve.Else():
                            with dve.If(c < 2):
                                expert(e, *CLASSES[1])
                            with dve.Else():
                                expert(e, *CLASSES[2])
                    dve.wait_ge(s_fa, KT * (NE + 1))
                    for d in range(4):
                        residual(mixT[:, 2 * d:2 * d + 2, :], 2 * d, l, 1)
                ln(4 * l + 3)


_INS = ['x_prompt', 'x_sample', 'cache_k', 'cache_v', 'state_conv', 'state_delta', 'page_table', 'c_prompt', 'c_sample',
        'w_in', 'w_out', 'lam_params', 'subln_a', 'conv_w', 'a_log', 'dt_bias', 'norm_b', 'ada_w', 'ada_b',
        'ln1_g', 'ln1_b', 'ln2_g', 'ln2_b', 'dense_w_up', 'dense_w_down', 'moe_router', 'moe_router_b', 'moe_w_up', 'moe_w_down']
_OUTS = [(1, SEQ, D), (NSEQ, DSEQ, D), (DEPTH, 1, SEQ, H, P), (DEPTH, 1, SEQ, H, P), (DEPTH, 1, 3, 1536), (DEPTH, 1, H, P, P),
         (DEPTH, NSEQ, DSEQ, H, P), (DEPTH, NSEQ, DSEQ, H, P), (DEPTH, NSEQ, 3, 1536), (DEPTH, NSEQ, H, P, P)]


def kernel(**inputs):
    import concourse.bacc as _bacc
    from concourse.bass_utils import run_bass_kernel_spmd as _run

    nc = _bacc.Bacc("TRN2", target_bir_lowering=False, num_devices=1)
    arrays, args = {}, []
    host = [(n, np.ascontiguousarray(inputs[n])) for n in _INS]
    host += list(zip(("table_c", "table_dp", "table_ds", "table_dn"), constant_tables()))
    for name, a in host:
        arrays[f"in_{name}_dram"] = a
        args.append(nc.dram_tensor(f"in_{name}_dram", a.shape, mybir.dt.from_np(a.dtype), kind="ExternalInput").ap())
    for i, shape in enumerate(_OUTS):
        args.append(nc.dram_tensor(f"out_{i}_dram", shape, F32, kind="ExternalOutput").ap())
    trunk_kernel(nc, *args)
    r = _run(nc, [arrays], core_ids=[0])
    return tuple(r.results[0][f"out_{i}_dram"] for i in range(len(_OUTS)))
```
